# Optimizing a Trainium2 kernel written in Bass

```python
import jax, jax.numpy as jnp
from jax import lax
import numpy as np

D_MODEL = 1024
BATCH = 1
SEQ = 512
DEPTH = 2

LRU_WIDTH = 512
LRU_BLOCKS = 8
LRU_BLOCK = LRU_WIDTH // LRU_BLOCKS
CONV_WIDTH = 4
LRU_C = 8.0
MLA_HEADS = 4
QK_NOPE = 128
QK_ROPE = 64
QK_HEAD = QK_NOPE + QK_ROPE
V_HEAD = 128
Q_LORA = 768
KV_LORA = 256
MLA_WIDTH = MLA_HEADS * V_HEAD
MIX_WIDTH = LRU_WIDTH + MLA_WIDTH
IN_WIDTH = 2 * LRU_WIDTH + Q_LORA + KV_LORA + QK_ROPE
ROPE_BASE = 10000.0
Q_BLOCK = 128
N_EXPERTS = 16
N_GROUPS = 4
EXPERTS_PER_GROUP = N_EXPERTS // N_GROUPS
TOP_K = 2
D_EXPERT = 512
MOE_BLOCK = 128
DN_ALPHA = (2 * DEPTH) ** 0.25
DN_BETA = (8 * DEPTH) ** -0.25
EPS = 1e-6

kernel_name = 'hybrid_rglru_mla_moe_deepnorm'

def layer_norm(x, g, b):
    xf = x.astype(jnp.float32)
    mu = jnp.mean(xf, axis=-1, keepdims=True)
    var = jnp.mean(jnp.square(xf - mu), axis=-1, keepdims=True)
    return ((xf - mu) * lax.rsqrt(var + EPS) * g.astype(jnp.float32) + b.astype(jnp.float32)).astype(x.dtype)

def rms_norm(x, g):
    xf = x.astype(jnp.float32)
    ms = jnp.mean(xf * xf, axis=-1, keepdims=True)
    return (xf * lax.rsqrt(ms + EPS) * g.astype(jnp.float32)).astype(x.dtype)

def rope(x, pos):
    half = QK_ROPE // 2
    inv = ROPE_BASE ** (-jnp.arange(half, dtype=jnp.float32) / half)
    ang = pos.astype(jnp.float32)[:, None] * inv[None, :]
    cos = jnp.cos(ang)[None, :, None, :]
    sin = jnp.sin(ang)[None, :, None, :]
    xf = x.astype(jnp.float32)
    x1, x2 = xf[..., :half], xf[..., half:]
    return jnp.concatenate([x1 * cos - x2 * sin, x1 * sin + x2 * cos], axis=-1).astype(x.dtype)

def rg_lru_group(u, gate_in, conv_w, conv_b, w_rgate, b_rgate, w_igate, b_igate, lru_lambda):
    bsz, seq, _ = u.shape
    xc = lax.conv_general_dilated(u, conv_w[:, None, :], window_strides=(1,),
                                  padding=[(CONV_WIDTH - 1, 0)],
                                  dimension_numbers=('NWC', 'WIO', 'NWC'),
                                  feature_group_count=LRU_WIDTH) + conv_b
    xb = xc.reshape(bsz, seq, LRU_BLOCKS, LRU_BLOCK)
    r = jax.nn.sigmoid(jnp.einsum('bsnc,ncd->bsnd', xb, w_rgate) + b_rgate).reshape(bsz, seq, LRU_WIDTH)
    i = jax.nn.sigmoid(jnp.einsum('bsnc,ncd->bsnd', xb, w_igate) + b_igate).reshape(bsz, seq, LRU_WIDTH)
    log_a = (-LRU_C * r.astype(jnp.float32)) * jax.nn.softplus(-lru_lambda.astype(jnp.float32))
    a = jnp.exp(log_a)
    drive = jnp.sqrt(-jnp.expm1(2.0 * log_a)) * (i * xc).astype(jnp.float32)

    def combine(left, right):
        a1, b1 = left
        a2, b2 = right
        return a1 * a2, a2 * b1 + b2

    _, h = lax.associative_scan(combine, (a, drive), axis=1)
    return h.astype(u.dtype) * jax.nn.gelu(gate_in)

def causal_block_attention(q, k, v):
    bsz, seq, nh, dk = q.shape
    nb = seq // Q_BLOCK
    qb = q.reshape(bsz, nb, Q_BLOCK, nh, dk).transpose(1, 0, 2, 3, 4)
    k_pos = jnp.arange(seq)

    def one_block(args):
        qi, bi = args
        s = jnp.einsum('bqhd,bkhd->bhqk', qi, k, preferred_element_type=jnp.float32)
        q_pos = bi * Q_BLOCK + jnp.arange(Q_BLOCK)
        s = jnp.where(k_pos[None, :] <= q_pos[:, None], s, -jnp.inf)
        p = jax.nn.softmax(s, axis=-1)
        return jnp.einsum('bhqk,bkhd->bqhd', p.astype(v.dtype), v)

    out = lax.map(one_block, (qb, jnp.arange(nb)))
    return out.transpose(1, 0, 2, 3, 4).reshape(bsz, seq, nh * V_HEAD)

def mla_group(q_lat, kv_lat, k_rope_raw, q_norm_g, w_q_up, kv_norm_g, w_kv_up, pos):
    bsz, seq, _ = q_lat.shape
    q = jnp.einsum('bsr,rhd->bshd', rms_norm(q_lat, q_norm_g), w_q_up)
    q = jnp.concatenate([q[..., :QK_NOPE], rope(q[..., QK_NOPE:], pos)], axis=-1)
    kv = jnp.einsum('bsr,rhd->bshd', rms_norm(kv_lat, kv_norm_g), w_kv_up)
    k_nope, v = kv[..., :QK_NOPE], kv[..., QK_NOPE:]
    k_pe = rope(k_rope_raw[:, :, None, :], pos)
    k = jnp.concatenate([k_nope, jnp.broadcast_to(k_pe, (bsz, seq, MLA_HEADS, QK_ROPE))], axis=-1)
    return causal_block_attention(q * (QK_HEAD ** -0.5), k, v)

def route(x2, router_w, router_bias):
    n_tok = x2.shape[0]
    s = jax.nn.sigmoid(jnp.einsum('nd,de->ne', x2, router_w, preferred_element_type=jnp.float32))
    s_sel = (s + router_bias.astype(jnp.float32)).reshape(n_tok, N_GROUPS, EXPERTS_PER_GROUP)
    grp_score = jnp.sum(lax.top_k(s_sel, 2)[0], axis=-1)
    best_g = jnp.argmax(grp_score, axis=-1)
    _, local = lax.top_k(s_sel[jnp.arange(n_tok), best_g], TOP_K)
    expert_idx = best_g[:, None] * EXPERTS_PER_GROUP + local
    w = jnp.take_along_axis(s, expert_idx, axis=1)
    return expert_idx, w / jnp.sum(w, axis=-1, keepdims=True)

def moe_ffn(x2, router_w, router_bias, w_exp_gate, w_exp_up, w_exp_down):
    n_tok, d = x2.shape
    n_asg = n_tok * TOP_K
    expert_idx, gates = route(x2, router_w, router_bias)
    flat_e = expert_idx.reshape(-1)
    order = jnp.argsort(flat_e)
    sorted_e = flat_e[order]
    tok = order // TOP_K
    counts = jnp.bincount(flat_e, length=N_EXPERTS)
    padded = (counts + MOE_BLOCK - 1) // MOE_BLOCK * MOE_BLOCK
    pad_end = jnp.cumsum(padded)
    pad_start = pad_end - padded
    start = jnp.cumsum(counts) - counts
    dest = pad_start[sorted_e] + (jnp.arange(n_asg) - start[sorted_e])
    n_blocks = -(-n_asg // MOE_BLOCK) + N_EXPERTS
    buf = jnp.zeros((n_blocks * MOE_BLOCK, d), x2.dtype).at[dest].set(x2[tok])
    block_expert = jnp.minimum(jnp.searchsorted(pad_end, jnp.arange(n_blocks) * MOE_BLOCK, side='right'),
                               N_EXPERTS - 1)

    def expert_block(args):
        xb, e = args
        hb = jax.nn.silu(xb @ w_exp_gate[e]) * (xb @ w_exp_up[e])
        return hb @ w_exp_down[e]

    yb = lax.map(expert_block, (buf.reshape(n_blocks, MOE_BLOCK, d), block_expert))
    y_sorted = yb.reshape(n_blocks * MOE_BLOCK, d)[dest]
    g_sorted = gates.reshape(-1)[order].astype(x2.dtype)
    return jax.ops.segment_sum(y_sorted * g_sorted[:, None], tok, num_segments=n_tok)

def hybrid_layer(x, w_in, conv_w, conv_b, w_rgate, b_rgate, w_igate, b_igate, lru_lambda,
                 q_norm_g, w_q_up, kv_norm_g, w_kv_up, out_norm_g, w_out, ln1_g, ln1_b,
                 router_w, router_bias, w_exp_gate, w_exp_up, w_exp_down, ln2_g, ln2_b):
    bsz, seq, d = x.shape
    pos = jnp.arange(seq)
    z = jnp.einsum('bsd,dc->bsc', x, w_in)
    o1 = LRU_WIDTH
    o2 = 2 * LRU_WIDTH
    o3 = o2 + Q_LORA
    o4 = o3 + KV_LORA
    u, gate_in, q_lat, kv_lat, k_rope_raw = jnp.split(z, [o1, o2, o3, o4], axis=-1)
    lru_out = rg_lru_group(u, gate_in, conv_w, conv_b, w_rgate, b_rgate, w_igate, b_igate, lru_lambda)
    mla_out = mla_group(q_lat, kv_lat, k_rope_raw, q_norm_g, w_q_up, kv_norm_g, w_kv_up, pos)
    mix = jnp.concatenate([rms_norm(lru_out, out_norm_g[:LRU_WIDTH]),
                           rms_norm(mla_out, out_norm_g[LRU_WIDTH:])], axis=-1)
    h = jnp.einsum('bsc,cd->bsd', mix, w_out)
    x = layer_norm(DN_ALPHA * x + h, ln1_g, ln1_b)
    f = moe_ffn(x.reshape(bsz * seq, d), router_w, router_bias, w_exp_gate, w_exp_up, w_exp_down)
    return layer_norm(DN_ALPHA * x + f.reshape(bsz, seq, d), ln2_g, ln2_b)

def setup_inputs(seed: int = 0) -> dict:
    key = jax.random.key(seed)
    ks = jax.random.split(key, 24)
    L, D = DEPTH, D_MODEL
    nrm = lambda k, shape, scale: jax.random.normal(k, shape, jnp.float32) * scale
    x = jax.random.normal(ks[0], (BATCH, SEQ, D), jnp.float32)
    w_in = nrm(ks[1], (L, D, IN_WIDTH), D ** -0.5)
    conv_w = nrm(ks[2], (L, CONV_WIDTH, LRU_WIDTH), CONV_WIDTH ** -0.5)
    conv_b = nrm(ks[3], (L, LRU_WIDTH), 0.02)
    w_rgate = nrm(ks[4], (L, LRU_BLOCKS, LRU_BLOCK, LRU_BLOCK), LRU_BLOCK ** -0.5)
    b_rgate = nrm(ks[5], (L, LRU_BLOCKS, LRU_BLOCK), 0.02)
    w_igate = nrm(ks[6], (L, LRU_BLOCKS, LRU_BLOCK, LRU_BLOCK), LRU_BLOCK ** -0.5)
    b_igate = nrm(ks[7], (L, LRU_BLOCKS, LRU_BLOCK), 0.02)
    a0 = jax.random.uniform(ks[8], (L, LRU_WIDTH), jnp.float32, 0.9, 0.999)
    lru_lambda = jnp.log(a0) - jnp.log1p(-a0)
    q_norm_g = 1.0 + nrm(ks[9], (L, Q_LORA), 0.02)
    w_q_up = nrm(ks[10], (L, Q_LORA, MLA_HEADS, QK_HEAD), Q_LORA ** -0.5)
    kv_norm_g = 1.0 + nrm(ks[11], (L, KV_LORA), 0.02)
    kv_scale = jnp.concatenate([jnp.ones((QK_NOPE,), jnp.float32), jnp.full((V_HEAD,), DN_BETA, jnp.float32)])
    w_kv_up = nrm(ks[12], (L, KV_LORA, MLA_HEADS, QK_NOPE + V_HEAD), KV_LORA ** -0.5) * kv_scale
    out_norm_g = 1.0 + nrm(ks[13], (L, MIX_WIDTH), 0.02)
    w_out = nrm(ks[14], (L, MIX_WIDTH, D), MIX_WIDTH ** -0.5 * DN_BETA)
    ln1_g = 1.0 + nrm(ks[15], (L, D), 0.02)
    ln1_b = nrm(ks[16], (L, D), 0.02)
    router_w = nrm(ks[17], (D, N_EXPERTS), D ** -0.5)
    router_bias = nrm(ks[18], (N_EXPERTS,), 0.01)
    w_exp_gate = nrm(ks[19], (L, N_EXPERTS, D, D_EXPERT), D ** -0.5)
    w_exp_up = nrm(ks[20], (L, N_EXPERTS, D, D_EXPERT), D ** -0.5)
    w_exp_down = nrm(ks[21], (L, N_EXPERTS, D_EXPERT, D), D_EXPERT ** -0.5 * DN_BETA)
    ln2_g = 1.0 + nrm(ks[22], (L, D), 0.02)
    ln2_b = nrm(ks[23], (L, D), 0.02)
    return {'x': x, 'w_in': w_in, 'conv_w': conv_w, 'conv_b': conv_b,
            'w_rgate': w_rgate, 'b_rgate': b_rgate, 'w_igate': w_igate, 'b_igate': b_igate,
            'lru_lambda': lru_lambda, 'q_norm_g': q_norm_g, 'w_q_up': w_q_up,
            'kv_norm_g': kv_norm_g, 'w_kv_up': w_kv_up, 'out_norm_g': out_norm_g, 'w_out': w_out,
            'ln1_g': ln1_g, 'ln1_b': ln1_b, 'router_w': router_w, 'router_bias': router_bias,
            'w_exp_gate': w_exp_gate, 'w_exp_up': w_exp_up, 'w_exp_down': w_exp_down,
            'ln2_g': ln2_g, 'ln2_b': ln2_b}

def reference(x, w_in, conv_w, conv_b, w_rgate, b_rgate, w_igate, b_igate, lru_lambda,
              q_norm_g, w_q_up, kv_norm_g, w_kv_up, out_norm_g, w_out, ln1_g, ln1_b,
              router_w, router_bias, w_exp_gate, w_exp_up, w_exp_down, ln2_g, ln2_b):
    for l in range(DEPTH):
        x = hybrid_layer(x, w_in[l], conv_w[l], conv_b[l], w_rgate[l], b_rgate[l], w_igate[l], b_igate[l],
                         lru_lambda[l], q_norm_g[l], w_q_up[l], kv_norm_g[l], w_kv_up[l], out_norm_g[l],
                         w_out[l], ln1_g[l], ln1_b[l], router_w, router_bias,
                         w_exp_gate[l], w_exp_up[l], w_exp_down[l], ln2_g[l], ln2_b[l])
    return x


_drawn_inputs = setup_inputs


def setup_inputs(seed=0):
    import zlib

    import numpy as np

    out = dict(_drawn_inputs(seed))
    spreads = {}
    factors = {'b_rgate': 8.0, 'b_igate': 7.842, 'q_norm_g': 3.954, 'out_norm_g': 2.841}
    for name, (base, spread) in spreads.items():
        noise = np.random.default_rng([zlib.crc32(name.encode()), seed]).standard_normal(out[name].shape)
        drawn = base * np.exp(spread * noise) if base else spread * noise
        out[name] = __import__('jax').numpy.asarray(drawn.astype(out[name].dtype))
    for name, factor in factors.items():
        out[name] = (out[name] * factor).astype(out[name].dtype)
    return out
```

```python
from contextlib import ExitStack

import concourse.bass as bass
from concourse import mybir

F32 = mybir.dt.float32
F32R = mybir.dt.float32r
I32 = mybir.dt.int32
ALU = mybir.AluOpType
ACT = mybir.ActivationFunctionType
AX = mybir.AxisListType

P = 128
D = 1024
SEQ = 512
DEPTH = 2
LRU = 512
HEADS = 4
ROPE = 64
QK_HEAD = 192
Q_LORA = 768
KV_LORA = 256
N_EXP = 16
N_GRP = 4
F_EXP = 512
EPS = 1e-6
ALPHA = float((2 * DEPTH) ** 0.25)
BIG = 1e30
KB = 1024

TT = SEQ // P
DT = D // P
LT = LRU // P
QT = Q_LORA // P
KT = KV_LORA // P
FT = F_EXP // P
HALF = D // 2
CH = 1024
RA = 4
RING = 12
PAIRS = RING // 2
MAX_BLOCKS = N_EXP - 1 + SEQ * 2 // P

N_IN = QT + KT + 1 + 2 * LT
C_K = N_IN
C_V = C_K + 1
C_QN = C_V + 1
C_QR = C_QN + HEADS
C_OUT = C_QR + HEADS
N_CHUNK = C_OUT + 8
M_K = N_IN
M_V = M_K + HEADS
M_QN = M_V + TT
M_QR = M_QN + HEADS
M_END = M_QR + HEADS


def chunk_width(n):
    return Q_LORA if C_QN <= n < C_OUT else CH


SQ_GROUPS = (QT, KT, LT, HEADS)


def sq_taken(kappa):
    added = 0
    for n in SQ_GROUPS:
        if kappa < n:
            return added + max(kappa, 1)
        kappa -= n
        added += n - 1


ACT_HI = (0, 1, 2, 4, 5, 6, 8, 9, 10)
POOL_LO = (1, 4, 6, 9, 11)

IDENT, ONES, TRI, DUP, ROT = 0, 128, 256, 384, 512
CMASK = ROT + SEQ
EW = CMASK + P
GW = EW + TT * N_EXP
N_CST = GW + TT * N_GRP
CONV_W, CONV_B, B_R, B_I, LAM = 0, 4 * LT, 5 * LT, 6 * LT, 7 * LT
QG = 8 * LT
OG = QG + QT + KT
N_PAR = OG + DT


def build(nc, a, out):
    with ExitStack() as ctx:
        base = (nc.sbuf_base + 63) // 64 * 64

        def at(kb, name, shape, dt=F32):
            return nc.alloc_sbuf_tensor_at(name, shape, dt, offset=base + int(kb * KB))

        def sem(name):
            return ctx.enter_context(nc.semaphore(name))

        x = at(0, "x", [P, TT, D])
        cst = at(16, "cst", [P, N_CST])
        rw = at(21, "rw", [P, DT * N_EXP])
        rb = at(21.5, "rb", [P, TT * N_EXP])
        par = at(21.75, "par", [P, N_PAR])
        small = at(22, "small", [P, 1024])
        lnbc = at(26, "lnbc", [P, 2, D])
        gatew = at(26, "gatew", [P, 2 * LT, P])
        raw_a = at(34, "raw_a", [P, RA, CH])
        hi_a = at(50, "hi_a", [P, RA, CH], F32R)
        lo_a = at(66, "lo_a", [P, RA, CH], F32R)
        raw_b = at(82, "raw_b", [P, RING - RA, CH])
        hi_b = at(114, "hi_b", [P, RING - RA, CH], F32R)
        lo_b = at(146, "lo_b", [P, RING - RA, CH], F32R)
        n_hi = at(82, "n_hi", [P, DT, SEQ], F32R)
        n_lo = at(98, "n_lo", [P, DT, SEQ], F32R)
        xt_hi = at(114, "xt_hi", [P, DT, SEQ], F32R)
        xt_lo = at(130, "xt_lo", [P, DT, SEQ], F32R)
        q = at(114, "q", [P, 2 * HEADS, SEQ])
        x1t = at(114, "x1t", [P, DT, SEQ])
        kn = at(130, "kn", [P, HEADS, SEQ])
        v = at(138, "v", [P, TT, HEADS * P])
        z_gate = at(146, "z_gate", [P, LT, SEQ])
        z_lat = at(154, "z_lat", [P, QT + KT, SEQ])
        pt = at(154, "pt", [P, 2, TT, SEQ])
        root = at(82, "root", [P, LT, SEQ])
        z_u = at(170, "z_u", [P, LT, 3 + SEQ])
        prob = at(179, "prob", [P, 2, SEQ])
        krot = at(179, "krot", [P, SEQ])
        sq = at(183, "sq", [P, 2, SEQ])
        acc = at(187, "acc", [P, 2, SEQ])
        rstd = at(191, "rstd", [P, SEQ])
        kr = at(193, "kr", [P, SEQ])
        xc = at(195, "xc", [P, 2, SEQ])
        rt = at(199, "rt", [P, LT, SEQ])
        xg = at(179, "xg", [P, D])
        xb_hi = at(183, "xb_hi", [P, DT, P], F32R)
        xb_lo = at(187, "xb_lo", [P, DT, P], F32R)
        ht_hi = at(191, "ht_hi", [P, FT, P], F32R)
        ht_lo = at(193, "ht_lo", [P, FT, P], F32R)
        sg = at(195, "sg", [P, F_EXP])
        hb = at(197, "hb", [P, F_EXP])
        yb = at(199, "yb", [P, D])
        yg = at(82, "yg", [P, 2 * TT, D])

        def hi(j):
            return hi_a[:, j, :] if j < RA else hi_b[:, j - RA, :]

        def lo(j):
            return lo_a[:, j, :] if j < RA else lo_b[:, j - RA, :]

        def raw(j):
            return raw_a[:, j, :] if j < RA else raw_b[:, j - RA, :]

        def f(ap):
            return ap.bitcast(F32)

        ident = cst[:, IDENT:IDENT + P]
        ones = cst[:, ONES:ONES + P]
        tri = cst[:, TRI:TRI + P]
        cmask = cst[:, CMASK:CMASK + P]
        dup = cst[:, DUP:DUP + P]
        rot = cst[:, ROT:ROT + SEQ]

        bank = [ctx.enter_context(nc.psum_tensor(f"bank{i}", [P, 512], F32)) for i in range(8)]

        col = [0]

        def cols(n):
            s = small[:, col[0]:col[0] + n]
            col[0] += n
            return s

        eps = cols(1)
        sp_a, sp_b, sp_c, sp_d, sp_e = (cols(LT) for _ in range(5))
        c4 = cols(LT)
        nmax, psum_, pinv = cols(16), cols(16), cols(16)
        stats = [cols(12) for _ in range(TT)]
        mv = [cols(2) for _ in range(TT)]
        std, rstd_t, nmr = cols(TT), cols(TT), cols(TT)
        s_e, sel, masked, pen, oh1, oh2, tmp, use, dst = (cols(TT * N_EXP) for _ in range(9))
        g_a, g_b, g_c, g_d, g_e, g_f = (cols(TT * N_GRP) for _ in range(6))
        t_a, w1, w2, wr = (cols(TT) for _ in range(4))
        gate = cols(2 * TT)
        cnt, nb, cum, base16 = (cols(N_EXP) for _ in range(4))
        idx = cols(2 * TT).bitcast(I32)
        nblk = cols(N_EXP).bitcast(I32)
        onecol = cols(N_EXP)
        dstk = cols(2 * TT)
        assert col[0] <= 1024

        xbuf = nc.dram_tensor("xbuf", (MAX_BLOCKS + 2, P, D), F32).ap()
        xrows = xbuf.rearrange("b p d -> (b p) d")

        init, filled = sem("init"), sem("filled")
        scat = sem("scat")
        scat_goal, gath_goal = nc.scalar.alloc_register("scat_goal"), nc.vector.alloc_register("gath_goal")
        names = """par_in gates_in ln1_in ln2_in xt_t xt_h xt_l gemm ev_dve ev_act a_hi a_lo
            sqd sqa sums_q sums_kv rs_std nrm_h nrm_l kdup krd xcd gmm gact ixd tanhd geld sqrtd lrud
            sc nm ex pn ptr pte pv mla opd vd stdd lnx lng lnb x1d x1e lg sgd used_d pfx nbd
            chain_d mixs_l mixs_m nz lnm c4d
            xg_in xbt hbt sgs hbd xbh xbh2 xbl htt hth htl yev1 yevd yst allst
            sp_abs sp_exp pad""".split()
        S = {n: sem(n) for n in names}
        raw_in = [sem(f"raw_in{i}") for i in range(RA)]
        pair_in = [sem(f"pair_in{i}") for i in range(PAIRS)]
        w_hi = [sem(f"w_hi{j}") for j in range(RING)]
        w_lo = [sem(f"w_lo{j}") for j in range(RING)]
        w_used = [sem(f"w_used{j}") for j in range(RING)]
        gath = [sem(f"gath{i}") for i in range(TT)]
        every = list(S.values()) + raw_in + pair_in + w_hi + w_lo + w_used

        def chunk_freed(n):
            if n < C_K:
                return S["gemm"], n + 1
            if n == C_K:
                return S["gemm"], M_V
            if n == C_V:
                return S["gemm"], M_QN
            if n < C_OUT:
                return S["gemm"], M_QN + (n - C_QN) + 1
            return S["opd"], n - C_OUT + 1

        def evac_done(m):
            if m < M_K:
                return S["ev_dve"], m + 1
            if m < M_QR:
                return S["ev_act"], m - M_K + 1
            return S["ev_dve"], M_K + m - M_QR + 1

        with nc.Block() as block:
            @block.sync
            def _(sp):
                sp.dma_start(x[:, :, :], a["x"][0].rearrange("(i p) d -> p i d", p=P)).then_inc(init, 16)
                sp.dma_start(cst[:, :], a["cst"][:, :]).then_inc(init, 16)
                sp.dma_start(rw[:, :], a["rw"][:, :]).then_inc(init, 16)
                sp.dma_start(rb[:, :], a["rb"][:, :]).then_inc(init, 16)
                sp.wait_ge(init, 64)

            @block.vector
            def _(dve):
                nc.vector.memset(eps, EPS)
                nc.vector.memset(onecol, 1.0)
                dve.reg_mov(gath_goal, 32)

            @block.scalar
            def _(act):
                act.reg_mov(scat_goal, 16 * 2 * TT)
                act.wait_ge(init, 64)
                for b in range(MAX_BLOCKS + 2):
                    act.dma_start(xbuf[b], cst[:, 0:D]).then_inc(filled, 16)

        with nc.Fori(0, DEPTH) as ly:
            with nc.Block() as block:
                @block.sync
                def _(sp):
                    sp.dma_start(par[:, :], a["par"][bass.ds(ly, 1)].rearrange("l p n -> (l p) n")).then_inc(S["par_in"], 16)
                    sp.dma_start(gatew[:, :, :], a["gw"][bass.ds(ly, 1)].rearrange("l p (t n) -> (l p) t n", n=P)).then_inc(S["gates_in"], 16)
                    for n in range(N_CHUNK):
                        if n >= RA:
                            sp.wait_ge(S["a_lo"], n - RA + 1)
                        w = chunk_width(n)
                        sp.dma_start(raw(n % RA)[:, 0:w], a["wm"][bass.ds(ly, 1), n, :, 0:w].rearrange("l p n -> (l p) n")).then_inc(raw_in[n % RA], 16)
                    sp.wait_ge(S["gmm"], 2 * LT)
                    sp.dma_start(lnbc[:, :, :], a["ln"][bass.ds(ly, 1), 0].rearrange("l c d -> (l c) d").partition_broadcast(P)).then_inc(S["ln1_in"], 16)

                    sp.wait_ge(S["a_lo"], N_CHUNK)
                    for t in range(RA // 2):
                        sp.dma_start(raw_a[:, 2 * t:2 * t + 2, :], a["we"][bass.ds(ly, 1), 0, t].rearrange("l p n -> (l p) n").rearrange("p (c n) -> p c n", c=2)).then_inc(pair_in[t], 16)
                    sp.wait_ge(S["opd"], 8)
                    for t in range(RA // 2, PAIRS):
                        sp.dma_start(raw_b[:, 2 * t - RA:2 * t - RA + 2, :], a["we"][bass.ds(ly, 1), 0, t].rearrange("l p n -> (l p) n").rearrange("p (c n) -> p c n", c=2)).then_inc(pair_in[t], 16)
                    lap = sp.alloc_register("sp_lap")
                    sp.reg_mov(lap, 2)
                    with sp.Fori(1, N_EXP) as e:
                        for t in range(PAIRS):
                            sp.wait_ge(w_lo[2 * t], lap)
                            sp.wait_ge(w_lo[2 * t + 1], lap)
                            dst = raw_a[:, 2 * t:2 * t + 2, :] if 2 * t < RA else raw_b[:, 2 * t - RA:2 * t - RA + 2, :]
                            sp.dma_start(dst, a["we"][bass.ds(ly, 1), bass.ds(e, 1), t].rearrange("l e p n -> (l e p) n").rearrange("p (c n) -> p c n", c=2)).then_inc(pair_in[t], 16)
                        sp.reg_add(lap, lap, 1)
                    sp.wait_ge(S["lnb"], TT)
                    sp.dma_start(lnbc[:, :, :], a["ln"][bass.ds(ly, 1), 1].rearrange("l c d -> (l c) d").partition_broadcast(P)).then_inc(S["ln2_in"], 16)

                @block.tensor
                def _(pe):
                    def mm3(o, wh, wl, mh, ml, first, last):
                        nc.tensor.matmul(o, wh, mh, start=first, stop=False)
                        nc.tensor.matmul(o, wh, ml, start=False, stop=False)
                        return nc.tensor.matmul(o, wl, mh, start=False, stop=last)

                    for c in range(DT):
                        if c >= 2:
                            pe.wait_ge(S["xt_l"], c - 1)
                        for i in range(TT):
                            m = nc.tensor.transpose(bank[2 + c % 2][:, i * P:(i + 1) * P], x[:, i, c * P:(c + 1) * P], ident)
                        m.then_inc(S["xt_t"], 1)

                    for n in range(N_IN):
                        pe.wait_ge(S["a_lo"], n + 1)
                        if n == 0:
                            pe.wait_ge(S["xt_l"], DT)
                        if n >= 2:
                            pe.wait_ge(*evac_done(n - 2))
                        wh, wl = hi(n % RA), lo(n % RA)
                        for k in range(DT):
                            m = mm3(bank[n % 2][:, :], wh[:, k * P:(k + 1) * P], wl[:, k * P:(k + 1) * P], xt_hi[:, k, :], xt_lo[:, k, :], k == 0, k == DT - 1)
                        m.then_inc(S["gemm"], 1)
                        if n == QT + KT + 3:
                            pe.wait_ge(S["ev_dve"], QT + KT + 1)
                            nc.tensor.matmul(bank[7][:, :], dup, krot[:, :], start=True, stop=True).then_inc(S["kdup"], 1)
                            pe.wait_ge(S["sqa"], QT - 1)
                            nc.tensor.matmul(bank[6][:, :], ones, acc[:, 0, :], start=True, stop=True).then_inc(S["sums_q"], 1)
                            pe.wait_ge(S["sqa"], QT + KT - 2)
                            nc.tensor.matmul(bank[5][:, :], ones, acc[:, 1, :], start=True, stop=True).then_inc(S["sums_kv"], 1)

                    def up(m0, n, outs, kt, tile0, values=False):
                        pe.wait_ge(S["a_lo"], n + 1)
                        wh, wl = hi(n % RA), lo(n % RA)
                        for h in range(outs):
                            pe.wait_ge(*evac_done(m0 + h - 2))
                            for k in range(kt):
                                o = bank[(m0 + h) % 2][:, :]
                                if values:
                                    s = slice(h * P, (h + 1) * P)
                                    m = mm3(o, n_hi[:, tile0 + k, s], n_lo[:, tile0 + k, s], wh[:, k * SEQ:(k + 1) * SEQ], wl[:, k * SEQ:(k + 1) * SEQ], k == 0, k == kt - 1)
                                else:
                                    s = slice((k * outs + h) * P, (k * outs + h + 1) * P)
                                    m = mm3(o, wh[:, s], wl[:, s], n_hi[:, tile0 + k, :], n_lo[:, tile0 + k, :], k == 0, k == kt - 1)
                            m.then_inc(S["gemm"], 1)

                    def gates(t):
                        pe.wait_ge(S["xcd"], t + 1)
                        if t:
                            pe.wait_ge(S["gact"], 2 * t)
                        else:
                            pe.wait_ge(S["gates_in"], 16)
                            pe.wait_ge(S["rs_std"], 2)
                        nc.tensor.matmul(bank[4][:, :], gatew[:, t, :], xc[:, t % 2, :], start=True, stop=True).then_inc(S["gmm"], 1)
                        nc.tensor.matmul(bank[5][:, :], gatew[:, LT + t, :], xc[:, t % 2, :], start=True, stop=True).then_inc(S["gmm"], 1)

                    pe.wait_ge(S["nrm_l"], KT)
                    up(M_K, C_K, HEADS, KT, QT)
                    gates(0)
                    up(M_V, C_V, TT, KT, QT, values=True)
                    gates(1)
                    pe.wait_ge(S["nrm_l"], QT + KT)
                    for h in range(HEADS):
                        up(M_QN + h, C_QN + h, 1, QT, 0)
                    gates(2)
                    for h in range(HEADS):
                        up(M_QR + h, C_QR + h, 1, QT, 0)
                    gates(3)

                    def score(s):
                        h, i = s // TT, s % TT
                        w = (i + 1) * P
                        o = bank[4 + s % 2]
                        if s < 2:
                            pe.wait_ge(S["gact"], 2 * LT)
                        else:
                            pe.wait_ge(S["ex"], s - 1)
                        if s == 0:
                            pe.wait_ge(*evac_done(M_QR - 1))
                            pe.wait_ge(*evac_done(M_END - 1))
                            pe.wait_ge(S["krd"], 1)
                        nc.tensor.matmul(o[:, 0:w], q[:, h, i * P:w], kn[:, h, 0:w], start=True, stop=False)
                        nc.tensor.matmul(o[:, 0:w], q[:, HEADS + h, i * P:w], kr[:, 0:w], start=False, stop=False)
                        nc.tensor.matmul(o[:, i * P:w], ident, cmask, start=False, stop=True).then_inc(S["sc"], 1)

                    def values(h):
                        pe.wait_ge(S["pte"], TT * (h + 1))
                        if h:
                            pe.wait_ge(S["mla"], h)
                        for j in range(TT):
                            m = nc.tensor.matmul(bank[6][:, j * P:SEQ], v[:, j, h * P:(h + 1) * P], pt[:, h % 2, j, j * P:SEQ], start=(j == 0), stop=(j == TT - 1))
                        m.then_inc(S["pv"], 1)

                    STEPS = HEADS * TT
                    score(0)
                    for s in range(STEPS):
                        if s + 1 < STEPS:
                            score(s + 1)
                        pe.wait_ge(S["pn"], s + 1)
                        if s >= 2:
                            pe.wait_ge(S["pte"], s - 1)
                        for j in range(s % TT + 1):
                            m = nc.tensor.transpose(bank[2 + s % 2][:, j * P:(j + 1) * P], prob[:, s % 2, j * P:(j + 1) * P], ident)
                        m.then_inc(S["ptr"], 1)
                        if s % TT == 0 and s:
                            values(s // TT - 1)
                    values(HEADS - 1)

                    pe.wait_ge(S["sqa"], QT + KT - 2 + LT - 1)
                    nc.tensor.matmul(bank[7][:, :], ones, acc[:, 0, :], start=True, stop=True).then_inc(S["mixs_l"], 1)
                    pe.wait_ge(S["sqa"], QT + KT - 2 + 2 * (LT - 1))
                    nc.tensor.matmul(bank[5][:, :], ones, acc[:, 1, :], start=True, stop=True).then_inc(S["mixs_m"], 1)

                    for half in range(2):
                        for c in range(4):
                            pe.wait_ge(S["a_lo"], C_OUT + 4 * half + c + 1)
                            pe.wait_ge(S["nrm_l"], QT + KT + 2 * c + 2)
                            wh, wl = hi((C_OUT + c) % RA), lo((C_OUT + c) % RA)
                            for i in range(TT):
                                for kk in range(2):
                                    s = slice(i * P, (i + 1) * P)
                                    m = mm3(bank[4 * half + i][:, :], n_hi[:, 2 * c + kk, s], n_lo[:, 2 * c + kk, s], wh[:, kk * HALF:(kk + 1) * HALF], wl[:, kk * HALF:(kk + 1) * HALF],
                                            c == 0 and kk == 0, c == 3 and kk == 1)
                            m.then_inc(S["opd"], 1)

                    for i in range(TT):
                        pe.wait_ge(S["lnb"], i + 1)
                        for c in range(DT):
                            m = nc.tensor.transpose(bank[i + c // 4 * 4][:, c % 4 * P:(c % 4 + 1) * P], x[:, i, c * P:(c + 1) * P], ident)
                        m.then_inc(S["x1d"], 1)
                        pe.wait_ge(S["x1e"], i + 1)
                        for k in range(DT):
                            m = nc.tensor.matmul(bank[i][:, 0:N_EXP], x1t[:, k, i * P:(i + 1) * P], rw[:, k * N_EXP:(k + 1) * N_EXP], start=(k == 0), stop=(k == DT - 1))
                        m.then_inc(S["lg"], 1)

                    pe.wait_ge(S["used_d"], 1)
                    for i in range(TT):
                        for j in range(i + 1):
                            nc.tensor.matmul(bank[4][:, i * N_EXP:(i + 1) * N_EXP], tri if j == i else ones, use[:, j * N_EXP:(j + 1) * N_EXP], start=(j == 0), stop=(j == i))
                    for j in range(TT):
                        m = nc.tensor.matmul(bank[7][:, 0:N_EXP], ones, use[:, j * N_EXP:(j + 1) * N_EXP], start=(j == 0), stop=(j == TT - 1))
                    m.then_inc(S["pfx"], 1)

                    def turn_x(half, s):
                        for c in range(4 * half, 4 * half + 4):
                            m = nc.tensor.transpose(bank[2 + half][:, c % 4 * P:(c % 4 + 1) * P], xg[:, c * P:(c + 1) * P], ident)
                        m.then_inc(s, 1)

                    g, g16, lap = (pe.alloc_register(n) for n in ("pe_g", "pe_g16", "pe_lap"))
                    pe.reg_mov(g, 1)
                    pe.reg_mov(g16, 32)
                    pe.reg_mov(lap, 2)
                    pe.wait_ge(S["nbd"], 1)
                    pe.wait_ge(S["xg_in"], 16)
                    turn_x(0, S["xbt"])
                    turn_x(1, S["hbt"])
                    with pe.Fori(0, N_EXP) as e:
                        blocks = pe.value_load(nblk[0:1, bass.ds(e, 1)], min_val=1, max_val=TT)
                        with pe.Fori(0, blocks):
                            pe.wait_ge(S["xbl"], g)
                            for side in range(2):
                                for j in range(4 * side, 4 * side + 4):
                                    pe.wait_ge(w_lo[j], lap)
                                    for kk in range(2):
                                        k = 2 * (j % 4) + kk
                                        m = mm3(bank[side][:, :], xb_hi[:, k, :], xb_lo[:, k, :], hi(j)[:, kk * F_EXP:(kk + 1) * F_EXP], lo(j)[:, kk * F_EXP:(kk + 1) * F_EXP], k == 0, k == DT - 1)
                                    m.then_inc(w_used[j], 1)
                            pe.wait_ge(S["xg_in"], g16)
                            turn_x(0, S["xbt"])
                            pe.wait_ge(S["hbd"], g)
                            for c in range(FT):
                                m = nc.tensor.transpose(bank[4][:, c * P:(c + 1) * P], hb[:, c * P:(c + 1) * P], ident)
                            m.then_inc(S["htt"], 1)
                            turn_x(1, S["hbt"])
                            pe.wait_ge(S["yevd"], g)
                            pe.wait_ge(S["htl"], g)
                            for j in range(8, RING):
                                pe.wait_ge(w_lo[j], lap)
                                for half in range(2):
                                    m = mm3(bank[5 + half][:, :], ht_hi[:, j - 8, :], ht_lo[:, j - 8, :], hi(j)[:, half * HALF:(half + 1) * HALF], lo(j)[:, half * HALF:(half + 1) * HALF], j == 8, j == RING - 1)
                                m.then_inc(w_used[j], 1)
                            pe.reg_add(g, g, 1)
                            pe.reg_add(g16, g16, 16)
                        pe.reg_add(lap, lap, 1)

                @block.scalar
                def _(act):
                    def split(n):
                        w = chunk_width(n)
                        if n >= RA:
                            act.wait_ge(*chunk_freed(n - RA))
                        act.wait_ge(raw_in[n % RA], 16 * (n // RA + 1))
                        nc.scalar.activation(hi(n % RA)[:, 0:w], raw(n % RA)[:, 0:w], ACT.Copy).then_inc(S["a_hi"], 1)

                    def upper(tile, src):
                        nrm[0] += 1
                        act.wait_ge(S["nz"], nrm[0])
                        nc.scalar.activation(n_hi[:, tile, :], src, ACT.Copy).then_inc(S["nrm_h"], 1)

                    def square(kappa, src):
                        if kappa >= 2:
                            act.wait_ge(S["sqa"], sq_taken(kappa - 2))
                        nc.scalar.activation(sq[:, kappa % 2, :], src, ACT.Square).then_inc(S["sqd"], 1)

                    def deviation(src, width):
                        nc.scalar.activation(rstd[:, :], src[:, :], ACT.Sqrt, bias=eps, scale=1.0 / width).then_inc(S["rs_std"], 1)

                    nrm = [0]
                    for c in range(DT):
                        act.wait_ge(S["xt_t"], c + 1)
                        nc.scalar.activation(xt_hi[:, c, :], bank[2 + c % 2][:, :], ACT.Copy).then_inc(S["xt_h"], 1)
                    act.wait_ge(S["sp_abs"], 1)
                    nc.scalar.activation(sp_e, sp_a, ACT.Exp, scale=-1.0).then_inc(S["sp_exp"], 1)
                    for n in range(RA):
                        split(n)
                    for n in range(N_IN):
                        split(n + RA)
                        if n < QT + KT:
                            act.wait_ge(S["ev_dve"], n + 1)
                            square(n, z_lat[:, n, :])
                        if n == N_IN - 5:
                            act.wait_ge(S["kdup"], 1)
                            nc.scalar.activation(kr[:, :], bank[7][:, :], ACT.Copy).then_inc(S["krd"], 1)
                            act.wait_ge(S["sums_kv"], 1)
                            deviation(bank[5], KV_LORA)
                            for k in range(KT):
                                upper(QT + k, z_lat[:, QT + k, :])
                            act.wait_ge(S["sums_q"], 1)
                            deviation(bank[6], Q_LORA)
                        if N_IN - 5 < n < N_IN - 1:
                            for k in range(2):
                                tile = 2 * (n - N_IN + 4) + k
                                upper(tile, z_lat[:, tile, :])

                    def leave(m, dst, scale=1.0):
                        act.wait_ge(S["gemm"], m + 1)
                        nc.scalar.activation(dst, bank[m % 2][:, :], ACT.Copy, scale=scale).then_inc(S["ev_act"], 1)

                    def gates(t):
                        act.wait_ge(S["gmm"], 2 * t + 1)
                        nc.scalar.activation(rt[:, t, :], bank[4][:, :], ACT.Sigmoid, bias=par[:, B_R + t:B_R + t + 1]).then_inc(S["gact"], 1)
                        act.wait_ge(S["gmm"], 2 * t + 2)
                        nc.scalar.activation(z_u[:, t, 3:3 + SEQ], bank[5][:, :], ACT.Sigmoid, bias=par[:, B_I + t:B_I + t + 1]).then_inc(S["gact"], 1)
                        act.wait_ge(S["c4d"], 1)
                        act.wait_ge(S["gact"], 2 * t + 2)
                        nc.scalar.activation(rt[:, t, :], rt[:, t, :], ACT.Tanh, scale=c4[:, t:t + 1]).then_inc(S["tanhd"], 1)

                    for h in range(HEADS):
                        leave(M_K + h, kn[:, h, :])
                    split(C_K + RA)
                    gates(0)
                    for i in range(TT):
                        leave(M_V + i, v[:, i, :])
                    split(C_V + RA)
                    gates(1)
                    for h in range(HEADS):
                        leave(M_QN + h, q[:, h, :], QK_HEAD ** -0.5)
                        split(C_QN + h + RA)
                    gates(2)
                    for h in range(HEADS):
                        split(C_QR + h + RA)
                    gates(3)
                    act.wait_ge(S["tanhd"], LT)
                    for t in range(LT):
                        nc.scalar.activation(root[:, t, :], rt[:, t, :], ACT.Sqrt).then_inc(S["sqrtd"], 1)
                    for t in range(LT):
                        nc.scalar.activation(z_gate[:, t, :], z_gate[:, t, :], ACT.Gelu_apprx_tanh).then_inc(S["geld"], 1)

                    def leave_p(s):
                        h, i = s // TT, s % TT
                        act.wait_ge(S["ptr"], s + 1)
                        if h >= 2 and i == 0:
                            act.wait_ge(S["pv"], h - 1)
                        nc.scalar.activation(pt[:, h % 2, 0:i + 1, i * P:(i + 1) * P], bank[2 + s % 2][:, 0:(i + 1) * P].rearrange("p (j c) -> p j c", c=P), ACT.Copy).then_inc(S["pte"], 1)

                    STEPS = HEADS * TT
                    for s in range(STEPS):
                        w = (s % TT + 1) * P
                        act.wait_ge(S["nm"], s + 1)
                        if s >= 2:
                            act.wait_ge(S["ptr"], s - 1)
                        nc.scalar.activation(prob[:, s % 2, 0:w], bank[4 + s % 2][:, 0:w], ACT.Exp, bias=nmax[:, s:s + 1], accum_out=psum_[:, s:s + 1]).then_inc(S["ex"], 1)
                        if s:
                            leave_p(s - 1)
                        if s % TT == 3 and s > TT:
                            t = s // TT - 1
                            act.wait_ge(S["lrud"], t + 1)
                            square(QT + KT + t, z_gate[:, t, :])
                    leave_p(STEPS - 1)
                    act.wait_ge(S["lrud"], LT)
                    square(QT + KT + LT - 1, z_gate[:, LT - 1, :])
                    for h in range(HEADS):
                        act.wait_ge(S["mla"], h + 1)
                        square(QT + KT + LT + h, q[:, h, :])
                    act.wait_ge(S["mixs_l"], 1)
                    deviation(bank[7], LRU)
                    for t in range(LT):
                        upper(t, z_gate[:, t, :])
                    act.wait_ge(S["mixs_m"], 1)
                    deviation(bank[5], HEADS * P)
                    for h in range(HEADS):
                        upper(LT + h, q[:, h, :])
                    for n in range(C_OUT + 4, N_CHUNK):
                        split(n)

                    def norm(k):
                        for i in range(TT):
                            act.wait_ge(S["vd"], TT * k + i + 1)
                            nc.scalar.activation(std[:, i:i + 1], mv[i][:, 1:2], ACT.Sqrt, bias=eps).then_inc(S["stdd"], 1)
                            act.wait_ge(S["lnx"], TT * k + i + 1)
                            nc.scalar.activation(x[:, i, :], x[:, i, :], ACT.Identity, bias=nmr[:, i:i + 1], scale=rstd_t[:, i:i + 1]).then_inc(S["lng"], 1)

                    norm(0)
                    for i in range(TT):
                        act.wait_ge(S["x1d"], i + 1)
                        s = slice(i * P, (i + 1) * P)
                        nc.scalar.activation(x1t[:, 0:4, s], bank[i][:, :].rearrange("p (k c) -> p k c", c=P), ACT.Copy)
                        nc.scalar.activation(x1t[:, 4:8, s], bank[4 + i][:, :].rearrange("p (k c) -> p k c", c=P), ACT.Copy).then_inc(S["x1e"], 1)
                        act.wait_ge(S["lg"], i + 1)
                        nc.scalar.activation(s_e[:, i * N_EXP:(i + 1) * N_EXP], bank[i][:, 0:N_EXP], ACT.Sigmoid).then_inc(S["sgd"], 1)

                    g, gp, g16, lap, lap16, used = (act.alloc_register(n) for n in ("a_g", "a_gp", "a_g16", "a_lap", "a_lap16", "a_used"))
                    xrow, yrow = act.alloc_register("a_xrow"), act.alloc_register("a_yrow")
                    act.reg_mov(g, 1)
                    act.reg_mov(gp, 2)
                    act.reg_mov(g16, 16)
                    act.reg_mov(lap, 1)
                    act.reg_mov(lap16, 16)
                    act.reg_mov(used, 1)
                    act.reg_mov(xrow, 2)
                    act.reg_mov(yrow, 0)

                    def upper_w(j):
                        act.wait_ge(w_used[j], used)
                        act.wait_ge(pair_in[j // 2], lap16)
                        nc.scalar.activation(hi(j), raw(j), ACT.Copy).then_inc(w_hi[j], 1)

                    def upper_x(count):
                        act.wait_ge(S["xbt"], count)
                        nc.scalar.activation(xb_hi[:, 0:4, :], bank[2][:, :].rearrange("p (k c) -> p k c", c=P), ACT.Copy).then_inc(S["xbh"], 1)
                        act.wait_ge(S["hbt"], count)
                        nc.scalar.activation(xb_hi[:, 4:8, :], bank[3][:, :].rearrange("p (k c) -> p k c", c=P), ACT.Copy).then_inc(S["xbh2"], 1)

                    for j in ACT_HI:
                        upper_w(j)
                    act.reg_add(lap16, lap16, 16)
                    act.wait_ge(scat, scat_goal)
                    act.dma_start(xg[:, :], xbuf[0]).then_inc(S["xg_in"], 16)
                    upper_x(1)
                    act.dma_start(xg[:, :], xbuf[1]).then_inc(S["xg_in"], 16)

                    def one_block(split_next):
                        if split_next:
                            act.wait_ge(w_used[3], gp)
                        act.wait_ge(w_used[3], gp)
                        nc.scalar.activation(sg[:, :], bank[0][:, :], ACT.Silu).then_inc(S["sgs"], 1)
                        if split_next:
                            for j in ACT_HI[0:4]:
                                upper_w(j)
                        act.wait_ge(S["htt"], g)
                        nc.scalar.activation(ht_hi[:, :, :], bank[4][:, :].rearrange("p (k c) -> p k c", c=P), ACT.Copy).then_inc(S["hth"], 1)
                        upper_x(gp)
                        act.dma_start(xg[:, :], xbuf[bass.ds(act.snap(xrow, min_val=0, max_val=MAX_BLOCKS + 1), 1)].rearrange("b p d -> (b p) d")).then_inc(S["xg_in"], 16)
                        if split_next:
                            for j in ACT_HI[4:8]:
                                upper_w(j)
                        act.wait_ge(w_used[RING - 1], gp)
                        act.wait_ge(S["yst"], g16)
                        nc.scalar.activation(yb[:, 0:HALF], bank[5][:, :], ACT.Copy).then_inc(S["yev1"], 1)
                        nc.scalar.activation(yb[:, HALF:D], bank[6][:, :], ACT.Copy).then_inc(S["yevd"], 1)
                        act.wait_ge(S["yevd"], gp)
                        act.dma_start(xbuf[bass.ds(act.snap(yrow, min_val=0, max_val=MAX_BLOCKS - 1), 1)].rearrange("b p d -> (b p) d"), yb[:, :]).then_inc(S["yst"], 16)
                        if split_next:
                            for j in ACT_HI[8:]:
                                upper_w(j)
                        for r, by in ((g, 1), (gp, 1), (g16, 16), (xrow, 1), (yrow, 1)):
                            act.reg_add(r, r, by)

                    act.reg_add(scat_goal, scat_goal, 16 * 2 * TT)
                    act.wait_ge(S["nbd"], 1)

                    def expert(e, split_next):
                        blocks = act.value_load(nblk[0:1, bass.ds(e, 1)] if split_next else nblk[0:1, N_EXP - 1:N_EXP], min_val=1, max_val=TT)
                        with act.If(blocks > 1):
                            with act.Fori(1, blocks):
                                one_block(False)
                                act.reg_add(used, used, 1)
                        act.reg_add(used, used, 1)
                        one_block(split_next)

                    with act.Fori(0, N_EXP - 1) as e:
                        expert(e, True)
                        act.reg_add(lap16, lap16, 16)
                    expert(None, False)
                    act.wait_ge(S["yst"], g16)
                    act.wait_ge(S["xg_in"], g16)
                    nc.scalar.activation(small[:, 1023:1024], eps, ACT.Copy).then_inc(S["allst"], 1)
                    norm(1)

                @block.vector
                def _(dve):
                    done = [0]

                    def link(ins):
                        done[0] += 1
                        ins.then_inc(S["chain_d"], 1)
                        dve.wait_ge(S["chain_d"], done[0])

                    def split(n):
                        w = chunk_width(n)
                        dve.wait_ge(S["a_hi"], n + 1)
                        nc.vector.tensor_tensor(lo(n % RA)[:, 0:w], raw(n % RA)[:, 0:w], f(hi(n % RA)[:, 0:w]), ALU.subtract).then_inc(S["a_lo"], 1)

                    nrm = [0]

                    def lower(tile, src):
                        nrm[0] += 1
                        dve.wait_ge(S["nrm_h"], nrm[0])
                        nc.vector.tensor_tensor(n_lo[:, tile, :], src, f(n_hi[:, tile, :]), ALU.subtract).then_inc(S["nrm_l"], 1)

                    def normalise(which, tiles):
                        dve.wait_ge(S["rs_std"], which)
                        link(nc.vector.reciprocal(rstd[:, :], rstd[:, :]))
                        for tile, src, g in tiles:
                            nc.vector.scalar_tensor_tensor(out=src, in0=src, scalar=par[:, g:g + 1], in1=rstd[:, :], op0=ALU.mult, op1=ALU.mult).then_inc(S["nz"], 1)
                        for tile, src, g in tiles:
                            lower(tile, src)

                    dve.wait_ge(S["par_in"], 16)
                    lam = par[:, LAM:LAM + LT]
                    link(nc.vector.tensor_scalar(sp_b, lam, -1.0, None, ALU.mult))
                    nc.vector.tensor_tensor(sp_a, lam, sp_b, ALU.max).then_inc(S["sp_abs"], 1)
                    for c in range(DT):
                        dve.wait_ge(S["xt_h"], c + 1)
                        nc.vector.tensor_tensor(xt_lo[:, c, :], bank[2 + c % 2][:, :], f(xt_hi[:, c, :]), ALU.subtract).then_inc(S["xt_l"], 1)
                    for n in range(RA):
                        split(n)
                    dve.wait_ge(S["sp_exp"], 1)
                    link(nc.vector.tensor_scalar(sp_c, sp_e, 2.0, None, ALU.add))
                    link(nc.vector.reciprocal(sp_c, sp_c))
                    link(nc.vector.tensor_tensor(sp_c, sp_c, sp_e, ALU.mult))
                    link(nc.vector.tensor_tensor(sp_d, sp_c, sp_c, ALU.mult))
                    link(nc.vector.tensor_scalar(sp_a, sp_d, 1.0 / 17, 1.0 / 15, ALU.mult, ALU.add))
                    for k in (13, 11, 9, 7, 5, 3, 1):
                        link(nc.vector.tensor_tensor(sp_a, sp_a, sp_d, ALU.mult))
                        link(nc.vector.tensor_scalar(sp_a, sp_a, 1.0 / k, None, ALU.add))
                    link(nc.vector.tensor_tensor(sp_a, sp_a, sp_c, ALU.mult))
                    link(nc.vector.tensor_scalar(sp_b, sp_b, 0.0, None, ALU.max))
                    link(nc.vector.scalar_tensor_tensor(out=sp_a, in0=sp_a, scalar=2.0, in1=sp_b, op0=ALU.mult, op1=ALU.add))
                    nc.vector.tensor_scalar(c4, sp_a, 4.0, None, ALU.mult).then_inc(S["c4d"], 1)

                    for n in range(N_IN):
                        dve.wait_ge(S["gemm"], n + 1)
                        o = bank[n % 2]
                        if n < QT + KT:
                            m = nc.vector.tensor_copy(z_lat[:, n, :], o[:, :])
                        elif n == QT + KT:
                            m = nc.vector.tensor_tensor(krot[:, :], o[:, :], rot, ALU.mult)
                        elif n < QT + KT + 1 + LT:
                            m = nc.vector.tensor_copy(z_u[:, n - QT - KT - 1, 3:3 + SEQ], o[:, :])
                        else:
                            m = nc.vector.tensor_copy(z_gate[:, n - QT - KT - 1 - LT, :], o[:, :])
                        m.then_inc(S["ev_dve"], 1)
                        split(n + RA)
                        if n == N_IN - 5:
                            normalise(1, [(QT + k, z_lat[:, QT + k, :], QG + QT + k) for k in range(KT)])
                            dve.wait_ge(S["rs_std"], 2)
                            link(nc.vector.reciprocal(rstd[:, :], rstd[:, :]))
                        if N_IN - 5 < n < N_IN - 1:
                            for k in range(2):
                                tile = 2 * (n - N_IN + 4) + k
                                nc.vector.scalar_tensor_tensor(out=z_lat[:, tile, :], in0=z_lat[:, tile, :], scalar=par[:, QG + tile:QG + tile + 1], in1=rstd[:, :], op0=ALU.mult, op1=ALU.mult).then_inc(S["nz"], 1)
                            for k in range(2):
                                tile = 2 * (n - N_IN + 4) + k
                                lower(tile, z_lat[:, tile, :])

                    def conv(t):
                        if t == 0:
                            dve.wait_ge(S["pad"], 1)
                        if t >= 2:
                            dve.wait_ge(S["gmm"], 2 * (t - 1))
                            dve.wait_ge(S["ixd"], t - 1)
                        o = xc[:, t % 2, :]
                        link(nc.vector.tensor_scalar(o, z_u[:, t, 3:3 + SEQ], par[:, CONV_W + 3 * LT + t:CONV_W + 3 * LT + t + 1], par[:, CONV_B + t:CONV_B + t + 1], ALU.mult, ALU.add))
                        for w in range(3):
                            m = nc.vector.scalar_tensor_tensor(out=o, in0=z_u[:, t, w:w + SEQ], scalar=par[:, CONV_W + w * LT + t:CONV_W + w * LT + t + 1], in1=o, op0=ALU.mult, op1=ALU.add)
                            if w < 2:
                                link(m)
                        m.then_inc(S["xcd"], 1)

                    def gated_in(t):
                        dve.wait_ge(S["gact"], 2 * t + 2)
                        dve.wait_ge(S["xcd"], t + 1)
                        nc.vector.tensor_tensor(z_u[:, t, 3:3 + SEQ], z_u[:, t, 3:3 + SEQ], xc[:, t % 2, :], ALU.mult).then_inc(S["ixd"], 1)

                    conv(0)
                    conv(1)
                    split(C_K + RA)
                    gated_in(0)
                    conv(2)
                    split(C_V + RA)
                    gated_in(1)
                    conv(3)
                    for h in range(HEADS):
                        split(C_QN + h + RA)
                    gated_in(2)
                    for h in range(HEADS):
                        dve.wait_ge(S["gemm"], M_QR + h + 1)
                        nc.vector.scalar_tensor_tensor(out=q[:, HEADS + h, :], in0=bank[(M_QR + h) % 2][:, :], scalar=QK_HEAD ** -0.5, in1=rot, op0=ALU.mult, op1=ALU.mult).then_inc(S["ev_dve"], 1)
                        split(C_QR + h + RA)
                    gated_in(3)

                    def recur(t):
                        inv, decay = xc[:, 0, :], xc[:, 1, :]
                        u = z_u[:, t, 3:3 + SEQ]
                        dve.wait_ge(S["sqrtd"], LT)
                        dve.wait_ge(S["ixd"], LT)
                        dve.wait_ge(S["geld"], LT)
                        link(nc.vector.tensor_scalar(inv, rt[:, t, :], 1.0, None, ALU.add))
                        link(nc.vector.reciprocal(inv, inv))
                        nc.vector.tensor_scalar(decay, inv, 2.0, -1.0, ALU.mult, ALU.add)
                        link(nc.vector.scalar_tensor_tensor(out=inv, in0=inv, scalar=2.0, in1=root[:, t, :], op0=ALU.mult, op1=ALU.mult))
                        link(nc.vector.tensor_tensor(u, u, inv, ALU.mult))
                        link(nc.vector.tensor_tensor_scan(rt[:, t, :], decay, u, 0.0, ALU.mult, ALU.add))
                        nc.vector.tensor_tensor(z_gate[:, t, :], z_gate[:, t, :], rt[:, t, :], ALU.mult).then_inc(S["lrud"], 1)

                    def divide(s):
                        dve.wait_ge(S["ex"], s + 1)
                        link(nc.vector.reciprocal(pinv[:, s:s + 1], psum_[:, s:s + 1]))
                        w = (s % TT + 1) * P
                        nc.vector.tensor_scalar(prob[:, s % 2, 0:w], prob[:, s % 2, 0:w], pinv[:, s:s + 1], None, ALU.mult).then_inc(S["pn"], 1)

                    def head_out(h):
                        dve.wait_ge(S["pv"], h + 1)
                        nc.vector.tensor_copy(q[:, h, :], bank[6][:, :]).then_inc(S["mla"], 1)

                    STEPS = HEADS * TT
                    for s in range(STEPS):
                        w = (s % TT + 1) * P
                        dve.wait_ge(S["sc"], s + 1)
                        nc.vector.tensor_reduce(nmax[:, s:s + 1], bank[4 + s % 2][:, 0:w], AX.X, ALU.max, negate=True).then_inc(S["nm"], 1)
                        if s:
                            divide(s - 1)
                        if s >= TT and s % TT == 0:
                            recur(s // TT - 1)
                        if s >= TT and s % TT == 2:
                            head_out(s // TT - 1)
                    divide(STEPS - 1)
                    recur(LT - 1)
                    head_out(HEADS - 1)
                    normalise(3, [(t, z_gate[:, t, :], OG + t) for t in range(LT)])
                    normalise(4, [(LT + h, q[:, h, :], OG + LT + h) for h in range(HEADS)])
                    for n in range(C_OUT + 4, N_CHUNK):
                        split(n)

                    def moments(k, i):
                        nc.vector.bn_stats(stats[i][:, 0:6], x[:, i, 0:HALF])
                        link(nc.vector.bn_stats(stats[i][:, 6:12], x[:, i, HALF:D]))
                        nc.vector.bn_aggr(mv[i], stats[i]).then_inc(S["vd"], 1)

                    def invert(k, i):
                        dve.wait_ge(S["stdd"], TT * k + i + 1)
                        link(nc.vector.reciprocal(rstd_t[:, i:i + 1], std[:, i:i + 1]))
                        nc.vector.scalar_tensor_tensor(out=nmr[:, i:i + 1], in0=mv[i][:, 0:1], scalar=-1.0, in1=rstd_t[:, i:i + 1], op0=ALU.mult, op1=ALU.mult).then_inc(S["lnx"], 1)

                    def gain(k, i):
                        dve.wait_ge(S["lng"], TT * k + i + 1)
                        nc.vector.tensor_tensor(x[:, i, :], x[:, i, :], lnbc[:, 0, :], ALU.mult).then_inc(S["lnm"], 1)

                    dve.wait_ge(S["opd"], 8)
                    for i in range(TT + 1):
                        if i < TT:
                            for half in range(2):
                                s = slice(half * HALF, (half + 1) * HALF)
                                m = nc.vector.scalar_tensor_tensor(out=x[:, i, s], in0=x[:, i, s], scalar=ALPHA, in1=bank[4 * half + i][:, :], op0=ALU.mult, op1=ALU.add)
                                if half:
                                    link(m)
                            moments(0, i)
                            invert(0, i)
                        if i:
                            if i == 1:
                                dve.wait_ge(S["ln1_in"], 16)
                            gain(0, i - 1)

                    def rows(ap, n):
                        return ap.rearrange("p (i n) -> p i n", n=n)

                    def wide(ap, n):
                        return ap.unsqueeze(2).to_broadcast([P, ap.shape[1], n])

                    tt = nc.vector.tensor_tensor
                    dve.wait_ge(S["sgd"], TT)
                    link(tt(sel, s_e, rb[:, :], ALU.add))
                    quad = rows(sel, 4)
                    tt(g_a, quad[:, :, 0], quad[:, :, 1], ALU.max)
                    tt(g_b, quad[:, :, 0], quad[:, :, 1], ALU.min)
                    tt(g_c, quad[:, :, 2], quad[:, :, 3], ALU.max)
                    link(tt(g_d, quad[:, :, 2], quad[:, :, 3], ALU.min))
                    tt(g_e, g_a, g_c, ALU.max)
                    tt(g_f, g_a, g_c, ALU.min)
                    link(tt(g_b, g_b, g_d, ALU.max))
                    link(tt(g_f, g_f, g_b, ALU.max))
                    link(tt(g_e, g_e, g_f, ALU.add))

                    def first_best(values_, n, weights, out_):
                        link(nc.vector.tensor_reduce(t_a, rows(values_, n), AX.X, ALU.max))
                        link(tt(rows(out_, n), rows(values_, n), wide(t_a, n), ALU.is_equal))
                        link(tt(out_, out_, weights, ALU.mult))
                        link(nc.vector.tensor_reduce(t_a, rows(out_, n), AX.X, ALU.max))
                        link(tt(rows(out_, n), rows(out_, n), wide(t_a, n), ALU.is_equal))

                    first_best(g_e, N_GRP, cst[:, GW:GW + TT * N_GRP], g_a)
                    link(nc.vector.tensor_scalar(g_b, g_a, BIG, -BIG, ALU.mult, ALU.add))
                    link(tt(rows(masked, 4), quad, wide(g_a, 4), ALU.mult))
                    link(tt(rows(masked, 4), rows(masked, 4), wide(g_b, 4), ALU.add))
                    ew = cst[:, EW:EW + TT * N_EXP]
                    first_best(masked, N_EXP, ew, oh1)
                    link(nc.vector.scalar_tensor_tensor(out=masked, in0=oh1, scalar=-BIG, in1=masked, op0=ALU.mult, op1=ALU.add))
                    first_best(masked, N_EXP, ew, oh2)
                    tt(use, oh1, oh2, ALU.add).then_inc(S["used_d"], 1)
                    link(tt(tmp, s_e, oh1, ALU.mult))
                    link(nc.vector.tensor_reduce(w1, rows(tmp, N_EXP), AX.X, ALU.add))
                    link(tt(tmp, s_e, oh2, ALU.mult))
                    link(nc.vector.tensor_reduce(w2, rows(tmp, N_EXP), AX.X, ALU.add))
                    link(tt(wr, w1, w2, ALU.add))
                    link(nc.vector.reciprocal(wr, wr))
                    tt(gate[:, 0:TT], w1, wr, ALU.mult)
                    link(tt(gate[:, TT:2 * TT], w2, wr, ALU.mult))
                    dve.wait_ge(S["pfx"], 1)
                    link(nc.vector.tensor_copy(cnt, bank[7][:, 0:N_EXP]))
                    link(nc.vector.tensor_scalar(nb, cnt, float(P), 1.0, ALU.is_gt, ALU.add))
                    for k in range(2, TT):
                        link(nc.vector.scalar_tensor_tensor(out=nb, in0=cnt, scalar=float(k * P), in1=nb, op0=ALU.is_gt, op1=ALU.add))
                    link(nc.vector.tensor_copy(nblk, nb))
                    link(nc.vector.tensor_tensor_scan(cum, onecol, nb, 0.0, ALU.mult, ALU.add))
                    link(tt(cum, cum, nb, ALU.subtract))
                    link(nc.vector.tensor_scalar(base16, cum, float(P), None, ALU.mult))
                    link(tt(rows(dst, N_EXP), rows(bank[4][:, 0:TT * N_EXP], N_EXP), base16.unsqueeze(1).to_broadcast([P, TT, N_EXP]), ALU.add))
                    for k, oh in enumerate((oh1, oh2)):
                        link(tt(tmp, dst, oh, ALU.mult))
                        link(nc.vector.tensor_reduce(dstk[:, k * TT:(k + 1) * TT], rows(tmp, N_EXP), AX.X, ALU.add))
                    nc.vector.tensor_copy(idx, dstk).then_inc(S["nbd"], 1)

                    g, gp, lap, used, lap16 = (dve.alloc_register(n) for n in ("d_g", "d_gp", "d_lap", "d_used", "d_lap16"))
                    dve.reg_mov(g, 1)
                    dve.reg_mov(gp, 2)
                    dve.reg_mov(lap, 1)
                    dve.reg_mov(lap16, 16)
                    dve.reg_mov(used, 1)

                    def upper_w(j):
                        dve.wait_ge(w_used[j], used)
                        dve.wait_ge(pair_in[j // 2], lap16)
                        nc.vector.tensor_copy(hi(j), raw(j)).then_inc(w_hi[j], 1)

                    def lower_w(j):
                        dve.wait_ge(w_hi[j], lap)
                        nc.vector.tensor_tensor(lo(j), raw(j), f(hi(j)), ALU.subtract).then_inc(w_lo[j], 1)

                    def lower_x(count):
                        dve.wait_ge(S["xbh"], count)
                        nc.vector.tensor_tensor(xb_lo[:, 0:4, :], bank[2][:, :].rearrange("p (k c) -> p k c", c=P), f(xb_hi[:, 0:4, :]), ALU.subtract)
                        dve.wait_ge(S["xbh2"], count)
                        nc.vector.tensor_tensor(xb_lo[:, 4:8, :], bank[3][:, :].rearrange("p (k c) -> p k c", c=P), f(xb_hi[:, 4:8, :]), ALU.subtract).then_inc(S["xbl"], 1)

                    def split_w(js):
                        for j in js:
                            if j not in ACT_HI:
                                upper_w(j)
                            if j not in POOL_LO:
                                lower_w(j)

                    dve.wait_ge(S["lg"], TT)
                    split_w(range(0, 8))
                    lower_x(1)
                    split_w(range(8, RING))
                    dve.reg_add(lap, lap, 1)
                    dve.reg_add(lap16, lap16, 16)

                    def one_block(split_next):
                        if split_next:
                            split_w(range(0, 4))
                        dve.wait_ge(w_used[7], gp)
                        dve.wait_ge(S["sgs"], g)
                        nc.vector.tensor_tensor(hb[:, :], bank[1][:, :], sg[:, :], ALU.mult).then_inc(S["hbd"], 1)
                        if split_next:
                            split_w(range(4, 5))
                        dve.wait_ge(S["hth"], g)
                        nc.vector.tensor_tensor(ht_lo[:, :, :], bank[4][:, :].rearrange("p (k c) -> p k c", c=P), f(ht_hi[:, :, :]), ALU.subtract).then_inc(S["htl"], 1)
                        lower_x(gp)
                        if split_next:
                            split_w(range(5, RING))
                        dve.reg_add(g, g, 1)
                        dve.reg_add(gp, gp, 1)

                    def expert(e, split_next):
                        blocks = dve.value_load(nblk[0:1, bass.ds(e, 1)] if split_next else nblk[0:1, N_EXP - 1:N_EXP], min_val=1, max_val=TT)
                        with dve.If(blocks > 1):
                            with dve.Fori(1, blocks):
                                one_block(False)
                                dve.reg_add(used, used, 1)
                        dve.reg_add(used, used, 1)
                        one_block(split_next)

                    dve.wait_ge(S["nbd"], 1)
                    with dve.Fori(0, N_EXP - 1) as e:
                        expert(e, True)
                        dve.reg_add(lap, lap, 1)
                        dve.reg_add(lap16, lap16, 16)
                    expert(None, False)

                    for i in range(TT + 1):
                        if i < TT:
                            dve.wait_ge(gath[i], gath_goal)
                            link(nc.vector.tensor_scalar(yg[:, 2 * i, :], yg[:, 2 * i, :], gate[:, i:i + 1], None, ALU.mult))
                            link(nc.vector.scalar_tensor_tensor(out=yg[:, 2 * i, :], in0=yg[:, 2 * i + 1, :], scalar=gate[:, TT + i:TT + i + 1], in1=yg[:, 2 * i, :], op0=ALU.mult, op1=ALU.add))
                            link(nc.vector.scalar_tensor_tensor(out=x[:, i, :], in0=x[:, i, :], scalar=ALPHA, in1=yg[:, 2 * i, :], op0=ALU.mult, op1=ALU.add))
                            moments(1, i)
                            invert(1, i)
                        if i:
                            if i == 1:
                                dve.wait_ge(S["ln2_in"], 16)
                            gain(1, i - 1)
                    dve.reg_add(gath_goal, gath_goal, 32)

                @block.gpsimd
                def _(pool):
                    for j in range(RING):
                        pool.sem_inc(w_used[j], 1)
                        pool.sem_inc(w_lo[j], 1)
                    pool.sem_inc(S["yevd"], 1)
                    pool.sem_inc(S["yst"], 16)

                    nc.gpsimd.memset(z_u[:, :, 0:3], 0.0).then_inc(S["pad"], 1)

                    kappa, added = 0, 0
                    for grp, n in enumerate(SQ_GROUPS):
                        for k in range(n):
                            kappa += 1
                            if k == 0:
                                continue
                            pool.wait_ge(S["sqd"], kappa)
                            if k == 1 and grp >= 2:
                                pool.wait_ge(S[("sums_q", "sums_kv")[grp - 2]], 1)
                            if k >= 2:
                                pool.wait_ge(S["sqa"], added)
                            m0 = sq[:, 0, :] if k == 1 else acc[:, grp % 2, :]
                            nc.gpsimd.tensor_tensor(acc[:, grp % 2, :], m0, sq[:, 1, :] if k == 1 else sq[:, (kappa - 1) % 2, :], ALU.add).then_inc(S["sqa"], 1)
                            added += 1

                    def shift(k):
                        pool.wait_ge(S["ln1_in"] if k == 0 else S["ln2_in"], 16)
                        for i in range(TT):
                            pool.wait_ge(S["lnm"], TT * k + i + 1)
                            nc.gpsimd.tensor_tensor(x[:, i, :], x[:, i, :], lnbc[:, 1, :], ALU.add).then_inc(S["lnb"], 1)

                    shift(0)
                    pool.wait_ge(S["nbd"], 1)
                    pool.wait_ge(filled, 16 * (MAX_BLOCKS + 2))
                    pool.wait_ge(S["lnb"], TT)
                    for k in range(2):
                        for i in range(TT):
                            c = k * TT + i
                            pool.indirect_dma_start(out=xrows, out_offset=bass.IndirectOffsetOnAxis(ap=idx[:, c:c + 1], axis=0), in_=x[:, i, :], in_offset=None).then_inc(scat, 16)

                    lap = pool.alloc_register("p_lap")
                    pool.reg_mov(lap, 1)
                    with pool.Fori(0, N_EXP) as e:
                        for j in POOL_LO:
                            pool.wait_ge(w_hi[j], lap)
                            nc.gpsimd.tensor_tensor(lo(j), raw(j), f(hi(j)), ALU.subtract).then_inc(w_lo[j], 1)
                        pool.reg_add(lap, lap, 1)

                    pool.wait_ge(S["allst"], 1)
                    for i in range(TT):
                        for k in range(2):
                            c = k * TT + i
                            pool.indirect_dma_start(out=yg[:, 2 * i + k, :], out_offset=None, in_=xrows, in_offset=bass.IndirectOffsetOnAxis(ap=idx[:, c:c + 1], axis=0)).then_inc(gath[i], 16)
                    shift(1)

            with nc.Block() as block:
                @block.gpsimd
                def _(pool):
                    for s in every:
                        pool.sem_clear(s)

        with nc.Block() as block:
            @block.sync
            def _(sp):
                sp.dma_start(out[0].rearrange("(i p) d -> p i d", p=P), x[:, :, :]).then_inc(init, 16)
                sp.wait_ge(init, 80)


ARRAYS = ("x", "cst", "rw", "rb", "par", "gw", "ln", "wm", "we")


def kernel(x, w_in, conv_w, conv_b, w_rgate, b_rgate, w_igate, b_igate, lru_lambda, q_norm_g, w_q_up, kv_norm_g, w_kv_up,
           out_norm_g, w_out, ln1_g, ln1_b, router_w, router_bias, w_exp_gate, w_exp_up, w_exp_down, ln2_g, ln2_b):
    import numpy as np
    import concourse.bacc as bacc
    from concourse.bass_utils import run_bass_kernel_spmd

    pos = np.arange(SEQ, dtype=np.float32)
    inv = (np.float32(10000.0) ** (-np.arange(ROPE // 2, dtype=np.float32) / np.float32(ROPE // 2))).astype(np.float32)
    ang = pos[None, :] * inv[:, None]
    cos, sin = np.cos(ang), np.sin(ang)
    r = np.arange(P)
    pieces = [np.eye(P), np.ones((P, P)), r[:, None] < r[None, :],
              r[:, None] % ROPE == r[None, :] % ROPE, np.concatenate([cos, cos, -sin, sin]), np.where(r[None, :] <= r[:, None], 0.0, -BIG),
              np.tile(np.arange(N_EXP, 0, -1), (P, TT)), np.tile(np.arange(N_GRP, 0, -1), (P, TT))]
    cst = np.concatenate([np.asarray(p, np.float32) for p in pieces], axis=1)

    def tiles(w):
        w = np.asarray(w)
        return np.moveaxis(w.reshape(w.shape[0], w.shape[1] // P, P, *w.shape[2:]), 2, 1)

    def columns(v):
        v = np.asarray(v).reshape(DEPTH, -1)
        return np.moveaxis(v.reshape(DEPTH, -1, P), 2, 1)

    par = np.concatenate([columns(np.asarray(conv_w)), columns(conv_b), columns(b_rgate), columns(b_igate), columns(lru_lambda),
                          columns(q_norm_g), columns(kv_norm_g), columns(out_norm_g)], axis=2)
    gw = np.zeros((DEPTH, P, 2 * LT, P), np.float32)
    for s, w in enumerate((w_rgate, w_igate)):
        w = np.asarray(w).reshape(DEPTH, LT, 2, 64, 64)
        for b in range(2):
            gw[:, 64 * b:64 * b + 64, s * LT:(s + 1) * LT, 64 * b:64 * b + 64] = np.moveaxis(w[:, :, b], 2, 1)
    gw = gw.reshape(DEPTH, P, -1)
    turned = np.r_[0:32, 32:64, 32:64, 0:32]
    wi = np.asarray(w_in)
    order = [2 * LRU + P * t + r for t in range(QT + KT)] + [2 * LRU + Q_LORA + KV_LORA + turned] + [P * t + r for t in range(2 * LT)]
    wm = np.zeros((DEPTH, N_CHUNK, P, CH), np.float32)
    for n, c in enumerate(order):
        wm[:, n] = tiles(wi[:, :, c]).reshape(DEPTH, P, CH)
    kv = tiles(w_kv_up)
    wm[:, C_K] = kv[..., 0:P].reshape(DEPTH, P, CH)
    wm[:, C_V] = kv[..., P:].reshape(DEPTH, P, CH)
    qu = tiles(w_q_up)
    for h in range(HEADS):
        wm[:, C_QN + h, :, 0:Q_LORA] = qu[:, :, :, h, 0:P].reshape(DEPTH, P, -1)
        wm[:, C_QR + h, :, 0:Q_LORA] = qu[:, :, :, h, P + turned].reshape(DEPTH, P, -1)
    wo = tiles(w_out)
    for half in range(2):
        for c in range(4):
            wm[:, C_OUT + 4 * half + c] = wo[:, :, 2 * c:2 * c + 2, half * HALF:(half + 1) * HALF].reshape(DEPTH, P, CH)
    we = np.empty((DEPTH, N_EXP, PAIRS, P, 2 * CH), np.float32)
    for s, w in enumerate((w_exp_gate, w_exp_up)):
        w = np.asarray(w).reshape(DEPTH, N_EXP, 2, 4, P, F_EXP)
        we[:, :, 2 * s:2 * s + 2] = np.moveaxis(w, 4, 3).reshape(DEPTH, N_EXP, 2, P, 2 * CH)
    w = np.asarray(w_exp_down).reshape(DEPTH, N_EXP, 2, 2, P, D)
    we[:, :, 4:6] = np.moveaxis(w, 4, 3).reshape(DEPTH, N_EXP, 2, P, 2 * CH)
    ln = np.stack([np.stack([np.asarray(ln1_g), np.asarray(ln1_b)], 1), np.stack([np.asarray(ln2_g), np.asarray(ln2_b)], 1)], 1)
    rw = np.moveaxis(np.asarray(router_w).reshape(DT, P, N_EXP), 1, 0).reshape(P, -1)
    rb = np.ascontiguousarray(np.broadcast_to(np.asarray(router_bias), (P, TT, N_EXP)).reshape(P, -1))

    nc = bacc.Bacc("TRN2", target_bir_lowering=False, num_devices=1)
    host = dict(x=np.asarray(x), cst=cst, rw=rw, rb=rb, par=par, gw=gw, ln=ln, wm=wm, we=we)
    arrays, args = {}, {}
    for name in ARRAYS:
        arrays[name + "_in"] = np.ascontiguousarray(host[name])
        args[name] = nc.dram_tensor(name + "_in", arrays[name + "_in"].shape, F32, kind="ExternalInput").ap()
    out = nc.dram_tensor("out_dram", (1, SEQ, D), F32, kind="ExternalOutput").ap()
    build(nc, args, out)
    return run_bass_kernel_spmd(nc, [arrays], core_ids=[0]).results[0]["out_dram"]
```

```python
from contextlib import ExitStack

import concourse.bass as bass
from concourse import mybir

F32 = mybir.dt.float32
F32R = mybir.dt.float32r
I32 = mybir.dt.int32
ALU = mybir.AluOpType
ACT = mybir.ActivationFunctionType
AX = mybir.AxisListType

P = 128
D = 1024
SEQ = 512
DEPTH = 2
LRU = 512
HEADS = 4
ROPE = 64
QK_HEAD = 192
Q_LORA = 768
KV_LORA = 256
N_EXP = 16
N_GRP = 4
F_EXP = 512
EPS = 1e-6
ALPHA = float((2 * DEPTH) ** 0.25)
BIG = 1e30
KB = 1024

TT = SEQ // P
DT = D // P
LT = LRU // P
QT = Q_LORA // P
KT = KV_LORA // P
FT = F_EXP // P
HALF = D // 2
CH = 1024
RA = 4
RING = 12
PAIRS = RING // 2
MAX_BLOCKS = N_EXP - 1 + SEQ * 2 // P

N_IN = QT + KT + 1 + 2 * LT
C_K = N_IN
C_V = C_K + 1
C_Q = C_V + 1
C_OUT = C_Q + 2 * HEADS
N_CHUNK = C_OUT + 8
M_K = N_IN
M_V = M_K + HEADS
M_Q = M_V + TT


def chunk_width(n):
    return Q_LORA if C_Q <= n < C_OUT else CH


SQ_GROUPS = (QT, KT, LT, HEADS)


def sq_taken(kappa):
    added = 0
    for n in SQ_GROUPS:
        if kappa < n:
            return added + max(kappa, 1)
        kappa -= n
        added += n - 1


ACT_HI = (0, 1, 2, 4, 5, 6, 8, 9, 10)
POOL_LO = (1, 3, 4, 6, 7)

IDENT, ONES, TRI, DUP, ROT = 0, 128, 256, 384, 512
CMASK = ROT + SEQ
EW = CMASK + P
GW = EW + TT * N_EXP
N_CST = GW + TT * N_GRP
CONV_W, CONV_B, B_R, B_I, LAM = 0, 4 * LT, 5 * LT, 6 * LT, 7 * LT
QG = 8 * LT
OG = QG + QT + KT
N_PAR = OG + DT


def build(nc, a, out):
    with ExitStack() as ctx:
        base = (nc.sbuf_base + 63) // 64 * 64

        def at(kb, name, shape, dt=F32):
            return nc.alloc_sbuf_tensor_at(name, shape, dt, offset=base + int(kb * KB))

        def sem(name):
            return ctx.enter_context(nc.semaphore(name))

        x = at(0, "x", [P, TT, D])
        cst = at(16, "cst", [P, N_CST])
        rw = at(21, "rw", [P, DT * N_EXP])
        rb = at(21.5, "rb", [P, TT * N_EXP])
        par = at(21.75, "par", [P, N_PAR])
        small = at(22, "small", [P, 1024])
        lnbc = at(26, "lnbc", [P, 2, D])
        gatew = at(26, "gatew", [P, 2 * LT, P])
        raw_a = at(34, "raw_a", [P, RA, CH])
        hi_a = at(50, "hi_a", [P, RA, CH], F32R)
        lo_a = at(66, "lo_a", [P, RA, CH], F32R)
        raw_b = at(82, "raw_b", [P, RING - RA, CH])
        hi_b = at(114, "hi_b", [P, RING - RA, CH], F32R)
        lo_b = at(146, "lo_b", [P, RING - RA, CH], F32R)
        n_hi = at(82, "n_hi", [P, DT, SEQ], F32R)
        n_lo = at(98, "n_lo", [P, DT, SEQ], F32R)
        xt_hi = at(114, "xt_hi", [P, DT, SEQ], F32R)
        xt_lo = at(130, "xt_lo", [P, DT, SEQ], F32R)
        q = at(114, "q", [P, 2 * HEADS, SEQ])
        x1t = at(114, "x1t", [P, DT, SEQ])
        kn = at(130, "kn", [P, HEADS, SEQ])
        v = at(138, "v", [P, TT, HEADS * P])
        z_gate = at(146, "z_gate", [P, LT, SEQ])
        z_lat = at(154, "z_lat", [P, QT + KT, SEQ])
        pt = at(154, "pt", [P, 2, TT, SEQ])
        root = at(26, "root", [P, LT, SEQ])
        z_u = at(170, "z_u", [P, LT, 3 + SEQ])
        prob = at(179, "prob", [P, 2, SEQ])
        krot = at(179, "krot", [P, SEQ])
        sq = at(183, "sq", [P, 2, SEQ])
        acc = at(187, "acc", [P, 2, SEQ])
        rstd = at(191, "rstd", [P, SEQ])
        kr = at(193, "kr", [P, SEQ])
        xc = at(195, "xc", [P, 2, SEQ])
        rt = at(199, "rt", [P, LT, SEQ])
        xg = at(179, "xg", [P, D])
        xb_hi = at(183, "xb_hi", [P, DT, P], F32R)
        xb_lo = at(187, "xb_lo", [P, DT, P], F32R)
        ht_hi = at(191, "ht_hi", [P, FT, P], F32R)
        ht_lo = at(193, "ht_lo", [P, FT, P], F32R)
        sg = at(195, "sg", [P, F_EXP])
        hb = at(197, "hb", [P, F_EXP])
        yb = at(199, "yb", [P, D])
        yg = at(82, "yg", [P, 2 * TT, D])

        def hi(j):
            return hi_a[:, j, :] if j < RA else hi_b[:, j - RA, :]

        def lo(j):
            return lo_a[:, j, :] if j < RA else lo_b[:, j - RA, :]

        def raw(j):
            return raw_a[:, j, :] if j < RA else raw_b[:, j - RA, :]

        def f(ap):
            return ap.bitcast(F32)

        ident = cst[:, IDENT:IDENT + P]
        ones = cst[:, ONES:ONES + P]
        tri = cst[:, TRI:TRI + P]
        cmask = cst[:, CMASK:CMASK + P]
        dup = cst[:, DUP:DUP + P]
        rot = cst[:, ROT:ROT + SEQ]

        bank = [ctx.enter_context(nc.psum_tensor(f"bank{i}", [P, 512], F32)) for i in range(8)]

        col = [0]

        def cols(n):
            s = small[:, col[0]:col[0] + n]
            col[0] += n
            return s

        eps = cols(1)
        sp_a, sp_b, sp_c, sp_d, sp_e = (cols(LT) for _ in range(5))
        c4 = cols(LT)
        nmax, psum_, pinv = cols(16), cols(16), cols(16)
        stats = [cols(12) for _ in range(TT)]
        mv = [cols(2) for _ in range(TT)]
        std, rstd_t, nmr = cols(TT), cols(TT), cols(TT)
        s_e, sel, masked, pen, oh1, oh2, tmp, use, dst = (cols(TT * N_EXP) for _ in range(9))
        g_a, g_b, g_c, g_d, g_e, g_f = (cols(TT * N_GRP) for _ in range(6))
        t_a, w1, w2, wr = (cols(TT) for _ in range(4))
        gate = cols(2 * TT)
        cnt, nb, cum = (cols(N_EXP) for _ in range(3))
        tot, first, tmp2 = sel, pen, masked
        idx = cols(2 * TT).bitcast(I32)
        nblk = cols(N_EXP).bitcast(I32)
        onecol = cols(N_EXP)
        dstk = cols(2 * TT)
        assert col[0] <= 1024

        xbuf = nc.dram_tensor("xbuf", (MAX_BLOCKS + 2, P, D), F32).ap()
        xrows = xbuf.rearrange("b p d -> (b p) d")

        init, filled = sem("init"), sem("filled")
        scat = sem("scat")
        scat_goal, gath_goal = nc.scalar.alloc_register("scat_goal"), nc.vector.alloc_register("gath_goal")
        names = """par_in gates_in ln1_in ln2_in xt_t xt_h xt_l gemm ev_dve ev_act a_hi a_lo
            sqd sqa sums_q sums_kv rs_std nrm_h nrm_l kdup krd xcd gmm gact ixd tanhd geld sqrtd lrud
            sc nm ex pn ptr pte pv mla opd vd stdd lnx lng lnb lnp x1d x1e lg sgd used_d pfx nbd
            chain_d mixs_l mixs_m nz lnm c4d
            xg_in xbt hbt sgs hbd xbh xbh2 xbl htt hth htl yev1 yevd yst allst
            sp_abs sp_exp pad""".split()
        S = {n: sem(n) for n in names}
        raw_in = [sem(f"raw_in{i}") for i in range(RA)]
        pair_in = [sem(f"pair_in{i}") for i in range(PAIRS)]
        w_hi = [sem(f"w_hi{j}") for j in range(RING)]
        w_lo = [sem(f"w_lo{j}") for j in range(RING)]
        w_used = [sem(f"w_used{j}") for j in range(RING)]
        gath = [sem(f"gath{i}") for i in range(TT)]
        every = list(S.values()) + raw_in + pair_in + w_hi + w_lo + w_used

        def chunk_freed(n):
            if n < C_K:
                return S["gemm"], n + 1
            if n == C_K:
                return S["gemm"], M_V
            if n == C_V:
                return S["gemm"], M_Q
            if n < C_OUT:
                return S["gemm"], M_Q + (n - C_Q) + 1
            return S["opd"], n - C_OUT + 1

        def evac_done(m):
            if m < M_K:
                return S["ev_dve"], m + 1
            if m < M_Q:
                return S["ev_act"], m - M_K + 1
            if (m - M_Q) % 2 == 0:
                return S["ev_act"], M_Q - M_K + (m - M_Q) // 2 + 1
            return S["ev_dve"], M_K + (m - M_Q) // 2 + 1

        with nc.Block() as block:
            @block.sync
            def _(sp):
                sp.dma_start(x[:, :, :], a["x"][0].rearrange("(i p) d -> p i d", p=P)).then_inc(init, 16)
                sp.dma_start(cst[:, :], a["cst"][:, :]).then_inc(init, 16)
                sp.dma_start(rw[:, :], a["rw"][:, :]).then_inc(init, 16)
                sp.dma_start(rb[:, :], a["rb"][:, :]).then_inc(init, 16)
                sp.wait_ge(init, 64)

            @block.vector
            def _(dve):
                nc.vector.memset(eps, EPS)
                nc.vector.memset(onecol, 1.0)
                dve.reg_mov(gath_goal, 32)

            @block.scalar
            def _(act):
                act.reg_mov(scat_goal, 16 * 2 * TT)

        with nc.Fori(0, DEPTH) as ly:
            with nc.Block() as block:
                @block.sync
                def _(sp):
                    sp.dma_start(par[:, :], a["par"][bass.ds(ly, 1)].rearrange("l p n -> (l p) n")).then_inc(S["par_in"], 16)
                    sp.dma_start(gatew[:, :, :], a["gw"][bass.ds(ly, 1)].rearrange("l p (t n) -> (l p) t n", n=P)).then_inc(S["gates_in"], 16)
                    for n in range(N_CHUNK):
                        if n >= RA:
                            sp.wait_ge(S["a_lo"], n - RA + 1)
                        w = chunk_width(n)
                        sp.dma_start(raw(n % RA)[:, 0:w], a["wm"][bass.ds(ly, 1), n, :, 0:w].rearrange("l p n -> (l p) n")).then_inc(raw_in[n % RA], 16)
                        if RA <= n < RA + (MAX_BLOCKS + 3) // 2:
                            with sp.If(ly < 1):
                                for b in range(2 * (n - RA), min(2 * (n - RA) + 2, MAX_BLOCKS + 2)):
                                    sp.dma_start(xbuf[b], cst[:, 0:D]).then_inc(filled, 16)
                    sp.wait_ge(S["lrud"], LT)
                    sp.dma_start(lnbc[:, :, :], a["ln"][bass.ds(ly, 1), 0].rearrange("l c d -> (l c) d").partition_broadcast(P)).then_inc(S["ln1_in"], 16)

                    sp.wait_ge(S["a_lo"], N_CHUNK)
                    for t in range(RA // 2):
                        sp.dma_start(raw_a[:, 2 * t:2 * t + 2, :], a["we"][bass.ds(ly, 1), 0, t].rearrange("l p n -> (l p) n").rearrange("p (c n) -> p c n", c=2)).then_inc(pair_in[t], 16)
                    sp.wait_ge(S["opd"], 8)
                    for t in range(RA // 2, PAIRS):
                        sp.dma_start(raw_b[:, 2 * t - RA:2 * t - RA + 2, :], a["we"][bass.ds(ly, 1), 0, t].rearrange("l p n -> (l p) n").rearrange("p (c n) -> p c n", c=2)).then_inc(pair_in[t], 16)
                    def land(e, pairs):
                        for t in pairs:
                            dst = raw_a[:, 2 * t:2 * t + 2, :] if 2 * t < RA else raw_b[:, 2 * t - RA:2 * t - RA + 2, :]
                            sp.dma_start(dst, a["we"][bass.ds(ly, 1), bass.ds(e, 1), t].rearrange("l e p n -> (l e p) n").rearrange("p (c n) -> p c n", c=2)).then_inc(pair_in[t], 16)

                    one, two = sp.alloc_register("sp_one"), sp.alloc_register("sp_two")
                    sp.reg_mov(one, 1)
                    sp.reg_mov(two, 2)
                    for t in range(PAIRS - 2):
                        sp.wait_ge(w_lo[2 * t], 2)
                        sp.wait_ge(w_lo[2 * t + 1], 2)
                        land(1, [t])
                    with sp.Fori(1, N_EXP - 1) as e:
                        sp.reg_add(one, one, 1)
                        sp.reg_add(two, two, 1)
                        for t in range(PAIRS - 2):
                            sp.wait_ge(w_lo[2 * t], two)
                            sp.wait_ge(w_lo[2 * t + 1], two)
                            land(e + 1, [t])
                        for t in range(PAIRS - 2, PAIRS):
                            sp.wait_ge(w_lo[2 * t], one)
                            sp.wait_ge(w_lo[2 * t + 1], one)
                            land(e, [t])
                    for t in range(PAIRS - 2, PAIRS):
                        sp.wait_ge(w_lo[2 * t], N_EXP)
                        sp.wait_ge(w_lo[2 * t + 1], N_EXP)
                        land(N_EXP - 1, [t])
                    sp.wait_ge(S["lnb"], TT)
                    sp.dma_start(lnbc[:, :, :], a["ln"][bass.ds(ly, 1), 1].rearrange("l c d -> (l c) d").partition_broadcast(P)).then_inc(S["ln2_in"], 16)

                @block.tensor
                def _(pe):
                    def mm3(o, wh, wl, mh, ml, first, last):
                        nc.tensor.matmul(o, wh, mh, start=first, stop=False)
                        nc.tensor.matmul(o, wh, ml, start=False, stop=False)
                        return nc.tensor.matmul(o, wl, mh, start=False, stop=last)

                    for c in range(DT):
                        if c >= 2:
                            pe.wait_ge(S["xt_l"], c - 1)
                        for i in range(TT):
                            m = nc.tensor.transpose(bank[2 + c % 2][:, i * P:(i + 1) * P], x[:, i, c * P:(c + 1) * P], ident)
                        m.then_inc(S["xt_t"], 1)

                    for n in range(N_IN):
                        pe.wait_ge(S["a_lo"], n + 1)
                        if n == 0:
                            pe.wait_ge(S["xt_l"], DT)
                        if n >= 2:
                            pe.wait_ge(*evac_done(n - 2))
                        wh, wl = hi(n % RA), lo(n % RA)
                        for k in range(DT):
                            m = mm3(bank[n % 2][:, :], wh[:, k * P:(k + 1) * P], wl[:, k * P:(k + 1) * P], xt_hi[:, k, :], xt_lo[:, k, :], k == 0, k == DT - 1)
                        m.then_inc(S["gemm"], 1)
                        if n == QT + KT + 3:
                            pe.wait_ge(S["ev_dve"], QT + KT + 1)
                            nc.tensor.matmul(bank[7][:, :], dup, krot[:, :], start=True, stop=True).then_inc(S["kdup"], 1)
                            pe.wait_ge(S["sqa"], QT - 1)
                            nc.tensor.matmul(bank[6][:, :], ones, acc[:, 0, :], start=True, stop=True).then_inc(S["sums_q"], 1)
                            pe.wait_ge(S["sqa"], QT + KT - 2)
                            nc.tensor.matmul(bank[5][:, :], ones, acc[:, 1, :], start=True, stop=True).then_inc(S["sums_kv"], 1)

                    def up(m0, n, outs, kt, tile0, values=False):
                        pe.wait_ge(S["a_lo"], n + 1)
                        wh, wl = hi(n % RA), lo(n % RA)
                        for h in range(outs):
                            pe.wait_ge(*evac_done(m0 + h - 2))
                            for k in range(kt):
                                o = bank[(m0 + h) % 2][:, :]
                                if values:
                                    s = slice(h * P, (h + 1) * P)
                                    m = mm3(o, n_hi[:, tile0 + k, s], n_lo[:, tile0 + k, s], wh[:, k * SEQ:(k + 1) * SEQ], wl[:, k * SEQ:(k + 1) * SEQ], k == 0, k == kt - 1)
                                else:
                                    s = slice((k * outs + h) * P, (k * outs + h + 1) * P)
                                    m = mm3(o, wh[:, s], wl[:, s], n_hi[:, tile0 + k, :], n_lo[:, tile0 + k, :], k == 0, k == kt - 1)
                            m.then_inc(S["gemm"], 1)

                    def gates(t):
                        pe.wait_ge(S["xcd"], t + 1)
                        if t:
                            pe.wait_ge(S["gact"], 2 * t)
                        else:
                            pe.wait_ge(S["gates_in"], 16)
                            pe.wait_ge(S["rs_std"], 2)
                        nc.tensor.matmul(bank[4][:, :], gatew[:, t, :], xc[:, t % 2, :], start=True, stop=True).then_inc(S["gmm"], 1)
                        nc.tensor.matmul(bank[5][:, :], gatew[:, LT + t, :], xc[:, t % 2, :], start=True, stop=True).then_inc(S["gmm"], 1)

                    pe.wait_ge(S["nrm_l"], KT)
                    up(M_K, C_K, HEADS, KT, QT)
                    gates(0)
                    up(M_V, C_V, TT, KT, QT, values=True)
                    gates(1)
                    def queries(h, steps):
                        for t in steps:
                            part, k = t // QT, t % QT
                            m_, n = M_Q + 2 * h + part, C_Q + 2 * h + part
                            if k == 0:
                                pe.wait_ge(S["a_lo"], n + 1)
                                pe.wait_ge(*evac_done(m_ - 2))
                            s = slice(k * P, (k + 1) * P)
                            m = mm3(bank[m_ % 2][:, :], hi(n % RA)[:, s], lo(n % RA)[:, s], n_hi[:, k, :], n_lo[:, k, :], k == 0, k == QT - 1)
                            if k == QT - 1:
                                m.then_inc(S["gemm"], 1)

                    pe.wait_ge(S["nrm_l"], QT + KT)
                    queries(0, range(2 * QT))
                    gates(2)
                    gates(3)

                    def score(s):
                        h, i = s // TT, s % TT
                        w = (i + 1) * P
                        o = bank[4 + s % 2]
                        if s < 2:
                            pe.wait_ge(S["gact"], 2 * LT)
                        else:
                            pe.wait_ge(S["ex"], s - 1)
                        if i == 0:
                            pe.wait_ge(*evac_done(M_Q + 2 * h))
                            pe.wait_ge(*evac_done(M_Q + 2 * h + 1))
                        if s == 0:
                            pe.wait_ge(S["krd"], 1)
                        nc.tensor.matmul(o[:, 0:w], q[:, h, i * P:w], kn[:, h, 0:w], start=True, stop=False)
                        nc.tensor.matmul(o[:, 0:w], q[:, HEADS + h, i * P:w], kr[:, 0:w], start=False, stop=False)
                        nc.tensor.matmul(o[:, i * P:w], ident, cmask, start=False, stop=True).then_inc(S["sc"], 1)

                    def values(h):
                        pe.wait_ge(S["pte"], TT * (h + 1))
                        if h:
                            pe.wait_ge(S["mla"], h)
                        for j in range(TT):
                            m = nc.tensor.matmul(bank[6][:, j * P:SEQ], v[:, j, h * P:(h + 1) * P], pt[:, h % 2, j, j * P:SEQ], start=(j == 0), stop=(j == TT - 1))
                        m.then_inc(S["pv"], 1)

                    STEPS = HEADS * TT
                    score(0)
                    for s in range(STEPS):
                        if s + 1 < STEPS:
                            score(s + 1)
                        h, i = s // TT, s % TT
                        if i < 3 and h + 1 < HEADS:
                            queries(h + 1, range(4 * i, 4 * i + 4))
                        if i == 3 and h:
                            values(h - 1)
                        pe.wait_ge(S["pn"], s + 1)
                        if s >= 2:
                            pe.wait_ge(S["pte"], s - 1)
                        for j in range(s % TT + 1):
                            m = nc.tensor.transpose(bank[2 + s % 2][:, j * P:(j + 1) * P], prob[:, s % 2, j * P:(j + 1) * P], ident)
                        m.then_inc(S["ptr"], 1)
                    values(HEADS - 1)

                    pe.wait_ge(S["sqa"], QT + KT - 2 + LT - 1)
                    nc.tensor.matmul(bank[7][:, :], ones, acc[:, 0, :], start=True, stop=True).then_inc(S["mixs_l"], 1)
                    pe.wait_ge(S["sqa"], QT + KT - 2 + 2 * (LT - 1))
                    nc.tensor.matmul(bank[5][:, :], ones, acc[:, 1, :], start=True, stop=True).then_inc(S["mixs_m"], 1)

                    def project(half, c, i):
                        wh, wl = hi((C_OUT + c) % RA), lo((C_OUT + c) % RA)
                        for kk in range(2):
                            s = slice(i * P, (i + 1) * P)
                            m = mm3(bank[4 * half + i][:, :], n_hi[:, 2 * c + kk, s], n_lo[:, 2 * c + kk, s], wh[:, kk * HALF:(kk + 1) * HALF], wl[:, kk * HALF:(kk + 1) * HALF],
                                    c == 0 and kk == 0, c == 3 and kk == 1)
                        return m

                    for c in range(4):
                        pe.wait_ge(S["a_lo"], C_OUT + c + 1)
                        pe.wait_ge(S["nrm_l"], QT + KT + 2 * c + 2)
                        for i in range(TT):
                            m = project(0, c, i)
                        m.then_inc(S["opd"], 1)
                    for i in range(TT):
                        for c in range(4):
                            pe.wait_ge(S["a_lo"], C_OUT + 4 + c + 1)
                            m = project(1, c, i)
                        m.then_inc(S["opd"], 1)

                    for i in range(TT):
                        pe.wait_ge(S["lnb"], i + 1)
                        for c in range(DT):
                            m = nc.tensor.transpose(bank[i + c // 4 * 4][:, c % 4 * P:(c % 4 + 1) * P], x[:, i, c * P:(c + 1) * P], ident)
                        m.then_inc(S["x1d"], 1)
                        pe.wait_ge(S["x1e"], i + 1)
                        for k in range(DT):
                            m = nc.tensor.matmul(bank[i][:, 0:N_EXP], x1t[:, k, i * P:(i + 1) * P], rw[:, k * N_EXP:(k + 1) * N_EXP], start=(k == 0), stop=(k == DT - 1))
                        m.then_inc(S["lg"], 1)

                    pe.wait_ge(S["used_d"], 1)
                    nc.tensor.matmul(bank[4][:, 0:TT * N_EXP], tri, use, start=True, stop=True)
                    nc.tensor.matmul(bank[7][:, 0:TT * N_EXP], ones, use, start=True, stop=True).then_inc(S["pfx"], 1)

                    def turn_x(half, s):
                        for c in range(4 * half, 4 * half + 4):
                            m = nc.tensor.transpose(bank[2 + half][:, c % 4 * P:(c % 4 + 1) * P], xg[:, c * P:(c + 1) * P], ident)
                        m.then_inc(s, 1)

                    g, gm, g16, lap, lapd = (pe.alloc_register(n) for n in ("pe_g", "pe_gm", "pe_g16", "pe_lap", "pe_lapd"))
                    pe.reg_mov(g, 1)
                    pe.reg_mov(gm, 0)
                    pe.reg_mov(g16, 32)
                    pe.reg_mov(lap, 2)
                    pe.reg_mov(lapd, 2)

                    def down():
                        pe.wait_ge(S["yevd"], gm)
                        pe.wait_ge(S["htl"], gm)
                        for j in range(8, RING):
                            pe.wait_ge(w_lo[j], lapd)
                            for half in range(2):
                                m = mm3(bank[5 + half][:, :], ht_hi[:, j - 8, :], ht_lo[:, j - 8, :], hi(j)[:, half * HALF:(half + 1) * HALF], lo(j)[:, half * HALF:(half + 1) * HALF], j == 8, j == RING - 1)
                            m.then_inc(w_used[j], 1)

                    pe.wait_ge(S["nbd"], 1)
                    pe.wait_ge(S["xg_in"], 16)
                    turn_x(0, S["xbt"])
                    turn_x(1, S["hbt"])
                    with pe.Fori(0, N_EXP) as e:
                        blocks = pe.value_load(nblk[0:1, bass.ds(e, 1)], min_val=1, max_val=TT)
                        with pe.Fori(0, blocks):
                            pe.wait_ge(S["xbl"], g)
                            for side in range(2):
                                for j in range(4 * side, 4 * side + 4):
                                    pe.wait_ge(w_lo[j], lap)
                                    for kk in range(2):
                                        k = 2 * (j % 4) + kk
                                        m = mm3(bank[side][:, :], xb_hi[:, k, :], xb_lo[:, k, :], hi(j)[:, kk * F_EXP:(kk + 1) * F_EXP], lo(j)[:, kk * F_EXP:(kk + 1) * F_EXP], k == 0, k == DT - 1)
                                    m.then_inc(w_used[j], 1)
                            pe.wait_ge(S["xg_in"], g16)
                            turn_x(0, S["xbt"])
                            turn_x(1, S["hbt"])
                            with pe.If(pe.snap(gm, min_val=0, max_val=MAX_BLOCKS) > 0):
                                down()
                            pe.wait_ge(S["hbd"], g)
                            for c in range(FT):
                                m = nc.tensor.transpose(bank[4][:, c * P:(c + 1) * P], hb[:, c * P:(c + 1) * P], ident)
                            m.then_inc(S["htt"], 1)
                            pe.reg_add(g, g, 1)
                            pe.reg_add(gm, gm, 1)
                            pe.reg_add(g16, g16, 16)
                            pe.reg_add(lapd, lap, 0)
                        pe.reg_add(lap, lap, 1)
                    down()

                @block.scalar
                def _(act):
                    def split(n):
                        w = chunk_width(n)
                        if n >= RA:
                            act.wait_ge(*chunk_freed(n - RA))
                        act.wait_ge(raw_in[n % RA], 16 * (n // RA + 1))
                        nc.scalar.activation(hi(n % RA)[:, 0:w], raw(n % RA)[:, 0:w], ACT.Copy).then_inc(S["a_hi"], 1)

                    def upper(tile, src):
                        nrm[0] += 1
                        act.wait_ge(S["nz"], nrm[0])
                        nc.scalar.activation(n_hi[:, tile, :], src, ACT.Copy).then_inc(S["nrm_h"], 1)

                    def square(kappa, src):
                        if kappa >= 2:
                            act.wait_ge(S["sqa"], sq_taken(kappa - 2))
                        nc.scalar.activation(sq[:, kappa % 2, :], src, ACT.Square).then_inc(S["sqd"], 1)

                    def deviation(src, width):
                        nc.scalar.activation(rstd[:, :], src[:, :], ACT.Sqrt, bias=eps, scale=1.0 / width).then_inc(S["rs_std"], 1)

                    nrm = [0]
                    for c in range(DT):
                        act.wait_ge(S["xt_t"], c + 1)
                        nc.scalar.activation(xt_hi[:, c, :], bank[2 + c % 2][:, :], ACT.Copy).then_inc(S["xt_h"], 1)
                    act.wait_ge(S["sp_abs"], 1)
                    nc.scalar.activation(sp_e, sp_a, ACT.Exp, scale=-1.0).then_inc(S["sp_exp"], 1)
                    for n in range(RA):
                        split(n)
                    for n in range(N_IN):
                        split(n + RA)
                        if n < QT + KT:
                            act.wait_ge(S["ev_dve"], n + 1)
                            square(n, z_lat[:, n, :])
                        if n == N_IN - 5:
                            act.wait_ge(S["kdup"], 1)
                            nc.scalar.activation(kr[:, :], bank[7][:, :], ACT.Copy).then_inc(S["krd"], 1)
                            act.wait_ge(S["sums_kv"], 1)
                            deviation(bank[5], KV_LORA)
                            for k in range(KT):
                                upper(QT + k, z_lat[:, QT + k, :])
                            act.wait_ge(S["sums_q"], 1)
                            deviation(bank[6], Q_LORA)
                        if N_IN - 5 < n < N_IN - 1:
                            for k in range(2):
                                tile = 2 * (n - N_IN + 4) + k
                                upper(tile, z_lat[:, tile, :])

                    def leave(m, dst, scale=1.0):
                        act.wait_ge(S["gemm"], m + 1)
                        nc.scalar.activation(dst, bank[m % 2][:, :], ACT.Copy, scale=scale).then_inc(S["ev_act"], 1)

                    def gates(t):
                        act.wait_ge(S["gmm"], 2 * t + 1)
                        nc.scalar.activation(rt[:, t, :], bank[4][:, :], ACT.Sigmoid, bias=par[:, B_R + t:B_R + t + 1]).then_inc(S["gact"], 1)
                        act.wait_ge(S["gmm"], 2 * t + 2)
                        nc.scalar.activation(z_u[:, t, 3:3 + SEQ], bank[5][:, :], ACT.Sigmoid, bias=par[:, B_I + t:B_I + t + 1]).then_inc(S["gact"], 1)
                        act.wait_ge(S["c4d"], 1)
                        act.wait_ge(S["gact"], 2 * t + 2)
                        nc.scalar.activation(rt[:, t, :], rt[:, t, :], ACT.Tanh, scale=c4[:, t:t + 1]).then_inc(S["tanhd"], 1)

                    for h in range(HEADS):
                        leave(M_K + h, kn[:, h, :])
                    split(C_K + RA)
                    gates(0)
                    for i in range(TT):
                        leave(M_V + i, v[:, i, :])
                    split(C_V + RA)
                    gates(1)
                    def queries_out(h):
                        leave(M_Q + 2 * h, q[:, h, :], QK_HEAD ** -0.5)

                    queries_out(0)
                    split(C_Q + RA)
                    split(C_Q + 1 + RA)
                    gates(2)
                    gates(3)
                    act.wait_ge(S["tanhd"], LT)
                    for t in range(LT):
                        nc.scalar.activation(root[:, t, :], rt[:, t, :], ACT.Sqrt).then_inc(S["sqrtd"], 1)
                    for t in range(LT):
                        nc.scalar.activation(z_gate[:, t, :], z_gate[:, t, :], ACT.Gelu_apprx_tanh).then_inc(S["geld"], 1)

                    def leave_p(s):
                        h, i = s // TT, s % TT
                        act.wait_ge(S["ptr"], s + 1)
                        if h >= 2 and i == 0:
                            act.wait_ge(S["pv"], h - 1)
                        nc.scalar.activation(pt[:, h % 2, 0:i + 1, i * P:(i + 1) * P], bank[2 + s % 2][:, 0:(i + 1) * P].rearrange("p (j c) -> p j c", c=P), ACT.Copy).then_inc(S["pte"], 1)

                    STEPS = HEADS * TT
                    for s in range(STEPS):
                        w = (s % TT + 1) * P
                        act.wait_ge(S["nm"], s + 1)
                        if s >= 2:
                            act.wait_ge(S["ptr"], s - 1)
                        nc.scalar.activation(prob[:, s % 2, 0:w], bank[4 + s % 2][:, 0:w], ACT.Exp, bias=nmax[:, s:s + 1], accum_out=psum_[:, s:s + 1]).then_inc(S["ex"], 1)
                        if s:
                            leave_p(s - 1)
                        h, i = s // TT, s % TT
                        if h + 1 < HEADS and i == 2:
                            queries_out(h + 1)
                            split(C_Q + 2 * h + 2 + RA)
                        if h + 1 < HEADS and i == 3:
                            split(C_Q + 2 * h + 3 + RA)
                        if i == 3 and h:
                            t = h - 1
                            act.wait_ge(S["lrud"], t + 1)
                            square(QT + KT + t, z_gate[:, t, :])
                    leave_p(STEPS - 1)
                    act.wait_ge(S["lrud"], LT)
                    square(QT + KT + LT - 1, z_gate[:, LT - 1, :])
                    for h in range(HEADS):
                        act.wait_ge(S["mla"], h + 1)
                        square(QT + KT + LT + h, q[:, h, :])
                    act.wait_ge(S["mixs_l"], 1)
                    deviation(bank[7], LRU)
                    for t in range(LT):
                        upper(t, z_gate[:, t, :])
                    act.wait_ge(S["mixs_m"], 1)
                    deviation(bank[5], HEADS * P)
                    for h in range(HEADS):
                        upper(LT + h, q[:, h, :])
                    for n in range(C_OUT + 4, N_CHUNK):
                        split(n)

                    def norm(k):
                        for i in range(TT):
                            act.wait_ge(S["vd"], TT * k + i + 1)
                            nc.scalar.activation(std[:, i:i + 1], mv[i][:, 1:2], ACT.Sqrt, bias=eps).then_inc(S["stdd"], 1)
                            act.wait_ge(S["lnx"], TT * k + i + 1)
                            nc.scalar.activation(x[:, i, :], x[:, i, :], ACT.Identity, bias=nmr[:, i:i + 1], scale=rstd_t[:, i:i + 1]).then_inc(S["lng"], 1)

                    norm(0)
                    for i in range(TT):
                        act.wait_ge(S["x1d"], i + 1)
                        s = slice(i * P, (i + 1) * P)
                        nc.scalar.activation(x1t[:, 0:4, s], bank[i][:, :].rearrange("p (k c) -> p k c", c=P), ACT.Copy)
                        nc.scalar.activation(x1t[:, 4:8, s], bank[4 + i][:, :].rearrange("p (k c) -> p k c", c=P), ACT.Copy).then_inc(S["x1e"], 1)
                        act.wait_ge(S["lg"], i + 1)
                        nc.scalar.activation(s_e[:, i * N_EXP:(i + 1) * N_EXP], bank[i][:, 0:N_EXP], ACT.Sigmoid).then_inc(S["sgd"], 1)

                    g, gp, gm, gm16, g16, gp16, l1x, l2x = (act.alloc_register(n) for n in ("a_g", "a_gp", "a_gm", "a_gm16", "a_g16", "a_gp16", "a_l1x", "a_l2x"))
                    xrow, yrow = act.alloc_register("a_xrow"), act.alloc_register("a_yrow")
                    act.reg_mov(gm, 0)
                    act.reg_mov(g, 1)
                    act.reg_mov(gp, 2)
                    act.reg_mov(gm16, 0)
                    act.reg_mov(g16, 16)
                    act.reg_mov(gp16, 32)
                    act.reg_mov(l1x, 16)
                    act.reg_mov(l2x, 32)
                    act.reg_mov(xrow, 2)
                    act.reg_mov(yrow, 0)

                    def upper_w(js, used, landed):
                        for j in js:
                            if j in ACT_HI:
                                act.wait_ge(w_used[j], used)
                                act.wait_ge(pair_in[j // 2], landed)
                                nc.scalar.activation(hi(j), raw(j), ACT.Copy).then_inc(w_hi[j], 1)

                    def upper_x(count):
                        act.wait_ge(S["xbt"], count)
                        nc.scalar.activation(xb_hi[:, 0:4, :], bank[2][:, :].rearrange("p (k c) -> p k c", c=P), ACT.Copy).then_inc(S["xbh"], 1)
                        act.wait_ge(S["hbt"], count)
                        nc.scalar.activation(xb_hi[:, 4:8, :], bank[3][:, :].rearrange("p (k c) -> p k c", c=P), ACT.Copy).then_inc(S["xbh2"], 1)

                    def outputs():
                        act.wait_ge(w_used[RING - 1], g)
                        act.wait_ge(S["yst"], gm16)
                        nc.scalar.activation(yb[:, 0:HALF], bank[5][:, :], ACT.Copy)
                        nc.scalar.activation(yb[:, HALF:D], bank[6][:, :], ACT.Copy).then_inc(S["yevd"], 1)
                        act.wait_ge(S["yevd"], g)
                        act.dma_start(xbuf[bass.ds(act.snap(yrow, min_val=0, max_val=MAX_BLOCKS - 1), 1)].rearrange("b p d -> (b p) d"), yb[:, :]).then_inc(S["yst"], 16)
                        act.reg_add(yrow, yrow, 1)

                    upper_w(range(RING), 1, 16)
                    act.wait_ge(scat, scat_goal)
                    act.dma_start(xg[:, :], xbuf[0]).then_inc(S["xg_in"], 16)
                    upper_x(1)
                    act.dma_start(xg[:, :], xbuf[1]).then_inc(S["xg_in"], 16)
                    act.reg_add(scat_goal, scat_goal, 16 * 2 * TT)
                    act.wait_ge(S["nbd"], 1)

                    with act.Fori(0, N_EXP) as e:
                        blocks = act.value_load(nblk[0:1, bass.ds(e, 1)], min_val=1, max_val=TT)
                        with act.Fori(0, blocks) as b:
                            act.wait_ge(w_used[3], gp)
                            nc.scalar.activation(sg[:, :], bank[0][:, :], ACT.Silu).then_inc(S["sgs"], 1)
                            with act.If(b + 1 == blocks):
                                with act.If(e < N_EXP - 1):
                                    upper_w(range(0, 4), gp, l2x)
                            upper_x(gp)
                            act.dma_start(xg[:, :], xbuf[bass.ds(act.snap(xrow, min_val=0, max_val=MAX_BLOCKS + 1), 1)].rearrange("b p d -> (b p) d")).then_inc(S["xg_in"], 16)
                            with act.If(b + 1 == blocks):
                                with act.If(e < N_EXP - 1):
                                    upper_w(range(4, 8), gp, l2x)
                            act.wait_ge(S["htt"], g)
                            nc.scalar.activation(ht_hi[:, :, :], bank[4][:, :].rearrange("p (k c) -> p k c", c=P), ACT.Copy).then_inc(S["hth"], 1)
                            with act.If(act.snap(gm, min_val=0, max_val=MAX_BLOCKS) > 0):
                                outputs()
                            with act.If(b < 1):
                                with act.If(e > 0):
                                    upper_w(range(8, RING), g, l1x)
                            for r, by in ((g, 1), (gp, 1), (gm, 1), (gm16, 16), (g16, 16), (gp16, 16), (xrow, 1)):
                                act.reg_add(r, r, by)
                        act.reg_add(l1x, l1x, 16)
                        act.reg_add(l2x, l2x, 16)
                    outputs()
                    act.wait_ge(S["yst"], g16)
                    act.wait_ge(S["xg_in"], gp16)
                    nc.scalar.activation(small[:, 1023:1024], eps, ACT.Copy).then_inc(S["allst"], 1)
                    norm(1)

                @block.vector
                def _(dve):
                    done = [0]

                    def link(ins):
                        done[0] += 1
                        ins.then_inc(S["chain_d"], 1)
                        dve.wait_ge(S["chain_d"], done[0])

                    def split(n):
                        w = chunk_width(n)
                        dve.wait_ge(S["a_hi"], n + 1)
                        nc.vector.tensor_tensor(lo(n % RA)[:, 0:w], raw(n % RA)[:, 0:w], f(hi(n % RA)[:, 0:w]), ALU.subtract).then_inc(S["a_lo"], 1)

                    nrm = [0]

                    def lower(tile, src):
                        nrm[0] += 1
                        dve.wait_ge(S["nrm_h"], nrm[0])
                        nc.vector.tensor_tensor(n_lo[:, tile, :], src, f(n_hi[:, tile, :]), ALU.subtract).then_inc(S["nrm_l"], 1)

                    def normalise(which, tiles):
                        dve.wait_ge(S["rs_std"], which)
                        link(nc.vector.reciprocal(rstd[:, :], rstd[:, :]))
                        for tile, src, g in tiles:
                            nc.vector.scalar_tensor_tensor(out=src, in0=src, scalar=par[:, g:g + 1], in1=rstd[:, :], op0=ALU.mult, op1=ALU.mult).then_inc(S["nz"], 1)
                        for tile, src, g in tiles:
                            lower(tile, src)

                    dve.wait_ge(S["par_in"], 16)
                    lam = par[:, LAM:LAM + LT]
                    link(nc.vector.tensor_scalar(sp_b, lam, -1.0, None, ALU.mult))
                    nc.vector.tensor_tensor(sp_a, lam, sp_b, ALU.max).then_inc(S["sp_abs"], 1)
                    for c in range(DT):
                        dve.wait_ge(S["xt_h"], c + 1)
                        nc.vector.tensor_tensor(xt_lo[:, c, :], bank[2 + c % 2][:, :], f(xt_hi[:, c, :]), ALU.subtract).then_inc(S["xt_l"], 1)
                    for n in range(RA):
                        split(n)
                    dve.wait_ge(S["sp_exp"], 1)
                    link(nc.vector.tensor_scalar(sp_c, sp_e, 2.0, None, ALU.add))
                    link(nc.vector.reciprocal(sp_c, sp_c))
                    link(nc.vector.tensor_tensor(sp_c, sp_c, sp_e, ALU.mult))
                    link(nc.vector.tensor_tensor(sp_d, sp_c, sp_c, ALU.mult))
                    link(nc.vector.tensor_scalar(sp_a, sp_d, 1.0 / 17, 1.0 / 15, ALU.mult, ALU.add))
                    for k in (13, 11, 9, 7, 5, 3, 1):
                        link(nc.vector.tensor_tensor(sp_a, sp_a, sp_d, ALU.mult))
                        link(nc.vector.tensor_scalar(sp_a, sp_a, 1.0 / k, None, ALU.add))
                    link(nc.vector.tensor_tensor(sp_a, sp_a, sp_c, ALU.mult))
                    link(nc.vector.tensor_scalar(sp_b, sp_b, 0.0, None, ALU.max))
                    link(nc.vector.scalar_tensor_tensor(out=sp_a, in0=sp_a, scalar=2.0, in1=sp_b, op0=ALU.mult, op1=ALU.add))
                    nc.vector.tensor_scalar(c4, sp_a, 4.0, None, ALU.mult).then_inc(S["c4d"], 1)

                    for n in range(N_IN):
                        dve.wait_ge(S["gemm"], n + 1)
                        o = bank[n % 2]
                        if n < QT + KT:
                            m = nc.vector.tensor_copy(z_lat[:, n, :], o[:, :])
                        elif n == QT + KT:
                            m = nc.vector.tensor_tensor(krot[:, :], o[:, :], rot, ALU.mult)
                        elif n < QT + KT + 1 + LT:
                            m = nc.vector.tensor_copy(z_u[:, n - QT - KT - 1, 3:3 + SEQ], o[:, :])
                        else:
                            m = nc.vector.tensor_copy(z_gate[:, n - QT - KT - 1 - LT, :], o[:, :])
                        m.then_inc(S["ev_dve"], 1)
                        split(n + RA)
                        if n == N_IN - 5:
                            normalise(1, [(QT + k, z_lat[:, QT + k, :], QG + QT + k) for k in range(KT)])
                            dve.wait_ge(S["rs_std"], 2)
                            link(nc.vector.reciprocal(rstd[:, :], rstd[:, :]))
                        if N_IN - 5 < n < N_IN - 1:
                            for k in range(2):
                                tile = 2 * (n - N_IN + 4) + k
                                nc.vector.scalar_tensor_tensor(out=z_lat[:, tile, :], in0=z_lat[:, tile, :], scalar=par[:, QG + tile:QG + tile + 1], in1=rstd[:, :], op0=ALU.mult, op1=ALU.mult).then_inc(S["nz"], 1)
                            for k in range(2):
                                tile = 2 * (n - N_IN + 4) + k
                                lower(tile, z_lat[:, tile, :])

                    def conv(t):
                        if t == 0:
                            dve.wait_ge(S["pad"], 1)
                        if t >= 2:
                            dve.wait_ge(S["gmm"], 2 * (t - 1))
                            dve.wait_ge(S["ixd"], t - 1)
                        o = xc[:, t % 2, :]
                        link(nc.vector.tensor_scalar(o, z_u[:, t, 3:3 + SEQ], par[:, CONV_W + 3 * LT + t:CONV_W + 3 * LT + t + 1], par[:, CONV_B + t:CONV_B + t + 1], ALU.mult, ALU.add))
                        for w in range(3):
                            m = nc.vector.scalar_tensor_tensor(out=o, in0=z_u[:, t, w:w + SEQ], scalar=par[:, CONV_W + w * LT + t:CONV_W + w * LT + t + 1], in1=o, op0=ALU.mult, op1=ALU.add)
                            if w < 2:
                                link(m)
                        m.then_inc(S["xcd"], 1)

                    def gated_in(t):
                        dve.wait_ge(S["gact"], 2 * t + 2)
                        dve.wait_ge(S["xcd"], t + 1)
                        nc.vector.tensor_tensor(z_u[:, t, 3:3 + SEQ], z_u[:, t, 3:3 + SEQ], xc[:, t % 2, :], ALU.mult).then_inc(S["ixd"], 1)

                    conv(0)
                    conv(1)
                    split(C_K + RA)
                    gated_in(0)
                    conv(2)
                    split(C_V + RA)
                    gated_in(1)
                    conv(3)
                    def rotated_out(h):
                        m = M_Q + 2 * h + 1
                        dve.wait_ge(S["gemm"], m + 1)
                        nc.vector.scalar_tensor_tensor(out=q[:, HEADS + h, :], in0=bank[m % 2][:, :], scalar=QK_HEAD ** -0.5, in1=rot, op0=ALU.mult, op1=ALU.mult).then_inc(S["ev_dve"], 1)

                    split(C_Q + RA)
                    rotated_out(0)
                    split(C_Q + 1 + RA)
                    gated_in(2)
                    gated_in(3)

                    def recur(t):
                        inv, decay = xc[:, 0, :], xc[:, 1, :]
                        u = z_u[:, t, 3:3 + SEQ]
                        dve.wait_ge(S["sqrtd"], LT)
                        dve.wait_ge(S["ixd"], LT)
                        dve.wait_ge(S["geld"], LT)
                        link(nc.vector.tensor_scalar(inv, rt[:, t, :], 1.0, None, ALU.add))
                        link(nc.vector.reciprocal(inv, inv))
                        nc.vector.tensor_scalar(decay, inv, 2.0, -1.0, ALU.mult, ALU.add)
                        link(nc.vector.scalar_tensor_tensor(out=inv, in0=inv, scalar=2.0, in1=root[:, t, :], op0=ALU.mult, op1=ALU.mult))
                        link(nc.vector.tensor_tensor(u, u, inv, ALU.mult))
                        link(nc.vector.tensor_tensor_scan(rt[:, t, :], decay, u, 0.0, ALU.mult, ALU.add))
                        nc.vector.tensor_tensor(z_gate[:, t, :], z_gate[:, t, :], rt[:, t, :], ALU.mult).then_inc(S["lrud"], 1)

                    def divide(s):
                        dve.wait_ge(S["ex"], s + 1)
                        link(nc.vector.reciprocal(pinv[:, s:s + 1], psum_[:, s:s + 1]))
                        w = (s % TT + 1) * P
                        nc.vector.tensor_scalar(prob[:, s % 2, 0:w], prob[:, s % 2, 0:w], pinv[:, s:s + 1], None, ALU.mult).then_inc(S["pn"], 1)

                    def head_out(h):
                        dve.wait_ge(S["pv"], h + 1)
                        nc.vector.tensor_copy(q[:, h, :], bank[6][:, :]).then_inc(S["mla"], 1)

                    STEPS = HEADS * TT
                    for s in range(STEPS):
                        w = (s % TT + 1) * P
                        dve.wait_ge(S["sc"], s + 1)
                        nc.vector.tensor_reduce(nmax[:, s:s + 1], bank[4 + s % 2][:, 0:w], AX.X, ALU.max, negate=True).then_inc(S["nm"], 1)
                        if s:
                            divide(s - 1)
                        h, i = s // TT, s % TT
                        if h + 1 < HEADS and i == 2:
                            split(C_Q + 2 * h + 2 + RA)
                        if h + 1 < HEADS and i == 3:
                            rotated_out(h + 1)
                            split(C_Q + 2 * h + 3 + RA)
                        if h and i == 0:
                            if h >= 2:
                                head_out(h - 2)
                        if h and i == 1:
                            recur(h - 1)
                    divide(STEPS - 1)
                    head_out(HEADS - 2)
                    recur(LT - 1)
                    head_out(HEADS - 1)
                    normalise(3, [(t, z_gate[:, t, :], OG + t) for t in range(LT)])
                    normalise(4, [(LT + h, q[:, h, :], OG + LT + h) for h in range(HEADS)])
                    for n in range(C_OUT + 4, N_CHUNK):
                        split(n)

                    def moments(k, i):
                        nc.vector.bn_stats(stats[i][:, 0:6], x[:, i, 0:HALF])
                        link(nc.vector.bn_stats(stats[i][:, 6:12], x[:, i, HALF:D]))
                        nc.vector.bn_aggr(mv[i], stats[i]).then_inc(S["vd"], 1)

                    def invert(k, i):
                        dve.wait_ge(S["stdd"], TT * k + i + 1)
                        link(nc.vector.reciprocal(rstd_t[:, i:i + 1], std[:, i:i + 1]))
                        nc.vector.scalar_tensor_tensor(out=nmr[:, i:i + 1], in0=mv[i][:, 0:1], scalar=-1.0, in1=rstd_t[:, i:i + 1], op0=ALU.mult, op1=ALU.mult).then_inc(S["lnx"], 1)

                    def gain(k, i):
                        dve.wait_ge(S["lng"], TT * k + i + 1)
                        nc.vector.tensor_tensor(x[:, i, :], x[:, i, :], lnbc[:, 0, :], ALU.mult).then_inc(S["lnm"], 1)

                    def shift(k, i):
                        dve.wait_ge(S["lnm"], TT * k + i + 1)
                        nc.vector.tensor_tensor(x[:, i, :], x[:, i, :], lnbc[:, 1, :], ALU.add).then_inc(S["lnb"], 1)

                    for i in range(TT + 1):
                        if i < TT:
                            dve.wait_ge(S["opd"], 4 + i + 1)
                            for half in range(2):
                                s = slice(half * HALF, (half + 1) * HALF)
                                m = nc.vector.scalar_tensor_tensor(out=x[:, i, s], in0=x[:, i, s], scalar=ALPHA, in1=bank[4 * half + i][:, :], op0=ALU.mult, op1=ALU.add)
                                if half:
                                    link(m)
                            moments(0, i)
                        if i:
                            if i == 1:
                                dve.wait_ge(S["ln1_in"], 16)
                            gain(0, i - 1)
                        if i < TT:
                            invert(0, i)
                        if i:
                            shift(0, i - 1)

                    def rows(ap, n):
                        return ap.rearrange("p (i n) -> p i n", n=n)

                    def wide(ap, n):
                        return ap.unsqueeze(2).to_broadcast([P, ap.shape[1], n])

                    tt = nc.vector.tensor_tensor
                    dve.wait_ge(S["sgd"], TT)
                    link(tt(sel, s_e, rb[:, :], ALU.add))
                    quad = rows(sel, 4)
                    tt(g_a, quad[:, :, 0], quad[:, :, 1], ALU.max)
                    tt(g_b, quad[:, :, 0], quad[:, :, 1], ALU.min)
                    tt(g_c, quad[:, :, 2], quad[:, :, 3], ALU.max)
                    link(tt(g_d, quad[:, :, 2], quad[:, :, 3], ALU.min))
                    tt(g_e, g_a, g_c, ALU.max)
                    tt(g_f, g_a, g_c, ALU.min)
                    link(tt(g_b, g_b, g_d, ALU.max))
                    link(tt(g_f, g_f, g_b, ALU.max))
                    link(tt(g_e, g_e, g_f, ALU.add))

                    def first_best(values_, n, weights, out_):
                        link(nc.vector.tensor_reduce(t_a, rows(values_, n), AX.X, ALU.max))
                        link(tt(rows(out_, n), rows(values_, n), wide(t_a, n), ALU.is_equal))
                        link(tt(out_, out_, weights, ALU.mult))
                        link(nc.vector.tensor_reduce(t_a, rows(out_, n), AX.X, ALU.max))
                        link(tt(rows(out_, n), rows(out_, n), wide(t_a, n), ALU.is_equal))

                    first_best(g_e, N_GRP, cst[:, GW:GW + TT * N_GRP], g_a)
                    link(nc.vector.tensor_scalar(g_b, g_a, BIG, -BIG, ALU.mult, ALU.add))
                    link(tt(rows(masked, 4), quad, wide(g_a, 4), ALU.mult))
                    link(tt(rows(masked, 4), rows(masked, 4), wide(g_b, 4), ALU.add))
                    ew = cst[:, EW:EW + TT * N_EXP]
                    first_best(masked, N_EXP, ew, oh1)
                    link(nc.vector.scalar_tensor_tensor(out=masked, in0=oh1, scalar=-BIG, in1=masked, op0=ALU.mult, op1=ALU.add))
                    first_best(masked, N_EXP, ew, oh2)
                    tt(use, oh1, oh2, ALU.add).then_inc(S["used_d"], 1)
                    dve.wait_ge(S["pfx"], 1)
                    link(nc.vector.tensor_copy(tot, bank[7][:, 0:TT * N_EXP]))
                    link(nc.vector.tensor_reduce(cnt, tot.rearrange("p (i n) -> p n i", n=N_EXP), AX.X, ALU.add))
                    link(nc.vector.tensor_scalar(nb, cnt, float(P), 1.0, ALU.is_gt, ALU.add))
                    for k in range(2, TT):
                        link(nc.vector.scalar_tensor_tensor(out=nb, in0=cnt, scalar=float(k * P), in1=nb, op0=ALU.is_gt, op1=ALU.add))
                    link(nc.vector.tensor_tensor_scan(cum, onecol, nb, 0.0, ALU.mult, ALU.add))
                    link(tt(cum, cum, nb, ALU.subtract))
                    link(nc.vector.tensor_scalar(first[:, 0:N_EXP], cum, float(P), None, ALU.mult))
                    for i in range(1, TT):
                        link(tt(first[:, i * N_EXP:(i + 1) * N_EXP], first[:, (i - 1) * N_EXP:i * N_EXP], tot[:, (i - 1) * N_EXP:i * N_EXP], ALU.add))
                    link(tt(dst, bank[4][:, 0:TT * N_EXP], first, ALU.add))
                    tt(tmp, dst, oh1, ALU.mult)
                    link(tt(tmp2, dst, oh2, ALU.mult))
                    nc.vector.tensor_reduce(dstk[:, 0:TT], rows(tmp, N_EXP), AX.X, ALU.add)
                    link(nc.vector.tensor_reduce(dstk[:, TT:2 * TT], rows(tmp2, N_EXP), AX.X, ALU.add))
                    nc.vector.tensor_copy(nblk, nb)
                    nc.vector.tensor_copy(idx, dstk).then_inc(S["nbd"], 1)
                    dve.wait_ge(S["nbd"], 1)
                    link(tt(tmp, s_e, oh1, ALU.mult))
                    link(nc.vector.tensor_reduce(w1, rows(tmp, N_EXP), AX.X, ALU.add))
                    link(tt(tmp, s_e, oh2, ALU.mult))
                    link(nc.vector.tensor_reduce(w2, rows(tmp, N_EXP), AX.X, ALU.add))
                    link(tt(wr, w1, w2, ALU.add))
                    link(nc.vector.reciprocal(wr, wr))
                    tt(gate[:, 0:TT], w1, wr, ALU.mult)
                    link(tt(gate[:, TT:2 * TT], w2, wr, ALU.mult))

                    g, gp, l1, l2, l1x, l2x = (dve.alloc_register(n) for n in ("d_g", "d_gp", "d_l1", "d_l2", "d_l1x", "d_l2x"))
                    dve.reg_mov(g, 1)
                    dve.reg_mov(gp, 2)
                    dve.reg_mov(l1, 1)
                    dve.reg_mov(l2, 2)
                    dve.reg_mov(l1x, 16)
                    dve.reg_mov(l2x, 32)

                    def split_w(js, used, landed, lap):
                        for j in js:
                            if j not in ACT_HI:
                                dve.wait_ge(w_used[j], used)
                                dve.wait_ge(pair_in[j // 2], landed)
                                nc.vector.tensor_copy(hi(j), raw(j)).then_inc(w_hi[j], 1)
                            if j not in POOL_LO:
                                dve.wait_ge(w_hi[j], lap)
                                nc.vector.tensor_tensor(lo(j), raw(j), f(hi(j)), ALU.subtract).then_inc(w_lo[j], 1)

                    def lower_x(count):
                        dve.wait_ge(S["xbh"], count)
                        nc.vector.tensor_tensor(xb_lo[:, 0:4, :], bank[2][:, :].rearrange("p (k c) -> p k c", c=P), f(xb_hi[:, 0:4, :]), ALU.subtract)
                        dve.wait_ge(S["xbh2"], count)
                        nc.vector.tensor_tensor(xb_lo[:, 4:8, :], bank[3][:, :].rearrange("p (k c) -> p k c", c=P), f(xb_hi[:, 4:8, :]), ALU.subtract).then_inc(S["xbl"], 1)

                    dve.wait_ge(S["lg"], TT)
                    split_w(range(0, 8), 1, 16, 1)
                    lower_x(1)
                    split_w(range(8, RING), 1, 16, 1)

                    with dve.Fori(0, N_EXP) as e:
                        blocks = dve.value_load(nblk[0:1, bass.ds(e, 1)], min_val=1, max_val=TT)
                        with dve.Fori(0, blocks) as b:
                            with dve.If(b + 1 == blocks):
                                with dve.If(e < N_EXP - 1):
                                    split_w(range(0, 4), gp, l2x, l2)
                            dve.wait_ge(w_used[7], gp)
                            dve.wait_ge(S["sgs"], g)
                            nc.vector.tensor_tensor(hb[:, :], bank[1][:, :], sg[:, :], ALU.mult).then_inc(S["hbd"], 1)
                            lower_x(gp)
                            with dve.If(b + 1 == blocks):
                                with dve.If(e < N_EXP - 1):
                                    split_w(range(4, 8), gp, l2x, l2)
                            dve.wait_ge(S["hth"], g)
                            nc.vector.tensor_tensor(ht_lo[:, :, :], bank[4][:, :].rearrange("p (k c) -> p k c", c=P), f(ht_hi[:, :, :]), ALU.subtract).then_inc(S["htl"], 1)
                            with dve.If(b < 1):
                                with dve.If(e > 0):
                                    split_w(range(8, RING), g, l1x, l1)
                            dve.reg_add(g, g, 1)
                            dve.reg_add(gp, gp, 1)
                        for r, by in ((l1, 1), (l2, 1), (l1x, 16), (l2x, 16)):
                            dve.reg_add(r, r, by)

                    for i in range(TT + 1):
                        if i < TT:
                            dve.wait_ge(gath[i], gath_goal)
                            link(nc.vector.tensor_scalar(yg[:, 2 * i, :], yg[:, 2 * i, :], gate[:, i:i + 1], None, ALU.mult))
                            link(nc.vector.scalar_tensor_tensor(out=yg[:, 2 * i, :], in0=yg[:, 2 * i + 1, :], scalar=gate[:, TT + i:TT + i + 1], in1=yg[:, 2 * i, :], op0=ALU.mult, op1=ALU.add))
                            link(nc.vector.scalar_tensor_tensor(out=x[:, i, :], in0=x[:, i, :], scalar=ALPHA, in1=yg[:, 2 * i, :], op0=ALU.mult, op1=ALU.add))
                            moments(1, i)
                        if i:
                            if i == 1:
                                dve.wait_ge(S["ln2_in"], 16)
                            gain(1, i - 1)
                        if i < TT:
                            invert(1, i)
                        if i == TT:
                            shift(1, i - 1)
                    dve.reg_add(gath_goal, gath_goal, 32)

                @block.gpsimd
                def _(pool):
                    for j in range(RING):
                        pool.sem_inc(w_used[j], 1)
                        pool.sem_inc(w_lo[j], 1)
                    pool.sem_inc(S["yevd"], 1)
                    pool.sem_inc(S["yst"], 16)

                    nc.gpsimd.memset(z_u[:, :, 0:3], 0.0).then_inc(S["pad"], 1)

                    kappa, added = 0, 0
                    for grp, n in enumerate(SQ_GROUPS):
                        for k in range(n):
                            kappa += 1
                            if k == 0:
                                continue
                            pool.wait_ge(S["sqd"], kappa)
                            if k == 1 and grp >= 2:
                                pool.wait_ge(S[("sums_q", "sums_kv")[grp - 2]], 1)
                            if k >= 2:
                                pool.wait_ge(S["sqa"], added)
                            m0 = sq[:, 0, :] if k == 1 else acc[:, grp % 2, :]
                            nc.gpsimd.tensor_tensor(acc[:, grp % 2, :], m0, sq[:, 1, :] if k == 1 else sq[:, (kappa - 1) % 2, :], ALU.add).then_inc(S["sqa"], 1)
                            added += 1

                    pool.wait_ge(S["nbd"], 1)
                    pool.wait_ge(filled, 16 * (MAX_BLOCKS + 2))
                    pool.wait_ge(S["lnb"], TT)
                    for k in range(2):
                        for i in range(TT):
                            c = k * TT + i
                            pool.indirect_dma_start(out=xrows, out_offset=bass.IndirectOffsetOnAxis(ap=idx[:, c:c + 1], axis=0), in_=x[:, i, :], in_offset=None).then_inc(scat, 16)

                    lap = pool.alloc_register("p_lap")
                    pool.reg_mov(lap, 1)
                    with pool.Fori(0, N_EXP) as e:
                        for j in POOL_LO:
                            pool.wait_ge(w_hi[j], lap)
                            nc.gpsimd.tensor_tensor(lo(j), raw(j), f(hi(j)), ALU.subtract).then_inc(w_lo[j], 1)
                        pool.reg_add(lap, lap, 1)

                    pool.wait_ge(S["allst"], 1)
                    for i in range(TT):
                        for k in range(2):
                            c = k * TT + i
                            pool.indirect_dma_start(out=yg[:, 2 * i + k, :], out_offset=None, in_=xrows, in_offset=bass.IndirectOffsetOnAxis(ap=idx[:, c:c + 1], axis=0)).then_inc(gath[i], 16)
                    pool.wait_ge(S["ln2_in"], 16)
                    for i in range(TT - 1):
                        pool.wait_ge(S["lnm"], TT + i + 1)
                        nc.gpsimd.tensor_tensor(x[:, i, :], x[:, i, :], lnbc[:, 1, :], ALU.add).then_inc(S["lnp"], 1)

            with nc.Block() as block:
                @block.gpsimd
                def _(pool):
                    for s in every:
                        pool.sem_clear(s)

        with nc.Block() as block:
            @block.sync
            def _(sp):
                sp.dma_start(out[0].rearrange("(i p) d -> p i d", p=P), x[:, :, :]).then_inc(init, 16)
                sp.wait_ge(init, 80)


ARRAYS = ("x", "cst", "rw", "rb", "par", "gw", "ln", "wm", "we")


def kernel(x, w_in, conv_w, conv_b, w_rgate, b_rgate, w_igate, b_igate, lru_lambda, q_norm_g, w_q_up, kv_norm_g, w_kv_up,
           out_norm_g, w_out, ln1_g, ln1_b, router_w, router_bias, w_exp_gate, w_exp_up, w_exp_down, ln2_g, ln2_b):
    import numpy as np
    import concourse.bacc as bacc
    from concourse.bass_utils import run_bass_kernel_spmd

    pos = np.arange(SEQ, dtype=np.float32)
    inv = (np.float32(10000.0) ** (-np.arange(ROPE // 2, dtype=np.float32) / np.float32(ROPE // 2))).astype(np.float32)
    ang = pos[None, :] * inv[:, None]
    cos, sin = np.cos(ang), np.sin(ang)
    r = np.arange(P)
    pieces = [np.eye(P), np.ones((P, P)), r[:, None] < r[None, :],
              r[:, None] % ROPE == r[None, :] % ROPE, np.concatenate([cos, cos, -sin, sin]), np.where(r[None, :] <= r[:, None], 0.0, -BIG),
              np.tile(np.arange(N_EXP, 0, -1), (P, TT)), np.tile(np.arange(N_GRP, 0, -1), (P, TT))]
    cst = np.concatenate([np.asarray(p, np.float32) for p in pieces], axis=1)

    def tiles(w):
        w = np.asarray(w)
        return np.moveaxis(w.reshape(w.shape[0], w.shape[1] // P, P, *w.shape[2:]), 2, 1)

    def columns(v):
        v = np.asarray(v).reshape(DEPTH, -1)
        return np.moveaxis(v.reshape(DEPTH, -1, P), 2, 1)

    par = np.concatenate([columns(np.asarray(conv_w)), columns(conv_b), columns(b_rgate), columns(b_igate), columns(lru_lambda),
                          columns(q_norm_g), columns(kv_norm_g), columns(out_norm_g)], axis=2)
    gw = np.zeros((DEPTH, P, 2 * LT, P), np.float32)
    for s, w in enumerate((w_rgate, w_igate)):
        w = np.asarray(w).reshape(DEPTH, LT, 2, 64, 64)
        for b in range(2):
            gw[:, 64 * b:64 * b + 64, s * LT:(s + 1) * LT, 64 * b:64 * b + 64] = np.moveaxis(w[:, :, b], 2, 1)
    gw = gw.reshape(DEPTH, P, -1)
    turned = np.r_[0:32, 32:64, 32:64, 0:32]
    wi = np.asarray(w_in)
    order = [2 * LRU + P * t + r for t in range(QT + KT)] + [2 * LRU + Q_LORA + KV_LORA + turned] + [P * t + r for t in range(2 * LT)]
    wm = np.zeros((DEPTH, N_CHUNK, P, CH), np.float32)
    for n, c in enumerate(order):
        wm[:, n] = tiles(wi[:, :, c]).reshape(DEPTH, P, CH)
    kv = tiles(w_kv_up)
    wm[:, C_K] = kv[..., 0:P].reshape(DEPTH, P, CH)
    wm[:, C_V] = kv[..., P:].reshape(DEPTH, P, CH)
    qu = tiles(w_q_up)
    for h in range(HEADS):
        wm[:, C_Q + 2 * h, :, 0:Q_LORA] = qu[:, :, :, h, 0:P].reshape(DEPTH, P, -1)
        wm[:, C_Q + 2 * h + 1, :, 0:Q_LORA] = qu[:, :, :, h, P + turned].reshape(DEPTH, P, -1)
    wo = tiles(w_out)
    for half in range(2):
        for c in range(4):
            wm[:, C_OUT + 4 * half + c] = wo[:, :, 2 * c:2 * c + 2, half * HALF:(half + 1) * HALF].reshape(DEPTH, P, CH)
    we = np.empty((DEPTH, N_EXP, PAIRS, P, 2 * CH), np.float32)
    for s, w in enumerate((w_exp_gate, w_exp_up)):
        w = np.asarray(w).reshape(DEPTH, N_EXP, 2, 4, P, F_EXP)
        we[:, :, 2 * s:2 * s + 2] = np.moveaxis(w, 4, 3).reshape(DEPTH, N_EXP, 2, P, 2 * CH)
    w = np.asarray(w_exp_down).reshape(DEPTH, N_EXP, 2, 2, P, D)
    we[:, :, 4:6] = np.moveaxis(w, 4, 3).reshape(DEPTH, N_EXP, 2, P, 2 * CH)
    ln = np.stack([np.stack([np.asarray(ln1_g), np.asarray(ln1_b)], 1), np.stack([np.asarray(ln2_g), np.asarray(ln2_b)], 1)], 1)
    rw = np.moveaxis(np.asarray(router_w).reshape(DT, P, N_EXP), 1, 0).reshape(P, -1)
    rb = np.ascontiguousarray(np.broadcast_to(np.asarray(router_bias), (P, TT, N_EXP)).reshape(P, -1))

    nc = bacc.Bacc("TRN2", target_bir_lowering=False, num_devices=1)
    host = dict(x=np.asarray(x), cst=cst, rw=rw, rb=rb, par=par, gw=gw, ln=ln, wm=wm, we=we)
    arrays, args = {}, {}
    for name in ARRAYS:
        arrays[name + "_in"] = np.ascontiguousarray(host[name])
        args[name] = nc.dram_tensor(name + "_in", arrays[name + "_in"].shape, F32, kind="ExternalInput").ap()
    out = nc.dram_tensor("out_dram", (1, SEQ, D), F32, kind="ExternalOutput").ap()
    build(nc, args, out)
    return run_bass_kernel_spmd(nc, [arrays], core_ids=[0]).results[0]["out_dram"]
```

```python
from contextlib import ExitStack

import concourse.bass as bass
from concourse import mybir

F32 = mybir.dt.float32
F32R = mybir.dt.float32r
I32 = mybir.dt.int32
ALU = mybir.AluOpType
ACT = mybir.ActivationFunctionType
AX = mybir.AxisListType

P = 128
D = 1024
SEQ = 512
DEPTH = 2
LRU = 512
HEADS = 4
ROPE = 64
QK_HEAD = 192
Q_LORA = 768
KV_LORA = 256
N_EXP = 16
N_GRP = 4
F_EXP = 512
EPS = 1e-6
ALPHA = float((2 * DEPTH) ** 0.25)
BIG = 1e30
KB = 1024

TT = SEQ // P
DT = D // P
LT = LRU // P
QT = Q_LORA // P
KT = KV_LORA // P
FT = F_EXP // P
HALF = D // 2
CH = 1024
RA = 4
RING = 12
PAIRS = RING // 2
MAX_BLOCKS = N_EXP - 1 + SEQ * 2 // P

N_IN = QT + KT + 1 + 2 * LT
C_K = N_IN
C_V = C_K + 1
C_Q = C_V + 1
C_OUT = C_Q + 2 * HEADS
N_CHUNK = C_OUT + 8
OUT_ORDER = ((0, 0), (0, 1), (1, 0), (1, 1), (0, 2), (0, 3), (1, 2), (1, 3))
M_K = N_IN
M_V = M_K + HEADS
M_Q = M_V + TT
MIX_STEP = 7
VALUE_STEPS = (7, 9, 13)
RECUR_STEPS = (0, 1, 4, 5)


def chunk_width(n):
    return Q_LORA if C_Q <= n < C_OUT else CH


SQ_GROUPS = (QT, KT, LT, HEADS)


def sq_taken(kappa):
    added = 0
    for n in SQ_GROUPS:
        if kappa < n:
            return added + max(kappa, 1)
        kappa -= n
        added += n - 1


ACT_HI = (0, 1, 2, 4, 5, 6, 8, 9, 10)
POOL_LO_0 = (1, 2, 5, 8, 9, 10, 11)
POOL_LO = (1, 3, 4, 6)

IDENT, ONES, TRI, DUP, ROT = 0, 128, 256, 384, 512
CMASK = ROT + SEQ
EW = CMASK + P
GW = EW + TT * N_EXP
EARLIER = GW + TT * N_GRP
N_CST = EARLIER + 16
CONV_W, CONV_B, B_R, B_I, LAM = 0, 4 * LT, 5 * LT, 6 * LT, 7 * LT
QG = 8 * LT
OG = QG + QT + KT
N_PAR = OG + DT


def build(nc, a, out):
    with ExitStack() as ctx:
        base = (nc.sbuf_base + 63) // 64 * 64

        def at(kb, name, shape, dt=F32):
            return nc.alloc_sbuf_tensor_at(name, shape, dt, offset=base + int(kb * KB))

        def sem(name):
            return ctx.enter_context(nc.semaphore(name))

        x = at(0, "x", [P, TT, D])
        cst = at(16, "cst", [P, N_CST])
        rw = at(21, "rw", [P, DT * N_EXP])
        rb = at(21.5, "rb", [P, TT * N_EXP])
        par = at(21.75, "par", [P, N_PAR])
        small = at(22, "small", [P, 1024])
        lnbc = at(26, "lnbc", [P, 2, D])
        gatew = at(26, "gatew", [P, 2 * LT, P])
        raw_a = at(34, "raw_a", [P, RA, CH])
        hi_a = at(50, "hi_a", [P, RA, CH], F32R)
        lo_a = at(66, "lo_a", [P, RA, CH], F32R)
        raw_b = at(82, "raw_b", [P, RING - RA, CH])
        hi_b = at(114, "hi_b", [P, RING - RA, CH], F32R)
        lo_b = at(146, "lo_b", [P, RING - RA, CH], F32R)
        n_hi = at(82, "n_hi", [P, DT, SEQ], F32R)
        n_lo = at(98, "n_lo", [P, DT, SEQ], F32R)
        xt_hi = at(114, "xt_hi", [P, DT, SEQ], F32R)
        xt_lo = at(130, "xt_lo", [P, DT, SEQ], F32R)
        q = at(114, "q", [P, 2 * HEADS, SEQ])
        x1t = at(179, "x1t", [P, DT, SEQ])
        kn = at(130, "kn", [P, HEADS, SEQ])
        v = at(138, "v", [P, TT, HEADS * P])
        z_gate = at(146, "z_gate", [P, LT, SEQ])
        z_lat = at(154, "z_lat", [P, QT + KT, SEQ])
        pt = at(154, "pt", [P, 2, TT, SEQ])
        root_a, root_b = at(162, "root_a", [P, 2, SEQ]), at(30, "root_b", [P, LT - 2, SEQ])
        z_u = at(170, "z_u", [P, LT, 3 + SEQ])
        prob = at(179, "prob", [P, 2, SEQ])
        krot = at(179, "krot", [P, SEQ])
        sq = at(183, "sq", [P, 2, SEQ])
        acc = at(187, "acc", [P, 2, SEQ])
        rstd = at(191, "rstd", [P, SEQ])
        kr = at(193, "kr", [P, SEQ])
        xc = at(195, "xc", [P, 2, SEQ])
        rt = at(199, "rt", [P, LT, SEQ])
        xg = at(179, "xg", [P, D])
        xb_hi = at(183, "xb_hi", [P, DT, P], F32R)
        xb_lo = at(187, "xb_lo", [P, DT, P], F32R)
        choose = at(191, "choose", [P, TT, P])
        ht_hi = at(191, "ht_hi", [P, FT, P], F32R)
        ht_lo = at(193, "ht_lo", [P, FT, P], F32R)
        sg = at(195, "sg", [P, F_EXP])
        hb = at(197, "hb", [P, F_EXP])
        yb = at(199, "yb", [P, D])
        N_BLK = MAX_BLOCKS + 2
        by_exp = at(199, "by_exp", [P, 2, N_BLK, N_EXP])
        pairs4 = at(199, "pairs4", [P, 2, 4 * TT * N_EXP])
        scores_t = at(201, "scores_t", [N_EXP, TT, P])
        yg = at(82, "yg", [P, 2 * TT, D])

        def hi(j):
            return hi_a[:, j, :] if j < RA else hi_b[:, j - RA, :]

        def lo(j):
            return lo_a[:, j, :] if j < RA else lo_b[:, j - RA, :]

        def raw(j):
            return raw_a[:, j, :] if j < RA else raw_b[:, j - RA, :]

        def f(ap):
            return ap.bitcast(F32)

        def root(t):
            return root_a[:, t, :] if t < 2 else root_b[:, t - 2, :]

        ident = cst[:, IDENT:IDENT + P]
        ones = cst[:, ONES:ONES + P]
        tri = cst[:, TRI:TRI + P]
        cmask = cst[:, CMASK:CMASK + P]
        dup = cst[:, DUP:DUP + P]
        rot = cst[:, ROT:ROT + SEQ]

        bank = [ctx.enter_context(nc.psum_tensor(f"bank{i}", [P, 512], F32)) for i in range(8)]

        col = [0]

        def cols(n):
            s = small[:, col[0]:col[0] + n]
            col[0] += n
            return s

        eps = cols(1)
        sp_a, sp_b, sp_c, sp_d, sp_e = (cols(LT) for _ in range(5))
        c4, c8 = cols(LT), cols(LT)
        nmax, psum_, pinv = cols(16), cols(16), cols(16)
        stats = [cols(12) for _ in range(TT)]
        mv = [cols(2) for _ in range(TT)]
        std, rstd_t, nmr = cols(TT), cols(TT), cols(TT)
        s_e, sel, masked, rank, oh1, oh2, tmp, use = (cols(TT * N_EXP) for _ in range(8))
        g_a, g_e = (cols(TT * N_GRP) for _ in range(2))
        t_a, w1, w2, wr = (cols(TT) for _ in range(4))
        gate = cols(2 * TT)
        cnt, nb, cum = (cols(N_EXP) for _ in range(3))
        tot, first, tmp2, dst = sel, rank, masked, use
        iota = cols(P)
        idx = cols(2 * TT).bitcast(I32)
        nblk = cols(N_EXP).bitcast(I32)
        blk0, filled_rows = sel[:, 0:N_BLK], masked[:, 0:N_BLK]
        brows = cols(N_BLK).bitcast(I32)
        dstk = cols(2 * TT)
        assert col[0] < 1024

        xbuf = nc.dram_tensor("xbuf", (MAX_BLOCKS + 2, P, D), F32).ap()
        xrows = xbuf.rearrange("b p d -> (b p) d")

        init, filled = sem("init"), sem("filled")
        scat = sem("scat")
        scat_goal, gath_goal = nc.scalar.alloc_register("scat_goal"), nc.vector.alloc_register("gath_goal")
        pre_in = [sem(f"pre_in{i}") for i in range(RA)]
        pre_goal = nc.scalar.alloc_register("pre_goal")
        names = """par_in gates_in ln1_in ln2_in xt_t xt_h xt_l gemm ev_dve ev_act a_hi a_lo
            sqd sqa sums_q sums_kv rs_std nrm_h nrm_l kdup krd xcd gmm gact ixd tanhd geld sqrtd lrud decd
            sc nm ex pn ptr pte pv mla opd vd stdd lnx lng lnb lnp x1d x1e lg sgd used_d pfx nbd
            chain_d mixs_l mixs_m nz lnm lnm_p chosen scd rowsd c4d xal
            xg_in xbt hbt sgs hbd xbh xbh2 xbl htt hth htl yev1 yevd yst allst
            sp_abs sp_exp pad""".split()
        S = {n: sem(n) for n in names}
        raw_in = [sem(f"raw_in{i}") for i in range(RA)]
        pair_in = [sem(f"pair_in{i}") for i in range(PAIRS)]
        w_hi = [sem(f"w_hi{j}") for j in range(RING)]
        w_lo = [sem(f"w_lo{j}") for j in range(RING)]
        w_used = [sem(f"w_used{j}") for j in range(RING)]
        gath = [sem(f"gath{i}") for i in range(TT)]
        every = list(S.values()) + raw_in + pair_in + w_hi + w_lo + w_used

        def chunk_freed(n):
            if n < C_K:
                return S["gemm"], n + 1
            if n == C_K:
                return S["gemm"], M_V
            if n == C_V:
                return S["gemm"], M_Q
            if n < C_OUT:
                return S["gemm"], M_Q + (n - C_Q) + 1
            return S["opd"], (n - C_OUT) // 2 + 1

        def evac_done(m):
            if m < M_K:
                return S["ev_dve"], m + 1
            if m < M_Q:
                return S["ev_act"], m - M_K + 1
            if (m - M_Q) % 2 == 0:
                return S["ev_act"], M_Q - M_K + (m - M_Q) // 2 + 1
            return S["ev_dve"], M_K + (m - M_Q) // 2 + 1

        def normed(i):
            return (S["lnp"], i + 1) if i < TT - 1 else (S["lnb"], 1)

        with nc.Block() as block:
            @block.sync
            def _(sp):
                sp.dma_start(x[:, :, :], a["x"][0].rearrange("(i p) d -> p i d", p=P)).then_inc(init, 16)
                sp.dma_start(cst[:, :], a["cst"][:, 0:N_CST]).then_inc(init, 16)
                sp.dma_start(iota, a["cst"][:, N_CST:N_CST + P]).then_inc(init, 16)
                sp.dma_start(rw[:, :], a["rw"][:, :]).then_inc(init, 16)
                sp.dma_start(rb[:, :], a["rb"][:, :]).then_inc(init, 16)
                for n in range(RA):
                    sp.dma_start(raw(n), a["wm"][0, n]).then_inc(pre_in[n], 16)
                sp.wait_ge(init, 80)

            @block.vector
            def _(dve):
                nc.vector.memset(eps, EPS)
                dve.reg_mov(gath_goal, 32)

            @block.scalar
            def _(act):
                act.reg_mov(scat_goal, 16 * 2 * TT)
                act.reg_mov(pre_goal, 16)

        with nc.Fori(0, DEPTH) as ly:
            with nc.Block() as block:
                @block.sync
                def _(sp):
                    sp.dma_start(par[:, :], a["par"][bass.ds(ly, 1)].rearrange("l p n -> (l p) n")).then_inc(S["par_in"], 16)
                    sp.dma_start(gatew[:, :, :], a["gw"][bass.ds(ly, 1)].rearrange("l p (t n) -> (l p) t n", n=P)).then_inc(S["gates_in"], 16)
                    for n in range(RA, N_CHUNK):
                        sp.wait_ge(S["a_lo"], n - RA + 1)
                        w = chunk_width(n)
                        sp.dma_start(raw(n % RA)[:, 0:w], a["wm"][bass.ds(ly, 1), n, :, 0:w].rearrange("l p n -> (l p) n")).then_inc(raw_in[n % RA], 16)
                        if n < RA + (MAX_BLOCKS + 3) // 2:
                            with sp.If(ly < 1):
                                for b in range(2 * (n - RA), min(2 * (n - RA) + 2, MAX_BLOCKS + 2)):
                                    sp.dma_start(xbuf[b], cst[:, 0:D]).then_inc(filled, 16)
                    sp.wait_ge(S["lrud"], LT)
                    sp.dma_start(lnbc[:, :, :], a["ln"][bass.ds(ly, 1), 0].rearrange("l c d -> (l c) d").partition_broadcast(P)).then_inc(S["ln1_in"], 16)

                    sp.wait_ge(S["a_lo"], N_CHUNK)
                    for t in range(RA // 2):
                        sp.dma_start(raw_a[:, 2 * t:2 * t + 2, :], a["we"][bass.ds(ly, 1), 0, t].rearrange("l p n -> (l p) n").rearrange("p (c n) -> p c n", c=2)).then_inc(pair_in[t], 16)
                    sp.wait_ge(S["opd"], 2 + TT)
                    for t in range(RA // 2, PAIRS):
                        sp.dma_start(raw_b[:, 2 * t - RA:2 * t - RA + 2, :], a["we"][bass.ds(ly, 1), 0, t].rearrange("l p n -> (l p) n").rearrange("p (c n) -> p c n", c=2)).then_inc(pair_in[t], 16)
                    def land(e, pairs):
                        for t in pairs:
                            dst = raw_a[:, 2 * t:2 * t + 2, :] if 2 * t < RA else raw_b[:, 2 * t - RA:2 * t - RA + 2, :]
                            sp.dma_start(dst, a["we"][bass.ds(ly, 1), bass.ds(e, 1), t].rearrange("l e p n -> (l e p) n").rearrange("p (c n) -> p c n", c=2)).then_inc(pair_in[t], 16)

                    one, two = sp.alloc_register("sp_one"), sp.alloc_register("sp_two")
                    sp.reg_mov(one, 1)
                    sp.reg_mov(two, 2)
                    for t in range(PAIRS):
                        sp.wait_ge(w_lo[2 * t], 2)
                        sp.wait_ge(w_lo[2 * t + 1], 2)
                        land(1, [t])
                    with sp.Fori(1, N_EXP - 1) as e:
                        sp.reg_add(one, one, 1)
                        sp.reg_add(two, two, 1)
                        for t in range(PAIRS - 2):
                            sp.wait_ge(w_lo[2 * t], two)
                            sp.wait_ge(w_lo[2 * t + 1], two)
                            land(e + 1, [t])
                        with sp.If(e > 1):
                            for t in range(PAIRS - 2, PAIRS):
                                sp.wait_ge(w_lo[2 * t], one)
                                sp.wait_ge(w_lo[2 * t + 1], one)
                                land(e, [t])
                    for t in range(PAIRS - 2, PAIRS):
                        sp.wait_ge(w_lo[2 * t], N_EXP)
                        sp.wait_ge(w_lo[2 * t + 1], N_EXP)
                        land(N_EXP - 1, [t])
                    for n in range(RA):
                        sp.wait_ge(w_lo[n], N_EXP + 1)
                    with sp.If(ly < DEPTH - 1):
                        for n in range(RA):
                            sp.dma_start(raw(n), a["wm"][bass.ds(nc.s_assert_within(ly + 1, 1, DEPTH - 1, skip_runtime_bounds_check_because="the branch keeps it within"), 1), n].rearrange("l p n -> (l p) n")).then_inc(pre_in[n], 16)
                    sp.wait_ge(S["lnp"], TT - 1)
                    sp.wait_ge(S["lnb"], 1)
                    sp.dma_start(lnbc[:, :, :], a["ln"][bass.ds(ly, 1), 1].rearrange("l c d -> (l c) d").partition_broadcast(P)).then_inc(S["ln2_in"], 16)

                @block.tensor
                def _(pe):
                    def mm3(o, wh, wl, mh, ml, first, last):
                        nc.tensor.matmul(o, wh, mh, start=first, stop=False)
                        nc.tensor.matmul(o, wh, ml, start=False, stop=False)
                        return nc.tensor.matmul(o, wl, mh, start=False, stop=last)

                    for c in range(DT):
                        if c >= 6:
                            pe.wait_ge(S["xt_l"], c - 5)
                        for i in range(TT):
                            m = nc.tensor.transpose(bank[2 + c % 6][:, i * P:(i + 1) * P], x[:, i, c * P:(c + 1) * P], ident)
                        m.then_inc(S["xt_t"], 1)

                    for n in range(N_IN):
                        pe.wait_ge(S["a_lo"], n + 1)
                        if n >= 2:
                            pe.wait_ge(*evac_done(n - 2))
                        wh, wl = hi(n % RA), lo(n % RA)
                        for k in range(DT):
                            if n == 0:
                                pe.wait_ge(S["xt_l"], k + 1)
                            m = mm3(bank[n % 2][:, :], wh[:, k * P:(k + 1) * P], wl[:, k * P:(k + 1) * P], xt_hi[:, k, :], xt_lo[:, k, :], k == 0, k == DT - 1)
                        m.then_inc(S["gemm"], 1)
                        if n == QT + KT + 1:
                            pe.wait_ge(S["ev_dve"], QT + KT + 1)
                            nc.tensor.matmul(bank[7][:, :], dup, krot[:, :], start=True, stop=True).then_inc(S["kdup"], 1)
                            pe.wait_ge(S["sqa"], QT - 1)
                            nc.tensor.matmul(bank[6][:, :], ones, acc[:, 0, :], start=True, stop=True).then_inc(S["sums_q"], 1)
                            pe.wait_ge(S["sqa"], QT + KT - 2)
                            nc.tensor.matmul(bank[5][:, :], ones, acc[:, 1, :], start=True, stop=True).then_inc(S["sums_kv"], 1)

                    def up(m0, n, outs, kt, tile0, values=False):
                        pe.wait_ge(S["a_lo"], n + 1)
                        wh, wl = hi(n % RA), lo(n % RA)
                        for h in range(outs):
                            pe.wait_ge(*evac_done(m0 + h - 2))
                            for k in range(kt):
                                o = bank[(m0 + h) % 2][:, :]
                                if values:
                                    s = slice(h * P, (h + 1) * P)
                                    m = mm3(o, n_hi[:, tile0 + k, s], n_lo[:, tile0 + k, s], wh[:, k * SEQ:(k + 1) * SEQ], wl[:, k * SEQ:(k + 1) * SEQ], k == 0, k == kt - 1)
                                else:
                                    s = slice((k * outs + h) * P, (k * outs + h + 1) * P)
                                    m = mm3(o, wh[:, s], wl[:, s], n_hi[:, tile0 + k, :], n_lo[:, tile0 + k, :], k == 0, k == kt - 1)
                            m.then_inc(S["gemm"], 1)

                    def gates(t):
                        pe.wait_ge(S["xcd"], t + 1)
                        if t:
                            pe.wait_ge(S["gact"], 2 * t)
                        else:
                            pe.wait_ge(S["gates_in"], 16)
                            pe.wait_ge(S["rs_std"], 2)
                        nc.tensor.matmul(bank[4][:, :], gatew[:, t, :], xc[:, t % 2, :], start=True, stop=True).then_inc(S["gmm"], 1)
                        nc.tensor.matmul(bank[5][:, :], gatew[:, LT + t, :], xc[:, t % 2, :], start=True, stop=True).then_inc(S["gmm"], 1)

                    pe.wait_ge(S["nrm_l"], KT)
                    up(M_K, C_K, HEADS, KT, QT)
                    gates(0)
                    up(M_V, C_V, TT, KT, QT, values=True)
                    gates(1)
                    def queries(h, steps):
                        for t in steps:
                            part, k = t // QT, t % QT
                            m_, n = M_Q + 2 * h + part, C_Q + 2 * h + part
                            if k == 0:
                                pe.wait_ge(S["a_lo"], n + 1)
                                pe.wait_ge(*evac_done(m_ - 2))
                            s = slice(k * P, (k + 1) * P)
                            m = mm3(bank[m_ % 2][:, :], hi(n % RA)[:, s], lo(n % RA)[:, s], n_hi[:, k, :], n_lo[:, k, :], k == 0, k == QT - 1)
                            if k == QT - 1:
                                m.then_inc(S["gemm"], 1)

                    pe.wait_ge(S["nrm_l"], QT + KT)
                    queries(0, range(2 * QT))
                    gates(2)
                    gates(3)
                    queries(1, range(2 * QT))

                    def score(s):
                        h, i = s // TT, s % TT
                        w = (i + 1) * P
                        o = bank[4 + s % 2]
                        if s < 2:
                            pe.wait_ge(S["gact"], 2 * LT)
                        else:
                            pe.wait_ge(S["ex"], s - 1)
                        if i == 0:
                            pe.wait_ge(*evac_done(M_Q + 2 * h))
                            pe.wait_ge(*evac_done(M_Q + 2 * h + 1))
                        if s == 0:
                            pe.wait_ge(S["krd"], 1)
                        nc.tensor.matmul(o[:, 0:w], q[:, h, i * P:w], kn[:, h, 0:w], start=True, stop=False)
                        nc.tensor.matmul(o[:, 0:w], q[:, HEADS + h, i * P:w], kr[:, 0:w], start=False, stop=False)
                        nc.tensor.matmul(o[:, i * P:w], ident, cmask, start=False, stop=True).then_inc(S["sc"], 1)

                    def values(h):
                        pe.wait_ge(S["pte"], TT * (h + 1))
                        if h:
                            pe.wait_ge(S["mla"], h)
                        for j in range(TT):
                            m = nc.tensor.matmul(bank[6][:, j * P:SEQ], v[:, j, h * P:(h + 1) * P], pt[:, h % 2, j, j * P:SEQ], start=(j == 0), stop=(j == TT - 1))
                        m.then_inc(S["pv"], 1)

                    def project(half, cs, i):
                        for c in cs:
                            n = C_OUT + OUT_ORDER.index((half, c))
                            pe.wait_ge(S["a_lo"], n + 1)
                            pe.wait_ge(S["nrm_l"], QT + KT + 2 * c + 2)
                            wh, wl = hi(n % RA), lo(n % RA)
                            for kk in range(2):
                                s = slice(i * P, (i + 1) * P)
                                m = mm3(bank[4 * half + i][:, :], n_hi[:, 2 * c + kk, s], n_lo[:, 2 * c + kk, s], wh[:, kk * HALF:(kk + 1) * HALF], wl[:, kk * HALF:(kk + 1) * HALF],
                                        c == 0 and kk == 0, c == 3 and kk == 1)
                        return m

                    def early(n):
                        half, tile = ((0, 0), (0, 1), (1, 3))[n // 2]
                        if n == 4:
                            pe.wait_ge(S["rs_std"], 3)
                        project(half, (n % 2,), tile)

                    STEPS = HEADS * TT
                    score(0)
                    for s in range(STEPS):
                        if s + 1 < STEPS:
                            score(s + 1)
                        h, i = s // TT, s % TT
                        if i < 3 and h + 2 < HEADS:
                            queries(h + 2, range(4 * i, 4 * i + 4))
                        if s in VALUE_STEPS:
                            values(VALUE_STEPS.index(s))
                        if s == MIX_STEP:
                            pe.wait_ge(S["sqa"], QT + KT - 2 + LT - 1)
                            nc.tensor.matmul(bank[7][:, :], ones, acc[:, 0, :], start=True, stop=True).then_inc(S["mixs_l"], 1)
                        if s >= STEPS - 5:
                            early(s - STEPS + 5)
                        pe.wait_ge(S["pn"], s + 1)
                        if s >= 2:
                            pe.wait_ge(S["pte"], s - 1)
                        for j in range(s % TT + 1):
                            m = nc.tensor.transpose(bank[2 + s % 2][:, j * P:(j + 1) * P], prob[:, s % 2, j * P:(j + 1) * P], ident)
                        m.then_inc(S["ptr"], 1)
                    early(5)
                    values(HEADS - 1)
                    project(0, (0, 1), 2)
                    pe.wait_ge(S["mla"], HEADS)
                    pe.wait_ge(S["sqa"], QT + KT - 2 + 2 * (LT - 1))
                    nc.tensor.matmul(bank[6][:, :], ones, acc[:, 1, :], start=True, stop=True).then_inc(S["mixs_m"], 1)
                    project(0, (0, 1), 3).then_inc(S["opd"], 1)
                    pe.wait_ge(S["ex"], STEPS)
                    project(1, (0, 1), 0)
                    project(1, (0, 1), 1)
                    pe.wait_ge(S["rs_std"], 4)
                    project(1, (0, 1), 2).then_inc(S["opd"], 1)
                    for i in range(TT):
                        project(0, (2,), i)
                    for i in range(TT):
                        project(0, (3,), i)
                        project(1, (2, 3), i).then_inc(S["opd"], 1)

                    def turn(i):
                        pe.wait_ge(*normed(i))
                        for c in range(DT):
                            m = nc.tensor.transpose(bank[i + c // 4 * 4][:, c % 4 * P:(c % 4 + 1) * P], x[:, i, c * P:(c + 1) * P], ident)
                        m.then_inc(S["x1d"], 1)

                    turn(0)
                    for i in range(TT):
                        if i + 1 < TT:
                            turn(i + 1)
                        pe.wait_ge(S["x1e"], i + 1)
                        for k in range(DT):
                            m = nc.tensor.matmul(bank[i][0:N_EXP, 0:P], rw[:, k * N_EXP:(k + 1) * N_EXP], x1t[:, k, i * P:(i + 1) * P], start=(k == 0), stop=(k == DT - 1))
                        m.then_inc(S["lg"], 1)
                    for i in range(TT):
                        pe.wait_ge(S["sgd"], i + 1)
                        m = nc.tensor.transpose(bank[4][:, i * N_EXP:(i + 1) * N_EXP], scores_t[:, i, :], ident[0:N_EXP, 0:N_EXP])
                    m.then_inc(S["scd"], 1)

                    pe.wait_ge(S["used_d"], 1)
                    nc.tensor.matmul(bank[5][:, 0:TT * N_EXP], tri, use, start=True, stop=True)
                    nc.tensor.matmul(bank[7][:, 0:TT * N_EXP], ones, use, start=True, stop=True).then_inc(S["pfx"], 1)

                    def turn_x(half, s):
                        for c in range(4 * half, 4 * half + 4):
                            m = nc.tensor.transpose(bank[2 + half][:, c % 4 * P:(c % 4 + 1) * P], xg[:, c * P:(c + 1) * P], ident)
                        m.then_inc(s, 1)

                    g, gm, g16, lap, lapd = (pe.alloc_register(n) for n in ("pe_g", "pe_gm", "pe_g16", "pe_lap", "pe_lapd"))
                    pe.reg_mov(g, 1)
                    pe.reg_mov(gm, 0)
                    pe.reg_mov(g16, 16)
                    pe.reg_mov(lap, 2)
                    pe.reg_mov(lapd, 2)

                    def down():
                        pe.wait_ge(S["yevd"], gm)
                        pe.wait_ge(S["htl"], gm)
                        for j in range(8, RING):
                            pe.wait_ge(w_lo[j], lapd)
                            for half in range(2):
                                m = mm3(bank[5 + half][:, :], ht_hi[:, j - 8, :], ht_lo[:, j - 8, :], hi(j)[:, half * HALF:(half + 1) * HALF], lo(j)[:, half * HALF:(half + 1) * HALF], j == 8, j == RING - 1)
                            m.then_inc(w_used[j], 1)

                    pe.wait_ge(S["chosen"], 1)
                    for c in range(DT):
                        for i in range(TT):
                            m = nc.tensor.matmul(bank[2 + c // 4][:, c % 4 * P:(c % 4 + 1) * P], x[:, i, c * P:(c + 1) * P], choose[:, i, :], start=(i == 0), stop=(i == TT - 1))
                        if c % 4 == 3:
                            m.then_inc((S["xbt"], S["hbt"])[c // 4], 1)
                    with pe.Fori(0, N_EXP) as e:
                        blocks = pe.value_load(nblk[0:1, bass.ds(e, 1)], min_val=1, max_val=TT)
                        with pe.Fori(0, blocks):
                            pe.wait_ge(S["xbl"], g)
                            for side in range(2):
                                for j in range(4 * side, 4 * side + 4):
                                    pe.wait_ge(w_lo[j], lap)
                                    for kk in range(2):
                                        k = 2 * (j % 4) + kk
                                        m = mm3(bank[side][:, :], xb_hi[:, k, :], xb_lo[:, k, :], hi(j)[:, kk * F_EXP:(kk + 1) * F_EXP], lo(j)[:, kk * F_EXP:(kk + 1) * F_EXP], k == 0, k == DT - 1)
                                    m.then_inc(w_used[j], 1)
                            pe.wait_ge(S["xg_in"], g16)
                            turn_x(0, S["xbt"])
                            turn_x(1, S["hbt"])
                            with pe.If(pe.snap(gm, min_val=0, max_val=MAX_BLOCKS) > 0):
                                down()
                            pe.wait_ge(S["hbd"], g)
                            for c in range(FT):
                                m = nc.tensor.transpose(bank[4][:, c * P:(c + 1) * P], hb[:, c * P:(c + 1) * P], ident)
                            m.then_inc(S["htt"], 1)
                            pe.reg_add(g, g, 1)
                            pe.reg_add(gm, gm, 1)
                            pe.reg_add(g16, g16, 16)
                            pe.reg_add(lapd, lap, 0)
                        pe.reg_add(lap, lap, 1)
                    down()

                @block.scalar
                def _(act):
                    def split(n):
                        w = chunk_width(n)
                        if n >= RA:
                            act.wait_ge(*chunk_freed(n - RA))
                            act.wait_ge(raw_in[n % RA], 16 * (n // RA))
                        else:
                            act.wait_ge(pre_in[n], pre_goal)
                        nc.scalar.activation(hi(n % RA)[:, 0:w], raw(n % RA)[:, 0:w], ACT.Copy).then_inc(S["a_hi"], 1)

                    def upper(tile, src):
                        nrm[0] += 1
                        act.wait_ge(S["nz"], nrm[0])
                        nc.scalar.activation(n_hi[:, tile, :], src, ACT.Copy).then_inc(S["nrm_h"], 1)

                    def square(kappa, src):
                        if kappa >= 2:
                            act.wait_ge(S["sqa"], sq_taken(kappa - 2))
                        nc.scalar.activation(sq[:, kappa % 2, :], src, ACT.Square).then_inc(S["sqd"], 1)

                    def deviation(src, width):
                        nc.scalar.activation(rstd[:, :], src[:, :], ACT.Sqrt, bias=eps, scale=1.0 / width).then_inc(S["rs_std"], 1)

                    nrm = [0]
                    split(0)
                    for c in range(DT):
                        act.wait_ge(S["xt_t"], c + 1)
                        nc.scalar.activation(xt_hi[:, c, :], bank[2 + c % 6][:, :], ACT.Copy).then_inc(S["xt_h"], 1)
                    act.wait_ge(S["sp_abs"], 1)
                    nc.scalar.activation(sp_e, sp_a, ACT.Exp, scale=-1.0).then_inc(S["sp_exp"], 1)
                    for n in range(1, RA):
                        split(n)
                    act.reg_add(pre_goal, pre_goal, 16)
                    for n in range(N_IN):
                        split(n + RA)
                        if n < QT + KT:
                            act.wait_ge(S["ev_dve"], n + 1)
                            square(n, z_lat[:, n, :])
                        if n == QT + KT + 2:
                            act.wait_ge(S["kdup"], 1)
                            nc.scalar.activation(kr[:, :], bank[7][:, :], ACT.Copy).then_inc(S["krd"], 1)
                            act.wait_ge(S["sums_kv"], 1)
                            deviation(bank[5], KV_LORA)
                            for k in range(KT):
                                upper(QT + k, z_lat[:, QT + k, :])
                            act.wait_ge(S["sums_q"], 1)
                            deviation(bank[6], Q_LORA)
                        if QT + KT + 4 <= n < QT + KT + 4 + QT // 2:
                            for k in range(2):
                                tile = 2 * (n - QT - KT - 4) + k
                                upper(tile, z_lat[:, tile, :])

                    def leave(m, dst, scale=1.0):
                        act.wait_ge(S["gemm"], m + 1)
                        nc.scalar.activation(dst, bank[m % 2][:, :], ACT.Copy, scale=scale).then_inc(S["ev_act"], 1)

                    def gates(t):
                        act.wait_ge(S["gmm"], 2 * t + 1)
                        nc.scalar.activation(rt[:, t, :], bank[4][:, :], ACT.Sigmoid, bias=par[:, B_R + t:B_R + t + 1]).then_inc(S["gact"], 1)
                        act.wait_ge(S["gmm"], 2 * t + 2)
                        nc.scalar.activation(z_u[:, t, 3:3 + SEQ], bank[5][:, :], ACT.Sigmoid, bias=par[:, B_I + t:B_I + t + 1]).then_inc(S["gact"], 1)
                        if t == 0:
                            act.wait_ge(S["c4d"], 1)
                            act.wait_ge(S["nrm_l"], QT + KT)
                        act.wait_ge(S["gact"], 2 * t + 2)
                        nc.scalar.activation(root(t), rt[:, t, :], ACT.Tanh, scale=c4[:, t:t + 1]).then_inc(S["tanhd"], 1)

                    for h in range(HEADS):
                        leave(M_K + h, kn[:, h, :])
                    split(C_K + RA)
                    gates(0)
                    for i in range(TT):
                        leave(M_V + i, v[:, i, :])
                    split(C_V + RA)
                    gates(1)
                    act.wait_ge(S["ev_dve"], N_IN)
                    for t in range(LT):
                        nc.scalar.activation(z_gate[:, t, :], z_gate[:, t, :], ACT.Gelu_apprx_tanh).then_inc(S["geld"], 1)

                    def queries_out(h):
                        leave(M_Q + 2 * h, q[:, h, :], QK_HEAD ** -0.5)

                    queries_out(0)
                    split(C_Q + RA)
                    split(C_Q + 1 + RA)
                    gates(2)
                    gates(3)
                    act.wait_ge(S["tanhd"], LT)
                    for t in range(LT):
                        nc.scalar.activation(root(t), root(t), ACT.Sqrt).then_inc(S["sqrtd"], 1)
                    queries_out(1)

                    def decay(t):
                        nc.scalar.activation(rt[:, t, :], rt[:, t, :], ACT.Exp, scale=c8[:, t:t + 1]).then_inc(S["decd"], 1)

                    def leave_p(s):
                        h, i = s // TT, s % TT
                        act.wait_ge(S["ptr"], s + 1)
                        if h >= 2 and i == 0:
                            act.wait_ge(S["pv"], h - 1)
                        nc.scalar.activation(pt[:, h % 2, 0:i + 1, i * P:(i + 1) * P], bank[2 + s % 2][:, 0:(i + 1) * P].rearrange("p (j c) -> p j c", c=P), ACT.Copy).then_inc(S["pte"], 1)

                    decay(0)
                    STEPS = HEADS * TT
                    for s in range(STEPS):
                        w = (s % TT + 1) * P
                        act.wait_ge(S["nm"], s + 1)
                        if s >= 2:
                            act.wait_ge(S["ptr"], s - 1)
                        nc.scalar.activation(prob[:, s % 2, 0:w], bank[4 + s % 2][:, 0:w], ACT.Exp, bias=nmax[:, s:s + 1], accum_out=psum_[:, s:s + 1]).then_inc(S["ex"], 1)
                        if s:
                            leave_p(s - 1)
                        h, i = s // TT, s % TT
                        if h + 2 < HEADS and i == 2:
                            queries_out(h + 2)
                        if h + 1 < HEADS and i == 2:
                            split(C_Q + 2 * h + 2 + RA)
                        if h + 1 < HEADS and i == 3:
                            split(C_Q + 2 * h + 3 + RA)
                        if s == 0:
                            decay(1)
                        if s in (2, 3):
                            decay(s)
                        if s - 1 in RECUR_STEPS:
                            t = RECUR_STEPS.index(s - 1)
                            act.wait_ge(S["lrud"], t + 1)
                            square(QT + KT + t, z_gate[:, t, :])
                        if s == MIX_STEP:
                            act.wait_ge(S["mixs_l"], 1)
                            deviation(bank[7], LRU)
                        if s in (MIX_STEP + 2, MIX_STEP + 3):
                            for t in range(2 * (s - MIX_STEP - 2), 2 * (s - MIX_STEP - 1)):
                                upper(t, z_gate[:, t, :])
                        if s in (10, 12):
                            t = (s - 10) // 2
                            act.wait_ge(S["mla"], t + 1)
                            square(QT + KT + LT + t, q[:, t, :])
                    leave_p(STEPS - 1)
                    for h in range(HEADS - 2, HEADS):
                        act.wait_ge(S["mla"], h + 1)
                        square(QT + KT + LT + h, q[:, h, :])
                    act.wait_ge(S["mixs_m"], 1)
                    deviation(bank[6], HEADS * P)
                    split(C_OUT + 4)
                    split(C_OUT + 5)
                    for h in range(HEADS):
                        upper(LT + h, q[:, h, :])
                    split(C_OUT + 6)
                    split(C_OUT + 7)

                    def norm(k):
                        for i in range(TT):
                            if k == 0 and i == TT - 1:
                                transposed_out(0)
                            act.wait_ge(S["vd"], TT * k + i + 1)
                            nc.scalar.activation(std[:, i:i + 1], mv[i][:, 1:2], ACT.Sqrt, bias=eps).then_inc(S["stdd"], 1)
                            act.wait_ge(S["lnx"], TT * k + i + 1)
                            nc.scalar.activation(x[:, i, :], x[:, i, :], ACT.Identity, bias=nmr[:, i:i + 1], scale=rstd_t[:, i:i + 1]).then_inc(S["lng"], 1)

                    def upper_0(js):
                        act.wait_ge(S["opd"], 2 + TT)
                        for j in js:
                            act.wait_ge(pair_in[j // 2], 16)
                            nc.scalar.activation(hi(j), raw(j), ACT.Copy).then_inc(w_hi[j], 1)

                    def transposed_out(i):
                        act.wait_ge(S["x1d"], i + 1)
                        s = slice(i * P, (i + 1) * P)
                        nc.scalar.activation(x1t[:, 0:4, s], bank[i][:, :].rearrange("p (k c) -> p k c", c=P), ACT.Copy)
                        nc.scalar.activation(x1t[:, 4:8, s], bank[4 + i][:, :].rearrange("p (k c) -> p k c", c=P), ACT.Copy).then_inc(S["x1e"], 1)

                    norm(0)
                    def sigmoid(i):
                        act.wait_ge(S["lg"], i + 1)
                        nc.scalar.activation(scores_t[:, i, :], bank[i][0:N_EXP, 0:P], ACT.Sigmoid).then_inc(S["sgd"], 1)

                    for i in range(1, TT):
                        upper_0(range(2 * i - 2, 2 * i))
                        transposed_out(i)
                        if i > 1:
                            sigmoid(i - 2)
                    sigmoid(TT - 2)
                    sigmoid(TT - 1)
                    upper_0(range(2 * TT, RING))

                    g, gp, gm, gm16, g16, l1x, l2x = (act.alloc_register(n) for n in ("a_g", "a_gp", "a_gm", "a_gm16", "a_g16", "a_l1x", "a_l2x"))
                    xrow, yrow = act.alloc_register("a_xrow"), act.alloc_register("a_yrow")
                    act.reg_mov(gm, 0)
                    act.reg_mov(g, 1)
                    act.reg_mov(gp, 2)
                    act.reg_mov(gm16, 0)
                    act.reg_mov(g16, 16)
                    act.reg_mov(l1x, 16)
                    act.reg_mov(l2x, 32)
                    act.reg_mov(xrow, 2)
                    act.reg_mov(yrow, 0)

                    def upper_w(js, used, landed):
                        for j in js:
                            if j in ACT_HI:
                                act.wait_ge(w_used[j], used)
                                act.wait_ge(pair_in[j // 2], landed)
                                nc.scalar.activation(hi(j), raw(j), ACT.Copy).then_inc(w_hi[j], 1)

                    def upper_x(count):
                        act.wait_ge(S["xbt"], count)
                        nc.scalar.activation(xb_hi[:, 0:4, :], bank[2][:, :].rearrange("p (k c) -> p k c", c=P), ACT.Copy).then_inc(S["xbh"], 1)
                        act.wait_ge(S["hbt"], count)
                        nc.scalar.activation(xb_hi[:, 4:8, :], bank[3][:, :].rearrange("p (k c) -> p k c", c=P), ACT.Copy).then_inc(S["xbh2"], 1)

                    def travel(rows, dma):
                        with act.If(rows > P // 2):
                            with act.If(rows > 3 * P // 4):
                                dma(P)
                            with act.If(rows <= 3 * P // 4):
                                dma(3 * P // 4)
                        with act.If(rows <= P // 2):
                            with act.If(rows > P // 4):
                                dma(P // 2)
                            with act.If(rows <= P // 4):
                                dma(P // 4)

                    def store(n):
                        act.dma_start(xbuf[bass.ds(act.snap(yrow, min_val=0, max_val=MAX_BLOCKS - 1), 1), 0:n].rearrange("b p d -> (b p) d"), yb[0:n, :]).then_inc(S["yst"], 16)

                    def fetch(n):
                        act.dma_start(xg[0:n, :], xbuf[bass.ds(act.snap(xrow, min_val=0, max_val=MAX_BLOCKS + 1), 1), 0:n].rearrange("b p d -> (b p) d")).then_inc(S["xg_in"], 16)

                    def outputs():
                        act.wait_ge(w_used[RING - 1], g)
                        act.wait_ge(S["yst"], gm16)
                        nc.scalar.activation(yb[:, 0:HALF], bank[5][:, :], ACT.Copy)
                        nc.scalar.activation(yb[:, HALF:D], bank[6][:, :], ACT.Copy).then_inc(S["yevd"], 1)
                        act.wait_ge(S["yevd"], g)
                        travel(act.value_load(brows[0:1, bass.ds(act.snap(yrow, min_val=0, max_val=MAX_BLOCKS - 1), 1)], min_val=0, max_val=P), store)
                        act.reg_add(yrow, yrow, 1)

                    upper_x(1)
                    act.wait_ge(scat, scat_goal)
                    act.dma_start(xg[:, :], xbuf[1]).then_inc(S["xg_in"], 16)
                    act.reg_add(scat_goal, scat_goal, 16 * 2 * TT)
                    act.wait_ge(S["rowsd"], 1)

                    with act.Fori(0, N_EXP) as e:
                        blocks = act.value_load(nblk[0:1, bass.ds(e, 1)], min_val=1, max_val=TT)
                        with act.Fori(0, blocks) as b:
                            act.wait_ge(w_used[3], gp)
                            nc.scalar.activation(sg[:, :], bank[0][:, :], ACT.Silu).then_inc(S["sgs"], 1)
                            with act.If(b + 1 == blocks):
                                with act.If(e < N_EXP - 1):
                                    upper_w(range(0, 4), gp, l2x)
                            upper_x(gp)
                            travel(act.value_load(brows[0:1, bass.ds(act.snap(xrow, min_val=0, max_val=MAX_BLOCKS + 1), 1)], min_val=0, max_val=P), fetch)
                            with act.If(b + 1 == blocks):
                                with act.If(e < N_EXP - 1):
                                    upper_w(range(4, 8), gp, l2x)
                            with act.If(b < 1):
                                with act.If(e > 0):
                                    upper_w(range(8, RING), g, l1x)
                            act.wait_ge(S["htt"], g)
                            nc.scalar.activation(ht_hi[:, :, :], bank[4][:, :].rearrange("p (k c) -> p k c", c=P), ACT.Copy).then_inc(S["hth"], 1)
                            with act.If(act.snap(gm, min_val=0, max_val=MAX_BLOCKS) > 0):
                                outputs()
                            for r, by in ((g, 1), (gp, 1), (gm, 1), (gm16, 16), (g16, 16), (xrow, 1)):
                                act.reg_add(r, r, by)
                        act.reg_add(l1x, l1x, 16)
                        act.reg_add(l2x, l2x, 16)
                    outputs()
                    act.wait_ge(S["yst"], g16)
                    act.wait_ge(S["xg_in"], g16)
                    nc.scalar.activation(small[:, 1023:1024], eps, ACT.Copy).then_inc(S["allst"], 1)
                    norm(1)

                @block.vector
                def _(dve):
                    done = [0]

                    def link(ins):
                        done[0] += 1
                        ins.then_inc(S["chain_d"], 1)
                        dve.wait_ge(S["chain_d"], done[0])

                    def split(n):
                        w = chunk_width(n)
                        dve.wait_ge(S["a_hi"], n + 1)
                        nc.vector.tensor_tensor(lo(n % RA)[:, 0:w], raw(n % RA)[:, 0:w], f(hi(n % RA)[:, 0:w]), ALU.subtract).then_inc(S["a_lo"], 1)

                    nrm = [0]

                    def lower(tile, src):
                        nrm[0] += 1
                        dve.wait_ge(S["nrm_h"], nrm[0])
                        nc.vector.tensor_tensor(n_lo[:, tile, :], src, f(n_hi[:, tile, :]), ALU.subtract).then_inc(S["nrm_l"], 1)

                    def normalise(which, tiles):
                        dve.wait_ge(S["rs_std"], which)
                        link(nc.vector.reciprocal(rstd[:, :], rstd[:, :]))
                        scaled(tiles)
                        lowered(tiles)

                    def scaled(tiles):
                        for tile, src, g in tiles:
                            nc.vector.scalar_tensor_tensor(out=src, in0=src, scalar=par[:, g:g + 1], in1=rstd[:, :], op0=ALU.mult, op1=ALU.mult).then_inc(S["nz"], 1)

                    def lowered(tiles):
                        for tile, src, g in tiles:
                            lower(tile, src)

                    dve.wait_ge(S["par_in"], 16)
                    lam = par[:, LAM:LAM + LT]
                    link(nc.vector.tensor_scalar(sp_b, lam, -1.0, None, ALU.mult))
                    nc.vector.tensor_tensor(sp_a, lam, sp_b, ALU.max).then_inc(S["sp_abs"], 1)
                    split(0)
                    for c in range(DT):
                        dve.wait_ge(S["xt_h"], c + 1)
                        nc.vector.tensor_tensor(xt_lo[:, c, :], bank[2 + c % 6][:, :], f(xt_hi[:, c, :]), ALU.subtract).then_inc(S["xt_l"], 1)
                    for n in range(1, RA):
                        split(n)
                    dve.wait_ge(S["sp_exp"], 1)
                    link(nc.vector.tensor_scalar(sp_c, sp_e, 2.0, None, ALU.add))
                    link(nc.vector.reciprocal(sp_c, sp_c))
                    link(nc.vector.tensor_tensor(sp_c, sp_c, sp_e, ALU.mult))
                    link(nc.vector.tensor_tensor(sp_d, sp_c, sp_c, ALU.mult))
                    link(nc.vector.tensor_scalar(sp_a, sp_d, 1.0 / 17, 1.0 / 15, ALU.mult, ALU.add))
                    for k in (13, 11, 9, 7, 5, 3, 1):
                        link(nc.vector.tensor_tensor(sp_a, sp_a, sp_d, ALU.mult))
                        link(nc.vector.tensor_scalar(sp_a, sp_a, 1.0 / k, None, ALU.add))
                    link(nc.vector.tensor_tensor(sp_a, sp_a, sp_c, ALU.mult))
                    link(nc.vector.tensor_scalar(sp_b, sp_b, 0.0, None, ALU.max))
                    link(nc.vector.scalar_tensor_tensor(out=sp_a, in0=sp_a, scalar=2.0, in1=sp_b, op0=ALU.mult, op1=ALU.add))
                    nc.vector.tensor_scalar(c8, sp_a, -8.0, None, ALU.mult)
                    nc.vector.tensor_scalar(c4, sp_a, 4.0, None, ALU.mult).then_inc(S["c4d"], 1)

                    for n in range(N_IN):
                        dve.wait_ge(S["gemm"], n + 1)
                        o = bank[n % 2]
                        if n < QT + KT:
                            m = nc.vector.tensor_copy(z_lat[:, n, :], o[:, :])
                        elif n == QT + KT:
                            m = nc.vector.tensor_tensor(krot[:, :], o[:, :], rot, ALU.mult)
                        elif n < QT + KT + 1 + LT:
                            m = nc.vector.tensor_copy(z_u[:, n - QT - KT - 1, 3:3 + SEQ], o[:, :])
                        else:
                            m = nc.vector.tensor_copy(z_gate[:, n - QT - KT - 1 - LT, :], o[:, :])
                        m.then_inc(S["ev_dve"], 1)
                        split(n + RA)
                        if n == QT + KT + 2:
                            normalise(1, [(QT + k, z_lat[:, QT + k, :], QG + QT + k) for k in range(KT)])
                        if n == QT + KT + 3:
                            dve.wait_ge(S["rs_std"], 2)
                            link(nc.vector.reciprocal(rstd[:, :], rstd[:, :]))
                        if QT + KT + 4 <= n < QT + KT + 4 + QT // 2:
                            for k in range(2):
                                tile = 2 * (n - QT - KT - 4) + k
                                nc.vector.scalar_tensor_tensor(out=z_lat[:, tile, :], in0=z_lat[:, tile, :], scalar=par[:, QG + tile:QG + tile + 1], in1=rstd[:, :], op0=ALU.mult, op1=ALU.mult).then_inc(S["nz"], 1)
                            for k in range(2):
                                tile = 2 * (n - QT - KT - 4) + k
                                lower(tile, z_lat[:, tile, :])

                    def conv(t):
                        if t == 0:
                            dve.wait_ge(S["pad"], 1)
                        if t >= 2:
                            dve.wait_ge(S["gmm"], 2 * (t - 1))
                            dve.wait_ge(S["ixd"], t - 1)
                        o = xc[:, t % 2, :]
                        link(nc.vector.tensor_scalar(o, z_u[:, t, 3:3 + SEQ], par[:, CONV_W + 3 * LT + t:CONV_W + 3 * LT + t + 1], par[:, CONV_B + t:CONV_B + t + 1], ALU.mult, ALU.add))
                        for w in range(3):
                            m = nc.vector.scalar_tensor_tensor(out=o, in0=z_u[:, t, w:w + SEQ], scalar=par[:, CONV_W + w * LT + t:CONV_W + w * LT + t + 1], in1=o, op0=ALU.mult, op1=ALU.add)
                            if w < 2:
                                link(m)
                        m.then_inc(S["xcd"], 1)

                    def gated_in(t):
                        dve.wait_ge(S["gact"], 2 * t + 2)
                        dve.wait_ge(S["xcd"], t + 1)
                        nc.vector.tensor_tensor(z_u[:, t, 3:3 + SEQ], z_u[:, t, 3:3 + SEQ], xc[:, t % 2, :], ALU.mult).then_inc(S["ixd"], 1)

                    conv(0)
                    conv(1)
                    split(C_K + RA)
                    gated_in(0)
                    conv(2)
                    split(C_V + RA)
                    gated_in(1)
                    conv(3)
                    def rotated_out(h):
                        m = M_Q + 2 * h + 1
                        dve.wait_ge(S["gemm"], m + 1)
                        nc.vector.scalar_tensor_tensor(out=q[:, HEADS + h, :], in0=bank[m % 2][:, :], scalar=QK_HEAD ** -0.5, in1=rot, op0=ALU.mult, op1=ALU.mult).then_inc(S["ev_dve"], 1)

                    split(C_Q + RA)
                    rotated_out(0)
                    split(C_Q + 1 + RA)
                    gated_in(2)
                    gated_in(3)
                    rotated_out(1)

                    def recur(t):
                        drive = xc[:, t % 2, :]
                        u = z_u[:, t, 3:3 + SEQ]
                        dve.wait_ge(S["sqrtd"], LT)
                        dve.wait_ge(S["ixd"], LT)
                        dve.wait_ge(S["geld"], LT)
                        dve.wait_ge(S["decd"], t + 1)
                        link(nc.vector.scalar_tensor_tensor(out=drive, in0=rt[:, t, :], scalar=1.0, in1=root(t), op0=ALU.add, op1=ALU.mult))
                        link(nc.vector.tensor_tensor(u, u, drive, ALU.mult))
                        link(nc.vector.tensor_tensor_scan(drive, rt[:, t, :], u, 0.0, ALU.mult, ALU.add))
                        nc.vector.tensor_tensor(z_gate[:, t, :], z_gate[:, t, :], drive, ALU.mult).then_inc(S["lrud"], 1)

                    def divide(s):
                        dve.wait_ge(S["ex"], s + 1)
                        link(nc.vector.reciprocal(pinv[:, s:s + 1], psum_[:, s:s + 1]))
                        w = (s % TT + 1) * P
                        nc.vector.tensor_scalar(prob[:, s % 2, 0:w], prob[:, s % 2, 0:w], pinv[:, s:s + 1], None, ALU.mult).then_inc(S["pn"], 1)

                    def head_out(h):
                        dve.wait_ge(S["pv"], h + 1)
                        nc.vector.tensor_copy(q[:, h, :], bank[6][:, :]).then_inc(S["mla"], 1)

                    STEPS = HEADS * TT
                    for s in range(STEPS):
                        w = (s % TT + 1) * P
                        dve.wait_ge(S["sc"], s + 1)
                        nc.vector.tensor_reduce(nmax[:, s:s + 1], bank[4 + s % 2][:, 0:w], AX.X, ALU.max, negate=True).then_inc(S["nm"], 1)
                        if s:
                            divide(s - 1)
                        h, i = s // TT, s % TT
                        if h + 2 < HEADS and i == 3:
                            rotated_out(h + 2)
                        if h + 1 < HEADS and i == 3:
                            split(C_Q + 2 * h + 2 + RA)
                        if h and i == 0:
                            split(C_Q + 2 * h + 1 + RA)
                        if s in RECUR_STEPS:
                            recur(RECUR_STEPS.index(s))
                        if s - 1 in VALUE_STEPS:
                            head_out(VALUE_STEPS.index(s - 1))
                        if s in (MIX_STEP + 1, MIX_STEP + 2):
                            half = slice((s - MIX_STEP - 1) * HALF // 2, (s - MIX_STEP) * HALF // 2)
                            dve.wait_ge(S["rs_std"], 3)
                            link(nc.vector.reciprocal(rstd[:, half], rstd[:, half]))
                        t = 2 * (s - MIX_STEP - 2)
                        if s in (MIX_STEP + 3, MIX_STEP + 4):
                            lowered([(t - 2 + k, z_gate[:, t - 2 + k, :], 0) for k in range(2)])
                        if s in (MIX_STEP + 2, MIX_STEP + 3):
                            scaled([(t + k, z_gate[:, t + k, :], OG + t + k) for k in range(2)])
                    divide(STEPS - 1)
                    head_out(HEADS - 1)
                    dve.wait_ge(S["rs_std"], 4)
                    link(nc.vector.reciprocal(rstd[:, :], rstd[:, :]))
                    heads = [(LT + h, q[:, h, :], OG + LT + h) for h in range(HEADS)]
                    scaled(heads[0:3])
                    lowered(heads[0:2])
                    split(C_OUT + 4)
                    scaled(heads[3:4])
                    split(C_OUT + 5)
                    lowered(heads[2:4])
                    split(C_OUT + 6)
                    split(C_OUT + 7)

                    def moments(k, i):
                        nc.vector.bn_stats(stats[i][:, 0:6], x[:, i, 0:HALF])
                        link(nc.vector.bn_stats(stats[i][:, 6:12], x[:, i, HALF:D]))
                        nc.vector.bn_aggr(mv[i], stats[i]).then_inc(S["vd"], 1)

                    def invert(k, i):
                        dve.wait_ge(S["stdd"], TT * k + i + 1)
                        link(nc.vector.reciprocal(rstd_t[:, i:i + 1], std[:, i:i + 1]))
                        nc.vector.scalar_tensor_tensor(out=nmr[:, i:i + 1], in0=mv[i][:, 0:1], scalar=-1.0, in1=rstd_t[:, i:i + 1], op0=ALU.mult, op1=ALU.mult).then_inc(S["lnx"], 1)

                    def gain(k, i):
                        dve.wait_ge(S["lng"], TT * k + i + 1)
                        nc.vector.tensor_tensor(x[:, i, :], x[:, i, :], lnbc[:, 0, :], ALU.mult).then_inc(S["lnm"], 1)

                    def shift(k, i):
                        dve.wait_ge(S["lnm"], TT * k + i + 1)
                        nc.vector.tensor_tensor(x[:, i, :], x[:, i, :], lnbc[:, 1, :], ALU.add).then_inc(S["lnb"], 1)

                    for i in range(TT + 1):
                        if i < TT:
                            dve.wait_ge(S["opd"], 2 + i + 1)
                            for half in range(2):
                                s = slice(half * HALF, (half + 1) * HALF)
                                m = nc.vector.scalar_tensor_tensor(out=x[:, i, s], in0=x[:, i, s], scalar=ALPHA, in1=bank[4 * half + i][:, :], op0=ALU.mult, op1=ALU.add)
                                if half:
                                    link(m)
                            moments(0, i)
                        if i:
                            if i == 1:
                                dve.wait_ge(S["ln1_in"], 16)
                            gain(0, i - 1)
                        if i < TT:
                            invert(0, i)
                        if i == TT:
                            shift(0, i - 1)
                    def lower_0(js):
                        for j in js:
                            dve.wait_ge(w_hi[j], 1)
                            nc.vector.tensor_tensor(lo(j), raw(j), f(hi(j)), ALU.subtract).then_inc(w_lo[j], 1)

                    lower_0((0, 3, 4))
                    dve.wait_ge(pair_in[3], 16)
                    for j in (6, 7):
                        nc.vector.tensor_copy(hi(j), raw(j)).then_inc(w_hi[j], 1)
                    lower_0((6, 7))

                    def rows(ap, n):
                        return ap.rearrange("p (i n) -> p i n", n=n)

                    def wide(ap, n):
                        return ap.unsqueeze(2).to_broadcast([P, ap.shape[1], n])

                    tt = nc.vector.tensor_tensor
                    dve.wait_ge(S["scd"], 1)
                    nc.vector.tensor_copy(s_e, bank[4][:, 0:TT * N_EXP])
                    link(tt(sel, bank[4][:, 0:TT * N_EXP], rb[:, :], ALU.add))
                    QUADS = TT * N_GRP
                    other = rows(sel, 4).unsqueeze(2).to_broadcast([P, QUADS, 4, 4])
                    own = rows(sel, 4).unsqueeze(3).to_broadcast([P, QUADS, 4, 4])
                    earlier = cst[:, EARLIER:EARLIER + 16].rearrange("p (e j) -> p e j", j=4).unsqueeze(1).to_broadcast([P, QUADS, 4, 4])
                    larger, equal = (pairs4[:, k].rearrange("p (q e j) -> p q e j", e=4, j=4) for k in range(2))
                    tt(larger, other, own, ALU.is_gt)
                    link(tt(equal, other, own, ALU.is_equal))
                    link(tt(equal, equal, earlier, ALU.mult))
                    link(tt(pairs4[:, 0], pairs4[:, 0], pairs4[:, 1], ALU.add))
                    link(nc.vector.tensor_reduce(rank, rows(pairs4[:, 0], 4), AX.X, ALU.add))
                    link(nc.vector.tensor_scalar(tmp, rank, 1.5, None, ALU.is_gt))
                    link(nc.vector.tensor_scalar(use, tmp, -1.0, 1.0, ALU.mult, ALU.add))
                    link(tt(tmp, sel, use, ALU.mult))
                    link(nc.vector.tensor_reduce(g_e, rows(tmp, 4), AX.X, ALU.add))

                    def first_best(values_, n, weights, out_):
                        link(nc.vector.tensor_reduce(t_a, rows(values_, n), AX.X, ALU.max))
                        link(tt(rows(out_, n), rows(values_, n), wide(t_a, n), ALU.is_equal))
                        link(tt(out_, out_, weights, ALU.mult))
                        link(nc.vector.tensor_reduce(t_a, rows(out_, n), AX.X, ALU.max))
                        link(tt(rows(out_, n), rows(out_, n), wide(t_a, n), ALU.is_equal))

                    first_best(g_e, N_GRP, cst[:, GW:GW + TT * N_GRP], g_a)
                    tt(rows(use, 4), rows(use, 4), wide(g_a, 4), ALU.mult).then_inc(S["used_d"], 1)
                    link(nc.vector.tensor_scalar(oh1, rank, 0.5, None, ALU.is_gt))
                    link(nc.vector.tensor_scalar(oh1, oh1, -1.0, 1.0, ALU.mult, ALU.add))
                    dve.wait_ge(S["used_d"], 1)
                    link(tt(oh1, oh1, use, ALU.mult))
                    link(tt(oh2, use, oh1, ALU.subtract))
                    dve.wait_ge(S["pfx"], 1)
                    link(nc.vector.tensor_copy(tot, bank[7][:, 0:TT * N_EXP]))
                    link(nc.vector.tensor_reduce(cnt, tot.rearrange("p (i n) -> p n i", n=N_EXP), AX.X, ALU.add))
                    link(nc.vector.tensor_scalar(nb, cnt, float(P), 1.0, ALU.is_gt, ALU.add))
                    for k in range(2, TT):
                        link(nc.vector.scalar_tensor_tensor(out=nb, in0=cnt, scalar=float(k * P), in1=nb, op0=ALU.is_gt, op1=ALU.add))
                    link(nc.vector.tensor_tensor_scan(cum, ones[:, 0:N_EXP], nb, 0.0, ALU.mult, ALU.add))
                    link(tt(cum, cum, nb, ALU.subtract))
                    link(nc.vector.tensor_scalar(first[:, 0:N_EXP], cum, float(P), None, ALU.mult))
                    for i in range(1, TT):
                        link(tt(first[:, i * N_EXP:(i + 1) * N_EXP], first[:, (i - 1) * N_EXP:i * N_EXP], tot[:, (i - 1) * N_EXP:i * N_EXP], ALU.add))
                    link(tt(dst, bank[5][:, 0:TT * N_EXP], first, ALU.add))
                    tt(tmp, dst, oh1, ALU.mult)
                    link(tt(tmp2, dst, oh2, ALU.mult))
                    nc.vector.tensor_reduce(dstk[:, 0:TT], rows(tmp, N_EXP), AX.X, ALU.add)
                    link(nc.vector.tensor_reduce(dstk[:, TT:2 * TT], rows(tmp2, N_EXP), AX.X, ALU.add))
                    nc.vector.tensor_copy(nblk, nb)
                    nc.vector.tensor_copy(idx, dstk).then_inc(S["nbd"], 1)
                    dve.wait_ge(S["nbd"], 1)
                    for i in range(TT):
                        link(nc.vector.tensor_scalar(choose[:, i, :], iota, dstk[:, i:i + 1], None, ALU.is_equal))
                        m = nc.vector.scalar_tensor_tensor(out=choose[:, i, :], in0=iota, scalar=dstk[:, TT + i:TT + i + 1], in1=choose[:, i, :], op0=ALU.is_equal, op1=ALU.add)
                    m.then_inc(S["chosen"], 1)
                    g, gp, l1, l2, l1x, l2x = (dve.alloc_register(n) for n in ("d_g", "d_gp", "d_l1", "d_l2", "d_l1x", "d_l2x"))
                    dve.reg_mov(g, 1)
                    dve.reg_mov(gp, 2)
                    dve.reg_mov(l1, 1)
                    dve.reg_mov(l2, 2)
                    dve.reg_mov(l1x, 16)
                    dve.reg_mov(l2x, 32)

                    def split_w(js, used, landed, lap):
                        for j in js:
                            if j not in ACT_HI:
                                dve.wait_ge(w_used[j], used)
                                dve.wait_ge(pair_in[j // 2], landed)
                                nc.vector.tensor_copy(hi(j), raw(j)).then_inc(w_hi[j], 1)
                            if j not in POOL_LO:
                                dve.wait_ge(w_hi[j], lap)
                                nc.vector.tensor_tensor(lo(j), raw(j), f(hi(j)), ALU.subtract).then_inc(w_lo[j], 1)

                    def lower_x(count):
                        dve.wait_ge(S["xbh"], count)
                        nc.vector.tensor_tensor(xb_lo[:, 0:4, :], bank[2][:, :].rearrange("p (k c) -> p k c", c=P), f(xb_hi[:, 0:4, :]), ALU.subtract)
                        dve.wait_ge(S["xbh2"], count)
                        nc.vector.tensor_tensor(xb_lo[:, 4:8, :], bank[3][:, :].rearrange("p (k c) -> p k c", c=P), f(xb_hi[:, 4:8, :]), ALU.subtract).then_inc(S["xbl"], 1)

                    lower_x(1)

                    link(nc.vector.tensor_scalar(blk0, iota[:, 0:N_BLK], float(P), None, ALU.mult))
                    link(tt(cnt, cnt, first[:, 0:N_EXP], ALU.add))
                    mine, before = by_exp[:, 0], by_exp[:, 1]
                    ends = cnt.unsqueeze(1).to_broadcast([P, N_BLK, N_EXP])
                    starts = first[:, 0:N_EXP].unsqueeze(1).to_broadcast([P, N_BLK, N_EXP])
                    tt(mine, ends, wide(blk0, N_EXP), ALU.subtract)
                    link(tt(before, starts, wide(blk0, N_EXP), ALU.is_gt))
                    link(nc.vector.tensor_scalar(mine, mine, 0.0, float(P), ALU.max, ALU.min))
                    link(tt(before, before, mine, ALU.mult))
                    link(tt(mine, mine, before, ALU.subtract))
                    link(nc.vector.tensor_reduce(filled_rows, mine, AX.X, ALU.add))
                    nc.vector.tensor_copy(brows, filled_rows).then_inc(S["rowsd"], 1)
                    link(tt(tmp, s_e, oh1, ALU.mult))
                    link(nc.vector.tensor_reduce(w1, rows(tmp, N_EXP), AX.X, ALU.add))
                    link(tt(tmp, s_e, oh2, ALU.mult))
                    link(nc.vector.tensor_reduce(w2, rows(tmp, N_EXP), AX.X, ALU.add))
                    link(tt(wr, w1, w2, ALU.add))
                    link(nc.vector.reciprocal(wr, wr))
                    tt(gate[:, 0:TT], w1, wr, ALU.mult)
                    link(tt(gate[:, TT:2 * TT], w2, wr, ALU.mult))


                    with dve.Fori(0, N_EXP) as e:
                        blocks = dve.value_load(nblk[0:1, bass.ds(e, 1)], min_val=1, max_val=TT)
                        with dve.Fori(0, blocks) as b:
                            with dve.If(b + 1 == blocks):
                                with dve.If(e < N_EXP - 1):
                                    split_w(range(0, 4), gp, l2x, l2)
                            dve.wait_ge(w_used[7], gp)
                            dve.wait_ge(S["sgs"], g)
                            nc.vector.tensor_tensor(hb[:, :], bank[1][:, :], sg[:, :], ALU.mult).then_inc(S["hbd"], 1)
                            lower_x(gp)
                            with dve.If(b + 1 == blocks):
                                with dve.If(e < N_EXP - 1):
                                    split_w(range(4, 8), gp, l2x, l2)
                            with dve.If(b < 1):
                                with dve.If(e > 0):
                                    split_w(range(8, RING - 1), g, l1x, l1)
                            dve.wait_ge(S["hth"], g)
                            nc.vector.tensor_tensor(ht_lo[:, :, :], bank[4][:, :].rearrange("p (k c) -> p k c", c=P), f(ht_hi[:, :, :]), ALU.subtract).then_inc(S["htl"], 1)
                            with dve.If(b < 1):
                                with dve.If(e > 0):
                                    split_w(range(RING - 1, RING), g, l1x, l1)
                            dve.reg_add(g, g, 1)
                            dve.reg_add(gp, gp, 1)
                        for r, by in ((l1, 1), (l2, 1), (l1x, 16), (l2x, 16)):
                            dve.reg_add(r, r, by)

                    dve.wait_ge(S["xg_in"], 16)
                    for i in range(TT):
                        nc.vector.tensor_scalar(x[:, i, :], x[:, i, :], ALPHA, None, ALU.mult).then_inc(S["xal"], 1)
                    dve.wait_ge(S["xal"], TT)
                    for i in range(TT):
                            dve.wait_ge(gath[i], gath_goal)
                            for k in range(2):
                                link(nc.vector.scalar_tensor_tensor(out=x[:, i, :], in0=yg[:, 2 * i + k, :], scalar=gate[:, k * TT + i:k * TT + i + 1], in1=x[:, i, :], op0=ALU.mult, op1=ALU.add))
                            moments(1, i)
                            invert(1, i)
                    dve.wait_ge(S["ln2_in"], 16)
                    gain(1, TT - 1)
                    dve.wait_ge(S["lnm"], TT + 1)
                    nc.vector.tensor_tensor(x[:, TT - 1, :], x[:, TT - 1, :], lnbc[:, 1, :], ALU.add).then_inc(S["lnb"], 1)
                    dve.reg_add(gath_goal, gath_goal, 32)

                @block.gpsimd
                def _(pool):
                    for j in range(RING):
                        pool.sem_inc(w_used[j], 1)
                        pool.sem_inc(w_lo[j], 1)
                    pool.sem_inc(S["yevd"], 1)
                    pool.sem_inc(S["yst"], 16)

                    nc.gpsimd.memset(z_u[:, :, 0:3], 0.0).then_inc(S["pad"], 1)

                    kappa, added = 0, 0
                    for grp, n in enumerate(SQ_GROUPS):
                        for k in range(n):
                            kappa += 1
                            if k == 0:
                                continue
                            pool.wait_ge(S["sqd"], kappa)
                            if k == 1 and grp >= 2:
                                pool.wait_ge(S[("sums_q", "sums_kv")[grp - 2]], 1)
                            if k >= 2:
                                pool.wait_ge(S["sqa"], added)
                            m0 = sq[:, 0, :] if k == 1 else acc[:, grp % 2, :]
                            nc.gpsimd.tensor_tensor(acc[:, grp % 2, :], m0, sq[:, 1, :] if k == 1 else sq[:, (kappa - 1) % 2, :], ALU.add).then_inc(S["sqa"], 1)
                            added += 1

                    def moved(k):
                        for i in range(TT - 1):
                            if k:
                                if i == 0:
                                    pool.wait_ge(S["ln2_in"], 16)
                                pool.wait_ge(S["lng"], TT + i + 1)
                                nc.gpsimd.tensor_tensor(x[:, i, :], x[:, i, :], lnbc[:, 0, :], ALU.mult).then_inc(S["lnm_p"], 1)
                                pool.wait_ge(S["lnm_p"], i + 1)
                            else:
                                pool.wait_ge(S["lnm"], i + 1)
                            nc.gpsimd.tensor_tensor(x[:, i, :], x[:, i, :], lnbc[:, 1, :], ALU.add).then_inc(S["lnp"], 1)

                    moved(0)

                    for j in POOL_LO_0:
                        pool.wait_ge(w_hi[j], 1)
                        nc.gpsimd.tensor_tensor(lo(j), raw(j), f(hi(j)), ALU.subtract).then_inc(w_lo[j], 1)

                    pool.wait_ge(S["nbd"], 1)
                    pool.wait_ge(filled, 16 * (MAX_BLOCKS + 2))
                    pool.wait_ge(S["lnb"], 1)
                    for k in range(2):
                        for i in range(TT):
                            c = k * TT + i
                            pool.indirect_dma_start(out=xrows, out_offset=bass.IndirectOffsetOnAxis(ap=idx[:, c:c + 1], axis=0), in_=x[:, i, :], in_offset=None).then_inc(scat, 16)

                    lap = pool.alloc_register("p_lap")
                    pool.reg_mov(lap, 2)
                    with pool.Fori(1, N_EXP):
                        for j in POOL_LO:
                            pool.wait_ge(w_hi[j], lap)
                            nc.gpsimd.tensor_tensor(lo(j), raw(j), f(hi(j)), ALU.subtract).then_inc(w_lo[j], 1)
                        pool.reg_add(lap, lap, 1)

                    pool.wait_ge(S["allst"], 1)
                    for i in range(TT):
                        for k in range(2):
                            c = k * TT + i
                            pool.indirect_dma_start(out=yg[:, 2 * i + k, :], out_offset=None, in_=xrows, in_offset=bass.IndirectOffsetOnAxis(ap=idx[:, c:c + 1], axis=0)).then_inc(gath[i], 16)
                    moved(1)

            with nc.Block() as block:
                @block.gpsimd
                def _(pool):
                    for s in every[0::5]:
                        pool.sem_clear(s)

                @block.sync
                def _(sp):
                    for s in every[1::5]:
                        sp.sem_clear(s)

                @block.scalar
                def _(act):
                    for s in every[2::5]:
                        act.sem_clear(s)

                @block.vector
                def _(dve):
                    for s in every[3::5]:
                        dve.sem_clear(s)

                @block.tensor
                def _(pe):
                    for s in every[4::5]:
                        pe.sem_clear(s)

        with nc.Block() as block:
            @block.sync
            def _(sp):
                sp.dma_start(out[0].rearrange("(i p) d -> p i d", p=P), x[:, :, :]).then_inc(init, 16)
                sp.wait_ge(init, 96)


ARRAYS = ("x", "cst", "rw", "rb", "par", "gw", "ln", "wm", "we")


def kernel(x, w_in, conv_w, conv_b, w_rgate, b_rgate, w_igate, b_igate, lru_lambda, q_norm_g, w_q_up, kv_norm_g, w_kv_up,
           out_norm_g, w_out, ln1_g, ln1_b, router_w, router_bias, w_exp_gate, w_exp_up, w_exp_down, ln2_g, ln2_b):
    import numpy as np
    import concourse.bacc as bacc
    from concourse.bass_utils import run_bass_kernel_spmd

    pos = np.arange(SEQ, dtype=np.float32)
    inv = (np.float32(10000.0) ** (-np.arange(ROPE // 2, dtype=np.float32) / np.float32(ROPE // 2))).astype(np.float32)
    ang = pos[None, :] * inv[:, None]
    cos, sin = np.cos(ang), np.sin(ang)
    r = np.arange(P)
    pieces = [np.eye(P), np.ones((P, P)), r[:, None] < r[None, :],
              r[:, None] % ROPE == r[None, :] % ROPE, np.concatenate([cos, cos, -sin, sin]), np.where(r[None, :] <= r[:, None], 0.0, -BIG),
              np.tile(np.arange(N_EXP, 0, -1), (P, TT)), np.tile(np.arange(N_GRP, 0, -1), (P, TT)),
              np.tile((np.arange(4)[None, :] < np.arange(4)[:, None]).reshape(-1), (P, 1)), np.tile(r, (P, 1))]
    cst = np.concatenate([np.asarray(p, np.float32) for p in pieces], axis=1)

    def tiles(w):
        w = np.asarray(w)
        return np.moveaxis(w.reshape(w.shape[0], w.shape[1] // P, P, *w.shape[2:]), 2, 1)

    def columns(v):
        v = np.asarray(v).reshape(DEPTH, -1)
        return np.moveaxis(v.reshape(DEPTH, -1, P), 2, 1)

    par = np.concatenate([columns(np.asarray(conv_w)), columns(conv_b), columns(b_rgate), columns(b_igate), columns(lru_lambda),
                          columns(q_norm_g), columns(kv_norm_g), columns(out_norm_g)], axis=2)
    gw = np.zeros((DEPTH, P, 2 * LT, P), np.float32)
    for s, w in enumerate((w_rgate, w_igate)):
        w = np.asarray(w).reshape(DEPTH, LT, 2, 64, 64)
        for b in range(2):
            gw[:, 64 * b:64 * b + 64, s * LT:(s + 1) * LT, 64 * b:64 * b + 64] = np.moveaxis(w[:, :, b], 2, 1)
    gw = gw.reshape(DEPTH, P, -1)
    turned = np.r_[0:32, 32:64, 32:64, 0:32]
    wi = np.asarray(w_in)
    order = [2 * LRU + P * t + r for t in range(QT + KT)] + [2 * LRU + Q_LORA + KV_LORA + turned] + [P * t + r for t in range(2 * LT)]
    wm = np.zeros((DEPTH, N_CHUNK, P, CH), np.float32)
    for n, c in enumerate(order):
        wm[:, n] = tiles(wi[:, :, c]).reshape(DEPTH, P, CH)
    kv = tiles(w_kv_up)
    wm[:, C_K] = kv[..., 0:P].reshape(DEPTH, P, CH)
    wm[:, C_V] = kv[..., P:].reshape(DEPTH, P, CH)
    qu = tiles(w_q_up)
    for h in range(HEADS):
        wm[:, C_Q + 2 * h, :, 0:Q_LORA] = qu[:, :, :, h, 0:P].reshape(DEPTH, P, -1)
        wm[:, C_Q + 2 * h + 1, :, 0:Q_LORA] = qu[:, :, :, h, P + turned].reshape(DEPTH, P, -1)
    wo = tiles(w_out)
    for n, (half, c) in enumerate(OUT_ORDER):
        wm[:, C_OUT + n] = wo[:, :, 2 * c:2 * c + 2, half * HALF:(half + 1) * HALF].reshape(DEPTH, P, CH)
    we = np.empty((DEPTH, N_EXP, PAIRS, P, 2 * CH), np.float32)
    for s, w in enumerate((w_exp_gate, w_exp_up)):
        w = np.asarray(w).reshape(DEPTH, N_EXP, 2, 4, P, F_EXP)
        we[:, :, 2 * s:2 * s + 2] = np.moveaxis(w, 4, 3).reshape(DEPTH, N_EXP, 2, P, 2 * CH)
    w = np.asarray(w_exp_down).reshape(DEPTH, N_EXP, 2, 2, P, D)
    we[:, :, 4:6] = np.moveaxis(w, 4, 3).reshape(DEPTH, N_EXP, 2, P, 2 * CH)
    ln = np.stack([np.stack([np.asarray(ln1_g), np.asarray(ln1_b)], 1), np.stack([np.asarray(ln2_g), np.asarray(ln2_b)], 1)], 1)
    rw = np.moveaxis(np.asarray(router_w).reshape(DT, P, N_EXP), 1, 0).reshape(P, -1)
    rb = np.ascontiguousarray(np.broadcast_to(np.asarray(router_bias), (P, TT, N_EXP)).reshape(P, -1))

    nc = bacc.Bacc("TRN2", target_bir_lowering=False, num_devices=1)
    host = dict(x=np.asarray(x), cst=cst, rw=rw, rb=rb, par=par, gw=gw, ln=ln, wm=wm, we=we)
    arrays, args = {}, {}
    for name in ARRAYS:
        arrays[name + "_in"] = np.ascontiguousarray(host[name])
        args[name] = nc.dram_tensor(name + "_in", arrays[name + "_in"].shape, F32, kind="ExternalInput").ap()
    out = nc.dram_tensor("out_dram", (1, SEQ, D), F32, kind="ExternalOutput").ap()
    build(nc, args, out)
    return run_bass_kernel_spmd(nc, [arrays], core_ids=[0]).results[0]["out_dram"]
```
